# Optimizing a Trainium2 kernel written in Bass

```python
import math
import jax, jax.numpy as jnp
from jax import lax
import numpy as np

D_MODEL = 1024
BATCH = 1
SEQ = 512
DEPTH = 2

MIX_A = 512
MLSTM_HEADS = 4
MLSTM_DH = MIX_A // MLSTM_HEADS
MLSTM_CHUNK = 128
CONV_K = 4
MIX_B = D_MODEL - MIX_A
S5_GROUP = 16
S5_GROUPS = MIX_B // S5_GROUP
S5_STATE = 64
DT_MIN = 1e-3
DT_MAX = 1e-1
IN_A = 4 * MIX_A + 2 * MLSTM_HEADS + MIX_B

NSA_HEADS = 16
NSA_KV = 4
NSA_DH = D_MODEL // NSA_HEADS
KV_W = NSA_KV * NSA_DH
CMP_BLOCK = 32
CMP_STRIDE = 16
CMP_HIDDEN = 256
SEL_BLOCK = 64
SEL_TOPK = 16
WINDOW = 512
NSA_QBLOCK = 32
IN_C = D_MODEL + 6 * KV_W + 3 * NSA_HEADS
FORCE = 1e9

REL_BUCKETS = 32
REL_MAX_DIST = 128

MOE_GROUPS = 4
MOE_PER_GROUP = 4
MOE_EXPERTS = MOE_GROUPS * MOE_PER_GROUP
MOE_HIDDEN = 256
MOE_TOPK = 2

N_EVEN = (DEPTH + 1) // 2
N_ODD = DEPTH // 2
EPS = 1e-6
NEG = -1e30

kernel_name = 'hybrid_mlstm_s5_nsa_hmoe'

def _rmsnorm(x, g):
    xf = x.astype(jnp.float32)
    y = xf * lax.rsqrt(jnp.mean(xf * xf, axis=-1, keepdims=True) + EPS)
    return (y * g.astype(jnp.float32)).astype(x.dtype)

def _modulate(x, g, shift, scale):
    return _rmsnorm(x, g) * (1 + scale[:, None, :]) + shift[:, None, :]

def _masked_softmax(s, mask, axis):
    p = jax.nn.softmax(jnp.where(mask, s, NEG), axis=axis)
    return jnp.where(mask, p, 0.0)

def _t5_bucket(dist):
    dist = jnp.maximum(dist, 0)
    max_exact = REL_BUCKETS // 2
    log_ratio = jnp.log(jnp.maximum(dist, 1).astype(jnp.float32) / max_exact) / math.log(REL_MAX_DIST / max_exact)
    large = jnp.minimum(max_exact + (log_ratio * (REL_BUCKETS - max_exact)).astype(jnp.int32), REL_BUCKETS - 1)
    return jnp.where(dist < max_exact, dist, large)

def _causal_conv(x, w):
    return lax.conv_general_dilated(x, w[:, None, :].astype(x.dtype), window_strides=(1,),
                                    padding=[(CONV_K - 1, 0)],
                                    dimension_numbers=('NWC', 'WIO', 'NWC'),
                                    feature_group_count=x.shape[-1])

def _mlstm_chunkwise(q, k, v, i_pre, f_pre):
    f32 = jnp.float32
    B, S, H, DH = q.shape
    L = MLSTM_CHUNK
    NC = S // L
    ch = lambda t: t.reshape((B, NC, L) + t.shape[2:])
    q, k, v = ch(q), ch(k) * DH ** -0.5, ch(v)
    li = ch(i_pre)
    b = jnp.cumsum(jax.nn.log_sigmoid(ch(f_pre)), axis=2)
    b_last = b[:, :, -1]
    w = b_last[:, :, None] - b + li
    m_loc = jnp.max(w, axis=2)
    e = jnp.exp(w - m_loc[:, :, None])
    c_loc = jnp.einsum('bclh,bclhd,bclhe->bchde', e, v, k)
    n_loc = jnp.einsum('bclh,bclhe->bche', e, k)

    def step(carry, inp):
        c_st, n_st, m_st = carry
        c_l, n_l, m_l, b_l = inp
        m_new = jnp.maximum(b_l + m_st, m_l)
        a = jnp.exp(b_l + m_st - m_new)
        s = jnp.exp(m_l - m_new)
        new = (a[..., None, None] * c_st + s[..., None, None] * c_l,
               a[..., None] * n_st + s[..., None] * n_l, m_new)
        return new, (c_st, n_st, m_st)

    init = (jnp.zeros((B, H, DH, DH), f32), jnp.zeros((B, H, DH), f32), jnp.zeros((B, H), f32))
    xs = tuple(jnp.moveaxis(t, 1, 0) for t in (c_loc, n_loc, m_loc, b_last))
    _, (c0, n0, m0) = lax.scan(step, init, xs)
    c0, n0, m0 = (jnp.moveaxis(t, 0, 1) for t in (c0, n0, m0))

    causal = jnp.tril(jnp.ones((L, L), bool))
    log_d = jnp.where(causal[:, :, None], b[:, :, :, None] - b[:, :, None] + li[:, :, None], -jnp.inf)
    log_inter = b + m0[:, :, None]
    m_t = jnp.maximum(log_inter, jnp.max(log_d, axis=3))
    dmat = jnp.exp(log_d - m_t[:, :, :, None])
    a_inter = jnp.exp(log_inter - m_t)
    s = jnp.einsum('bcthd,bcshd->bctsh', q, k) * dmat
    num = jnp.einsum('bctsh,bcshd->bcthd', s, v) + a_inter[..., None] * jnp.einsum('bchde,bcthe->bcthd', c0, q)
    den = jnp.sum(s, axis=3) + a_inter * jnp.einsum('bche,bcthe->bcth', n0, q)
    h = num / jnp.maximum(jnp.abs(den), jnp.exp(-m_t))[..., None]
    return h.reshape(B, S, H, DH)

def _s5_ssm(u, lam_re, lam_im, log_dt, b_re, b_im, c_re, c_im, d_skip):
    f32 = jnp.float32
    lam = lax.complex(lam_re.astype(f32), lam_im.astype(f32))
    dt = jnp.exp(log_dt.astype(f32))[:, None]
    lam_bar = jnp.exp(lam * dt)
    b_bar = ((lam_bar - 1.0) / lam)[..., None] * lax.complex(b_re.astype(f32), b_im.astype(f32))
    c_mat = lax.complex(c_re.astype(f32), c_im.astype(f32))
    bu = jnp.einsum('gpc,bsgc->sbgp', b_bar, u.astype(jnp.complex64))
    a = jnp.broadcast_to(lam_bar, (u.shape[1],) + lam_bar.shape)

    def combine(e1, e2):
        a1, x1 = e1
        a2, x2 = e2
        return a1 * a2, a2[:, None] * x1 + x2

    _, states = lax.associative_scan(combine, (a, bu), axis=0)
    y = jnp.einsum('gcp,sbgp->bsgc', c_mat, states).real
    return y + d_skip.astype(f32) * u

def _mlstm_s5_mixer(h, w_in, conv_w, b_i, b_f, head_g, lam_re, lam_im, log_dt,
                    b_re, b_im, c_re, c_im, d_skip, glu_w, glu_b, w_out):
    f32 = jnp.float32
    B, S, _ = h.shape
    H, DH = MLSTM_HEADS, MLSTM_DH
    proj = (h @ w_in).astype(f32)
    qk, v, o_pre, i_pre, f_pre, u = jnp.split(
        proj, [2 * MIX_A, 3 * MIX_A, 4 * MIX_A, 4 * MIX_A + H, 4 * MIX_A + 2 * H], axis=-1)
    qk = jax.nn.silu(_causal_conv(qk, conv_w.astype(f32)))
    q, k = jnp.split(qk, 2, axis=-1)
    hm = _mlstm_chunkwise(q.reshape(B, S, H, DH), k.reshape(B, S, H, DH), v.reshape(B, S, H, DH),
                          i_pre + b_i.astype(f32), f_pre + b_f.astype(f32))
    hm = hm * lax.rsqrt(jnp.mean(hm * hm, axis=-1, keepdims=True) + EPS)
    hm = jax.nn.sigmoid(o_pre) * (hm.reshape(B, S, MIX_A) * head_g.astype(f32))
    ys = jax.nn.gelu(_s5_ssm(u.reshape(B, S, S5_GROUPS, S5_GROUP), lam_re, lam_im, log_dt,
                             b_re, b_im, c_re, c_im, d_skip))
    ys = ys * jax.nn.sigmoid(jnp.einsum('bsgc,gce->bsge', ys, glu_w.astype(f32)) + glu_b.astype(f32))
    mix = jnp.concatenate([hm, ys.reshape(B, S, MIX_B)], axis=-1)
    return mix.astype(h.dtype) @ w_out

def _nsa_mixer(h, w_in, b_gate, cmp_pos, cmp_w1, cmp_b1, cmp_w2, cmp_b2, rel_bias, w_out):
    f32 = jnp.float32
    B, S, _ = h.shape
    R = NSA_HEADS // NSA_KV
    proj = (h @ w_in).astype(f32)
    q, kc, vc, ks, vs, kw, vw, g = jnp.split(proj, [D_MODEL + i * KV_W for i in range(7)], axis=-1)
    q = q.reshape(B, S, NSA_KV, R, NSA_DH).transpose(0, 2, 3, 1, 4) * NSA_DH ** -0.5
    heads = lambda t: t.reshape(B, S, NSA_KV, NSA_DH).transpose(0, 2, 1, 3)
    kc, vc, ks, vs, kw, vw = (heads(t) for t in (kc, vc, ks, vs, kw, vw))
    gates = jax.nn.sigmoid(g + b_gate.astype(f32)).reshape(B, S, NSA_KV, R, 3).transpose(0, 2, 3, 1, 4)

    n_cmp = (S - CMP_BLOCK) // CMP_STRIDE + 1
    cmp_start = jnp.arange(n_cmp) * CMP_STRIDE
    cmp_end = cmp_start + CMP_BLOCK - 1
    cmp_idx = cmp_start[:, None] + jnp.arange(CMP_BLOCK)[None]

    def compress(t, j):
        blk = t[:, :, cmp_idx] + cmp_pos[j].astype(f32)
        flat = blk.reshape(B, NSA_KV, n_cmp, CMP_BLOCK * NSA_DH)
        hid = jax.nn.gelu(flat @ cmp_w1[j].astype(f32) + cmp_b1[j].astype(f32))
        return hid @ cmp_w2[j].astype(f32) + cmp_b2[j].astype(f32)

    k_cmp = compress(kc, 0)
    v_cmp = compress(vc, 1)

    n_sel = S // SEL_BLOCK
    sel_start = jnp.arange(n_sel) * SEL_BLOCK
    overlap = jnp.clip(jnp.minimum(cmp_start[:, None] + CMP_BLOCK, sel_start[None] + SEL_BLOCK)
                       - jnp.maximum(cmp_start[:, None], sel_start[None]), 0).astype(f32) / CMP_BLOCK
    k_blocks = ks.reshape(B, NSA_KV, n_sel, SEL_BLOCK, NSA_DH)
    v_blocks = vs.reshape(B, NSA_KV, n_sel, SEL_BLOCK, NSA_DH)
    top_n = min(SEL_TOPK, n_sel)

    pad = ((0, 0), (0, 0), (WINDOW, 0), (0, 0))
    kw_pad = jnp.pad(kw, pad)
    vw_pad = jnp.pad(vw, pad)
    table = rel_bias.astype(f32).reshape(REL_BUCKETS, NSA_KV, R)
    b_idx = jnp.arange(B)[:, None, None, None]
    g_idx = jnp.arange(NSA_KV)[None, :, None, None]

    def block(jq):
        q0 = jq * NSA_QBLOCK
        t = q0 + jnp.arange(NSA_QBLOCK)
        qb = lax.dynamic_slice_in_dim(q, q0, NSA_QBLOCK, axis=3)
        gb = lax.dynamic_slice_in_dim(gates, q0, NSA_QBLOCK, axis=3)
        dist = t[:, None] - cmp_end[None]
        bias = table[_t5_bucket(dist)].transpose(2, 3, 0, 1)
        s = jnp.einsum('bgrtd,bgnd->bgrtn', qb, k_cmp) + bias
        p_cmp = _masked_softmax(s, dist >= 0, axis=-1)
        o_cmp = jnp.einsum('bgrtn,bgnd->bgrtd', p_cmp, v_cmp)
        imp = jnp.einsum('bgrtn,nj->bgtj', p_cmp, overlap)
        blk_t = (t // SEL_BLOCK)[:, None]
        jj = jnp.arange(n_sel)[None]
        forced = (jj == 0) | (jj == blk_t) | (jj == blk_t - 1)
        score = jnp.where(forced, FORCE, jnp.where(jj <= blk_t, imp, -1.0))
        _, sel = lax.top_k(score, top_n)
        ksel = k_blocks[b_idx, g_idx, sel]
        vsel = v_blocks[b_idx, g_idx, sel]
        kpos = sel[..., None] * SEL_BLOCK + jnp.arange(SEL_BLOCK)
        dist = t[:, None, None] - kpos
        bias = jnp.moveaxis(table[_t5_bucket(dist), g_idx[..., None]], -1, 2)
        s = jnp.einsum('bgrtd,bgtnsd->bgrtns', qb, ksel) + bias
        p = _masked_softmax(s, (dist >= 0)[:, :, None], axis=(-2, -1))
        o_sel = jnp.einsum('bgrtns,bgtnsd->bgrtd', p, vsel)
        kwin = lax.dynamic_slice_in_dim(kw_pad, q0, WINDOW + NSA_QBLOCK, axis=2)
        vwin = lax.dynamic_slice_in_dim(vw_pad, q0, WINDOW + NSA_QBLOCK, axis=2)
        kpos = q0 - WINDOW + jnp.arange(WINDOW + NSA_QBLOCK)
        dist = t[:, None] - kpos[None]
        mask = (dist >= 0) & (dist < WINDOW) & (kpos[None] >= 0)
        bias = table[_t5_bucket(dist)].transpose(2, 3, 0, 1)
        s = jnp.einsum('bgrtd,bgkd->bgrtk', qb, kwin) + bias
        p = _masked_softmax(s, mask, axis=-1)
        o_win = jnp.einsum('bgrtk,bgkd->bgrtd', p, vwin)
        return gb[..., 0:1] * o_cmp + gb[..., 1:2] * o_sel + gb[..., 2:3] * o_win

    out = lax.map(block, jnp.arange(S // NSA_QBLOCK))
    out = out.transpose(1, 0, 4, 2, 3, 5).reshape(B, S, D_MODEL)
    return out.astype(h.dtype) @ w_out

def _hier_moe(h, wg, bg, we, be, w_gate, w_up, w_down):
    f32 = jnp.float32
    B, S, D = h.shape
    hf = h.reshape(B * S, D)
    grp_logits = (hf @ wg).astype(f32) + bg.astype(f32)
    _, g_top = lax.top_k(grp_logits, 1)
    p_g = jnp.take_along_axis(jax.nn.softmax(grp_logits, axis=-1), g_top, axis=1)
    exp_logits = jnp.einsum('nd,dge->nge', hf, we).astype(f32) + be.astype(f32)
    in_grp = jnp.take_along_axis(exp_logits, g_top[:, :, None], axis=1)[:, 0]
    top_v, top_i = lax.top_k(in_grp, MOE_TOPK)
    w = jax.nn.softmax(top_v, axis=-1) * p_g
    expert_id = g_top * MOE_PER_GROUP + top_i
    gate = jnp.sum(jax.nn.one_hot(expert_id, MOE_EXPERTS, dtype=f32) * w[..., None], axis=1)
    hid = jax.nn.silu(jnp.einsum('nd,edf->nef', hf, w_gate)) * jnp.einsum('nd,edf->nef', hf, w_up)
    y = jnp.einsum('nef,efd->nd', hid * gate[:, :, None].astype(hid.dtype), w_down)
    return y.reshape(B, S, D)

def setup_inputs(seed: int = 0) -> dict:
    key = jax.random.key(seed)
    ks = iter(jax.random.split(key, 40))
    f32 = jnp.float32
    nrm = lambda shape, std: jax.random.normal(next(ks), shape, f32) * std
    D = D_MODEL
    G, P, C = S5_GROUPS, S5_STATE, S5_GROUP
    inp = {}
    inp['x'] = nrm((BATCH, SEQ, D), 1.0)
    inp['c'] = nrm((BATCH, D), 1.0)
    inp['rel_bias'] = nrm((REL_BUCKETS, NSA_HEADS), 0.1)
    inp['ada_w'] = nrm((DEPTH, 2, D, 3 * D), 0.5 * D ** -0.5)
    inp['ada_b'] = nrm((DEPTH, 2, 3 * D), 0.02)
    inp['norm_g'] = 1.0 + nrm((DEPTH, 2, D), 0.05)
    inp['final_g'] = 1.0 + nrm((D,), 0.05)
    inp['a_w_in'] = nrm((N_EVEN, D, IN_A), D ** -0.5)
    inp['a_conv'] = nrm((N_EVEN, CONV_K, 2 * MIX_A), CONV_K ** -0.5)
    inp['a_b_i'] = nrm((N_EVEN, MLSTM_HEADS), 0.1)
    inp['a_b_f'] = jnp.linspace(3.0, 6.0, MLSTM_HEADS, dtype=f32) + nrm((N_EVEN, MLSTM_HEADS), 0.1)
    inp['a_head_g'] = 1.0 + nrm((N_EVEN, MIX_A), 0.05)
    inp['s5_lam_re'] = -0.5 + nrm((N_EVEN, G, P), 0.01)
    inp['s5_lam_im'] = jnp.pi * jnp.arange(P, dtype=f32) + nrm((N_EVEN, G, P), 0.01)
    inp['s5_log_dt'] = jax.random.uniform(next(ks), (N_EVEN, G), f32, math.log(DT_MIN), math.log(DT_MAX))
    inp['s5_b_re'] = nrm((N_EVEN, G, P, C), (2 * C) ** -0.5)
    inp['s5_b_im'] = nrm((N_EVEN, G, P, C), (2 * C) ** -0.5)
    inp['s5_c_re'] = nrm((N_EVEN, G, C, P), P ** -0.5)
    inp['s5_c_im'] = nrm((N_EVEN, G, C, P), P ** -0.5)
    inp['s5_d'] = nrm((N_EVEN, G, C), 1.0)
    inp['s5_glu_w'] = nrm((N_EVEN, G, C, C), C ** -0.5)
    inp['s5_glu_b'] = nrm((N_EVEN, G, C), 0.02)
    inp['a_w_out'] = nrm((N_EVEN, D, D), D ** -0.5)
    inp['n_w_in'] = nrm((N_ODD, D, IN_C), D ** -0.5)
    inp['n_b_gate'] = nrm((N_ODD, 3 * NSA_HEADS), 0.1)
    inp['n_cmp_pos'] = nrm((N_ODD, 2, CMP_BLOCK, NSA_DH), 0.1)
    inp['n_cmp_w1'] = nrm((N_ODD, 2, CMP_BLOCK * NSA_DH, CMP_HIDDEN), (CMP_BLOCK * NSA_DH) ** -0.5)
    inp['n_cmp_b1'] = nrm((N_ODD, 2, CMP_HIDDEN), 0.02)
    inp['n_cmp_w2'] = nrm((N_ODD, 2, CMP_HIDDEN, NSA_DH), CMP_HIDDEN ** -0.5)
    inp['n_cmp_b2'] = nrm((N_ODD, 2, NSA_DH), 0.02)
    inp['n_w_out'] = nrm((N_ODD, D, D), D ** -0.5)
    inp['r_grp_w'] = nrm((DEPTH, D, MOE_GROUPS), D ** -0.5)
    inp['r_grp_b'] = nrm((DEPTH, MOE_GROUPS), 0.01)
    inp['r_exp_w'] = nrm((DEPTH, D, MOE_GROUPS, MOE_PER_GROUP), D ** -0.5)
    inp['r_exp_b'] = nrm((DEPTH, MOE_GROUPS, MOE_PER_GROUP), 0.01)
    inp['e_w_gate'] = nrm((DEPTH, MOE_EXPERTS, D, MOE_HIDDEN), D ** -0.5)
    inp['e_w_up'] = nrm((DEPTH, MOE_EXPERTS, D, MOE_HIDDEN), D ** -0.5)
    inp['e_w_down'] = nrm((DEPTH, MOE_EXPERTS, MOE_HIDDEN, D), MOE_HIDDEN ** -0.5)
    return inp

def reference(x, c, rel_bias, ada_w, ada_b, norm_g, final_g,
              a_w_in, a_conv, a_b_i, a_b_f, a_head_g,
              s5_lam_re, s5_lam_im, s5_log_dt, s5_b_re, s5_b_im, s5_c_re, s5_c_im,
              s5_d, s5_glu_w, s5_glu_b, a_w_out,
              n_w_in, n_b_gate, n_cmp_pos, n_cmp_w1, n_cmp_b1, n_cmp_w2, n_cmp_b2, n_w_out,
              r_grp_w, r_grp_b, r_exp_w, r_exp_b, e_w_gate, e_w_up, e_w_down):
    mod = jnp.einsum('bd,lkde->lkbe', jax.nn.silu(c), ada_w) + ada_b[:, :, None, :]
    for layer in range(DEPTH):
        shift, scale, gate = jnp.split(mod[layer, 0], 3, axis=-1)
        h = _modulate(x, norm_g[layer, 0], shift, scale)
        if layer % 2 == 0:
            j = layer // 2
            y = _mlstm_s5_mixer(h, a_w_in[j], a_conv[j], a_b_i[j], a_b_f[j], a_head_g[j],
                                s5_lam_re[j], s5_lam_im[j], s5_log_dt[j], s5_b_re[j], s5_b_im[j],
                                s5_c_re[j], s5_c_im[j], s5_d[j], s5_glu_w[j], s5_glu_b[j], a_w_out[j])
        else:
            j = layer // 2
            y = _nsa_mixer(h, n_w_in[j], n_b_gate[j], n_cmp_pos[j], n_cmp_w1[j], n_cmp_b1[j],
                           n_cmp_w2[j], n_cmp_b2[j], rel_bias, n_w_out[j])
        x = x + gate[:, None, :] * y
        shift, scale, gate = jnp.split(mod[layer, 1], 3, axis=-1)
        h = _modulate(x, norm_g[layer, 1], shift, scale)
        x = x + gate[:, None, :] * _hier_moe(h, r_grp_w[layer], r_grp_b[layer], r_exp_w[layer], r_exp_b[layer],
                                             e_w_gate[layer], e_w_up[layer], e_w_down[layer])
    return _rmsnorm(x, final_g)


_drawn_inputs = setup_inputs


def setup_inputs(seed=0):
    import zlib

    import numpy as np

    out = dict(_drawn_inputs(seed))
    spreads = {}
    factors = {'rel_bias': 7.231,
     'a_b_i': 195.037,
     'a_head_g': 6.438,
     's5_lam_re': 64.0,
     's5_lam_im': 35.144,
     's5_log_dt': 46.544,
     's5_b_re': 49.712,
     's5_b_im': 52.976,
     's5_c_re': 40.16,
     's5_c_im': 42.232,
     's5_glu_b': 64.0,
     'n_b_gate': 8.0,
     'n_cmp_pos': 5.199,
     'n_cmp_b1': 31.133,
     'n_cmp_b2': 21.776,
     'r_grp_b': 15.448,
     'r_exp_b': 29.144}
    for name, (base, spread) in spreads.items():
        noise = np.random.default_rng([zlib.crc32(name.encode()), seed]).standard_normal(out[name].shape)
        drawn = base * np.exp(spread * noise) if base else spread * noise
        out[name] = __import__('jax').numpy.asarray(drawn.astype(out[name].dtype))
    for name, factor in factors.items():
        out[name] = (out[name] * factor).astype(out[name].dtype)
    return out
```

```python
from contextlib import ExitStack

import numpy as np

import concourse.bass as bass
from concourse import mybir

F32 = mybir.dt.float32
ALU = mybir.AluOpType
ACT = mybir.ActivationFunctionType
AX = mybir.AxisListType

P = 128
T = 512
D = 1024
KD = D // P
NT = T // P
MA = 512
MH = 4
G5, S5P, S5C = 32, 64, 16
TAU = 8
NCH = T // TAU
NPW = TAU + 1
NH, NKV, R, DH = 16, 4, 4, 64
NCMP, CL, CS = 31, 32, 16
CH = 256
NE, NG, NPG, FH = 16, 4, 4, 256
EPS = 1e-6
NEG = -1e30
REP = 8
BUCKETS, MAXD = 32, 128
NSLOT = 4
PB = 128
CC = 256
PI = float(np.pi)
C1 = 6.28125
C2 = float(np.float32(2 * np.pi - C1))
C3 = float(2 * np.pi - C1 - C2)
MAGIC = 12582912.0

STAGES = [("x", KD), ("param", 1), ("ct", 2), ("ada0", 1), ("s5_e", 8), ("s5_g", 8), ("norm0", 1),
          ("u", 4), ("u2", 8), ("ut", 4), ("gates", 2), ("qk", 4), ("s5_e1", 4), ("s5_eb", 4), ("qk2", 4),
          ("s5_zb", 4), ("s5_y", 4), ("v", 8), ("s5_glu", 4), ("o", 8), ("s5_k", 4), ("s5_t", 4),
          ("gcol", 1)]
STAGES += [("ml_h", 4 + MH * (1 + NT + 2)), ("ml_t", MH), ("ada1", 1), ("aout", KD), ("norm1", 1)]


EM = 1 + 4 + KD


def moe_stages(l):
    return [(f"route{l}", 1), (f"gt{l}", 1), (f"moe{l}", NE * EM)]


STAGES += moe_stages(0)
ITEMS = [(i, h, b) for i in range(NT) for h in range(NH) for b in range(2)]
NI = len(ITEMS)
ATT_ORDER = [(k, n - lag) for n in range(NI + 3) for k, lag in (("s", 0), ("t", 2), ("o", 3)) if 0 <= n - lag < NI]
ATT = {x: i for i, x in enumerate(ATT_ORDER)}
STAGES += [("ada2", 1), ("norm2", 1), ("nq", 8), ("nkc", 4), ("nks", 2), ("nvs", 4), ("nkw", 2),
           ("nvw", 4), ("ngate", 1), ("fvec", 2), ("biasc", 4), ("cpos", 4), ("chid", 4), ("kcmp", 1), ("vcmp", 1),
           ("cmpa", 5 * NT), ("att", len(ATT_ORDER)), ("ot", KD), ("ada3", 1), ("nout", KD), ("norm3", 1)]
STAGES += moe_stages(1)
STAGES += [("norm4", 1), ("xo", 8)]
BASE = {}
_n = 0
for _name, _count in STAGES:
    BASE[_name] = _n
    _n += _count

CHUNKS = ([("ada", 0, c) for c in range(12)] + [("ain", 0, c) for c in (8, 9, 0, 1, 2, 3, 4, 5, 6, 7)]
          + [("ada", 1, c) for c in range(12)] + [("aout", 0, c) for c in range(4)]
          + [(w, 0, e) for e in range(NE) for w in ("eg", "eu", "ed")]
          + [("ada", 2, c) for c in range(12)] + [("nin", 0, c) for c in range(10)]
          + [("cw", j, c) for j in range(2) for c in range(2)]
          + [("ada", 3, c) for c in range(12)] + [("nout", 0, c) for c in range(4)]
          + [(w, 1, e) for e in range(NE) for w in ("eg", "eu", "ed")])
CIDX = {c: i for i, c in enumerate(CHUNKS)}
LAST_TILE = {("ain", 0, 8): ("u", 1), ("ain", 0, 9): ("u", 3), ("ain", 0, 0): ("qk", 1), ("ain", 0, 1): ("qk", 3),
             ("ain", 0, 2): ("qk2", 1), ("ain", 0, 3): ("qk2", 3), ("ain", 0, 4): ("v", 3), ("ain", 0, 5): ("v", 7),
             ("ain", 0, 6): ("o", 3), ("ain", 0, 7): ("o", 7)}
LAST_TILE.update({("aout", 0, c): ("aout", 2 * c + 1) for c in range(4)})
LAST_TILE.update({("nin", 0, c): ("nq", 2 * c + 1) for c in range(4)})
LAST_TILE.update({("nin", 0, 4): ("nkc", 1), ("nin", 0, 5): ("nkc", 3), ("nin", 0, 6): ("nks", 1),
                  ("nin", 0, 7): ("nvs", 3), ("nin", 0, 8): ("nkw", 1), ("nin", 0, 9): ("nvw", 3)})
LAST_TILE.update({(w, l, e): (f"moe{l}", EM * e + i) for l in range(2) for e in range(NE)
                  for w, i in (("eg", 2), ("eu", 4), ("ed", EM - 1))})
LAST_TILE.update({("nout", 0, c): ("nout", 2 * c + 1) for c in range(4)})


NAMES = ["x", "c", "rel_bias", "ada_w", "ada_b", "norm_g", "final_g", "a_w_in", "a_conv", "a_b_i", "a_b_f",
         "a_head_g", "s5_lam_re", "s5_lam_im", "s5_log_dt", "s5_b_re", "s5_b_im", "s5_c_re", "s5_c_im", "s5_d",
         "s5_glu_w", "s5_glu_b", "a_w_out", "n_w_in", "n_b_gate", "n_cmp_pos", "n_cmp_w1", "n_cmp_b1",
         "n_cmp_w2", "n_cmp_b2", "n_w_out", "r_grp_w", "r_grp_b", "r_exp_w", "r_exp_b", "e_w_gate", "e_w_up",
         "e_w_down"]


def dims(ap, *free, off=0):
    return bass.AP(tensor=ap.tensor, offset=ap.offset + off, ap=[list(ap.ap[0])] + [list(f) for f in free])


def build(nc, a, onehot, out):
    bias_d = nc.dram_tensor("bias_rev", [NH, REP, 1024], F32, kind="Internal").ap()
    with ExitStack() as ctx:
        def sb(name, shape):
            return ctx.enter_context(nc.sbuf_tensor(name, shape, F32))

        def sem(name):
            return ctx.enter_context(nc.semaphore(name))

        banks = [ctx.enter_context(nc.psum_tensor(f"bank{i}", [P, 512], F32)) for i in range(8)]
        ring = sb("ring", [P, NSLOT, KD, CC])
        xT = sb("xT", [P, KD, T])
        hT = sb("hT", [P, KD, T])
        mixT = sb("mixT", [P, KD, T])
        arena = sb("arena", [P, 27136])
        ident = sb("ident", [P, P])
        ones = sb("ones", [P, P])
        par = sb("par", [P, 128 + 96])
        mod = sb("mod", [P, 4, 24])
        amul = sb("amul", [P, KD])
        sil = sb("sil", [P, KD])
        rstd = sb("rstd", [P, T])
        small = sb("small", [P, 96])

        def region(start, shape, parts=P, of=arena):
            n = int(np.prod(shape))
            ap = of[0:parts, start:start + n]
            if len(shape) == 1:
                return ap
            letters = "abcde"[:len(shape)]
            return ap.rearrange(f"p ({' '.join(letters)}) -> p {' '.join(letters)}",
                                **{x: s for x, s in zip(letters[1:], shape[1:])})

        Mt = region(0, [G5, P])
        ET = region(4096, [G5, P])
        Vaug = region(4096, [NT, MH, 129])
        F9 = region(8192, [G5, NPW, S5C])
        twc = region(12800, [G5, NCH])
        tws = region(14848, [G5, NCH])
        hmx = region(12800, [NT, MH, P])
        uk = region(16896, [G5, TAU, S5C])
        uk2 = region(16896, [TAU, MA], parts=NCH)
        Gk = region(16896, [G5, P], parts=16)
        ea = region(16896, [G5, NCH])
        za = region(18944, [G5, NCH])
        Wb = [region(16896 + 2048 * i, [NT, T]) for i in range(2)]
        qkT = region(20992, [KD, T])
        Ug = region(25088, [G5, NCH])
        Ba = region(20992, [G5, S5C])
        Bb = region(21504, [G5, S5C])
        Ca = region(22016, [G5, S5C])
        Cb = region(22528, [G5, S5C])
        Bba = region(23040, [G5, S5C])
        Bbb = region(23552, [G5, S5C])
        pc = region(24064, [G5, NPW])
        ps = region(24352, [G5, NPW])
        pt = region(24640, [G5, NPW])
        crow = region(25088, [2, 4, P])
        lrow = region(26112, [2, P], parts=32)
        s5s = region(26368, [16, G5])
        Ea = region(0, [G5, TAU, S5C], of=mixT[:, :, :].rearrange("p a b -> p (a b)"))
        so = region(0, [NT, MA], of=mixT[:, :, :].rearrange("p a b -> p (a b)"))
        F9f = region(8192, [G5, NPW * S5C])

        acc = region(0, [KD, T])
        hid = region(4096, [2, 2, T])
        sg = region(6144, [2, T])
        gT = region(7168, [T], parts=NE)
        rt = region(7680, [512])
        wr = sb("wr", [P, 2, KD, NG + NE])
        rb = sb("rb", [P, 2, NG + NE])
        biasT = region(0, [NH, T])
        biasC = region(8192, [NT, NH, 32])
        kTd = region(10240, [2, NKV, T])
        vN = region(14336, [2, NT, CC])
        kc2 = region(16384, [2, NKV, T + 1])
        on = region(16384, [NT, D])
        Pw = region(20488, [4, T])
        PT = region(22536, [4, T])
        oh = region(20488, [1024], parts=33)
        chid = region(22536, [2, 2, NKV, 32])
        wng = region(24584, [KD, 48])
        w2k = region(24968, [2, P])
        w2v = region(25224, [2, DH])
        b2v = region(25352, [DH])
        bng = region(25416, [48])
        gts = region(25464, [NT, 48])
        tab = region(25656, [NH], parts=33)
        kcT = region(25672, [NKV, 32])
        Vc = region(25800, [NKV, CC])
        cb = region(26824, [2, 2])
        stat = region(26832, [128])
        qT = mixT
        frs = region(23560, [1024], parts=NH)
        osb = region(8192, [NT, D])

        wif = sb("wif", [P, KD, 8])
        gluw = region(6160, [4, P])
        vecs = sb("vecs", [P, 8])
        d5 = sb("d5", [16, G5])
        glub = sb("glub", [P, G5])
        headg = region(6672, [MA])
        perm = sb("perm", [P, P])
        cpad = sb("cpad", [P, 2, T + 3])
        ct1 = sb("ct1", [P, T])
        grow = sb("grow", [4, 3, T])
        gcol = sb("gcol", [P, 2, NT, MH])
        sgn = sb("sgn", [P, 1])
        jj = sb("jj", [P, NCH])
        cmask = sb("cmask", [P, P])
        r8 = sb("r8", [P, G5])
        raw = sb("raw", [P, 2, P])

        wsem = [sem(f"chunk_in{i}") for i in range(NSLOT)]
        ada_used = sem("ada_used")
        full = [sem(f"bank_full{i}") for i in range(8)]
        free = [sem(f"bank_free{i}") for i in range(8)]
        names = ["x_in", "raw_in", "small_in", "const_ready", "x_ready", "par_ready", "sil_ready", "mod_ready",
                 "pow_ready", "e_ready", "et_ready", "g_ready", "m_in", "sq_ready", "h_part", "h_ready",
                 "uk_ready", "ug_ready", "act_s5", "dve_s5", "ea_ready", "za_ready", "xs_ready", "y_ready",
                 "ys_ready", "glu_in", "glu_used", "gates_ready", "gcol_ready", "cpad_ready", "conv_ready", "sig_ready",
                 "qk_ready", "v_ready", "so_ready", "arg_ready", "dexp_ready", "w_ready", "hm_ready",
                 "mixh_ready", "mix_ready", "x_upd", "dve_chain", "act_chain", "pool_chain", "dbg_out",
                 "sqrt_ready", "rs_ready", "sk_ready", "st_ready", "diag_ready", "var_ready", "act_gate",
                 "uk_free", "out_sem", "headg_in", "ut_ready", "cw_used", "out_ready", "wr_in", "gate_t", "esig", "hid_ready", "acc_chain",
                 "nsa_in", "oh_in", "q_ready", "kc_ready", "ktd_ready", "vn_ready", "f_ready", "f_out", "bias_in",
                 "biasc_ready", "cb_ready", "chid_ready", "kcmp_ready", "vcmp_ready", "cs_ready", "ce_ready", "cp_ready",
                 "pct_ready", "p_ready", "e_done", "pt_ready", "o_ready", "ot_ready", "ng_ready", "gsig", "route_e", "route_s", "cpre"]
        S = {n: sem(n) for n in names}

        def bank(stage, i=0):
            return banks[(BASE[stage] + i) % 8]

        def wait_full(eng, stage, i=0):
            n = BASE[stage] + i
            eng.wait_ge(full[n % 8], n // 8 + 1)

        def wait_bank(eng, stage, i=0):
            n = BASE[stage] + i
            if n // 8:
                eng.wait_ge(free[n % 8], n // 8)

        def fsem(stage, i=0):
            return full[(BASE[stage] + i) % 8]

        def rsem(stage, i=0):
            return free[(BASE[stage] + i) % 8]

        block = ctx.enter_context(nc.Block())

        @block.sync
        def _(sp):
            for t in range(NT):
                sp.dma_start(hT[:, 2 * t:2 * t + 2, :].rearrange("p a b -> p (a b)"),
                             a["x"][0, t * P:(t + 1) * P, :]).then_inc(S["x_in"], 16)
            ain_cols = [0, 256, 512, 768, 1024, 1280, 1536, 1792, 2056, 2312]
            src = {
                "ada": lambda m, c: a["ada_w"][m // 2, m % 2, :, c * CC:(c + 1) * CC],
                "ain": lambda m, c: a["a_w_in"][0, :, ain_cols[c]:ain_cols[c] + CC],
                "aout": lambda m, c: a["a_w_out"][0, :, c * CC:(c + 1) * CC],
                "nin": lambda m, c: a["n_w_in"][0, :, c * CC:(c + 1) * CC],
                "nout": lambda m, c: a["n_w_out"][0, :, c * CC:(c + 1) * CC],
                "cw": lambda j, c: a["n_cmp_w1"][0, j, c * 1024:(c + 1) * 1024, :],
                "eg": lambda l, e: a["e_w_gate"][l, e],
                "eu": lambda l, e: a["e_w_up"][l, e],
                "ed": lambda l, e: a["e_w_down"][l, e],
            }
            for i, (kind, m, c) in enumerate(CHUNKS):
                if i >= NSLOT:
                    k0, m0, c0 = CHUNKS[i - NSLOT]
                    if k0 == "cw":
                        sp.wait_ge(S["cw_used"], 2 * m0 + c0 + 1)
                    elif k0 == "ada":
                        sp.wait_ge(ada_used, 12 * m0 + c0 + 1)
                    else:
                        wait_full(sp, *LAST_TILE[(k0, m0, c0)])
                dst = ring[:, i % NSLOT, :, :]
                w = src[kind](m, c)
                if kind == "ed":
                    dst = dst.rearrange("p k c -> p (k c)").rearrange("p (k c) -> p k c", c=D)
                sp.dma_start(dst, w.rearrange("(k p) c -> p k c", p=P)).then_inc(wsem[i % NSLOT], 16)
            for t in range(NT):
                sp.wait_ge(S["out_ready"], 2 * t + 2)
                sp.dma_start(out[0, t * P:(t + 1) * P, :], osb[:, t, :]).then_inc(S["out_sem"], 16)
            sp.wait_ge(S["out_sem"], 16 * NT)

        def chunk(kind, m, c):
            return ring[:, CIDX[(kind, m, c)] % NSLOT]

        def wait_chunk(eng, kind, m, c):
            i = CIDX[(kind, m, c)]
            eng.wait_ge(wsem[i % NSLOT], 16 * (i // NSLOT + 1))

        small_loads = []

        def skv(tau, i):
            return uk2[:, tau, i * P:(i + 1) * P]

        @block.tensor
        def _(pe):
            mm, tr = nc.tensor.matmul, nc.tensor.transpose
            pe.wait_ge(S["const_ready"], 1)
            pe.wait_ge(S["x_in"], 16 * NT)
            for j in range(KD):
                for t in range(NT):
                    xin = hT[:, 2 * t:2 * t + 2, :].rearrange("p a b -> p (a b)")
                    last = tr(bank("x", j)[:, t * P:(t + 1) * P], xin[:, j * P:(j + 1) * P], ident[:, :])
                last.then_inc(fsem("x", j), 1)
            wait_bank(pe, "param")
            pe.wait_ge(S["raw_in"], RAW_IN)
            b = bank("param")
            tr(b[:, 0:128], raw[:, 0, :], ident[:, :])
            tr(b[:, 128:224], raw[0:96, 1, :], ident[0:96, 0:96])
            tr(b[:, 224:256], lrow[:, 0, :], ident[0:32, 0:32])
            tr(b[:, 256:288], lrow[:, 1, :], ident[0:32, 0:32]).then_inc(fsem("param"), 1)
            for s in range(2):
                wait_bank(pe, "ct", s)
                for t in range(4):
                    last = tr(bank("ct", s)[:, t * P:(t + 1) * P], crow[:, s, t, :], ident[:, :])
                last.then_inc(fsem("ct", s), 1)

            def ada(m):
                wait_bank(pe, f"ada{m}")
                pe.wait_ge(S["sil_ready"], 1)
                for c in range(12):
                    wait_chunk(pe, "ada", m, c)
                    w = chunk("ada", m, c)
                    for j in range(2):
                        for k in range(KD):
                            last = mm(bank(f"ada{m}")[:, 2 * c + j:2 * c + j + 1], w[:, k, j * P:(j + 1) * P],
                                      sil[:, k:k + 1], start=(k == 0), stop=(k == KD - 1))
                    last.then_inc(ada_used, 1)
                mm(bank(f"ada{m}")[:, 32:33], ones[:, :], sil[:, 0:1], start=True, stop=True).then_inc(fsem(f"ada{m}"), 1)

            def norm(m):
                wait_bank(pe, f"norm{m}")
                b = bank(f"norm{m}")
                for k in range(KD):
                    pe.wait_ge(S["sq_ready"], KD * m + k + 1)
                    last = mm(b[:, :], ones[:, :], hT[:, k, :], start=(k == 0), stop=(k == KD - 1))
                last.then_inc(fsem(f"norm{m}"), 1)

            ada(0)
            for g in range(G5):
                if g % 4 == 0:
                    wait_bank(pe, "s5_e", g // 4)
                    pe.wait_ge(S["e_ready"], 1)
                last = tr(bank("s5_e", g // 4)[:, (g % 4) * P:(g % 4 + 1) * P],
                          Ea[:, g].rearrange("p a b -> p (a b)"), ident[:, :])
                if g % 4 == 3:
                    last.then_inc(fsem("s5_e", g // 4), 1)
            for g in range(G5):
                if g % 4 == 0:
                    wait_bank(pe, "s5_g", g // 4)
                    pe.wait_ge(S["pow_ready"], 1)
                last = mm(bank("s5_g", g // 4)[0:16, (g % 4) * P:(g % 4 + 1) * P], Bba[:, g, :],
                          F9f[:, g, 0:P], start=True, stop=True)
                if g % 4 == 3:
                    last.then_inc(fsem("s5_g", g // 4), 1)
            norm(0)

            def tok_proj(stage, kind, m, cs, lhs, nwait=False):
                for n, c in enumerate(cs):
                    wait_chunk(pe, kind, m, c)
                    for t in range(NT):
                        wait_bank(pe, stage, 4 * n + t)
                        for k in range(KD):
                            last = mm(bank(stage, 4 * n + t)[:, 0:CC], lhs(k, t), chunk(kind, m, c)[:, k, :],
                                      start=(k == 0), stop=(k == KD - 1))
                        last.then_inc(fsem(stage, 4 * n + t), 1)

            def ch_proj(stage, kind, m, cs, first=0):
                for n, c in enumerate(cs):
                    wait_chunk(pe, kind, m, c)
                    for j in range(2):
                        i = first + 2 * n + j
                        wait_bank(pe, stage, i)
                        for k in range(KD):
                            last = mm(bank(stage, i)[:, :], chunk(kind, m, c)[:, k, j * P:(j + 1) * P], hT[:, k, :],
                                      start=(k == 0), stop=(k == KD - 1))
                        last.then_inc(fsem(stage, i), 1)

            pe.wait_ge(S["h_ready"], KD)
            ch_proj("u", "ain", 0, (8, 9))
            for i in range(8):
                wait_bank(pe, "u2", i)
                pe.wait_ge(S["ut_ready"], 4)
                for q in range(4):
                    last = tr(bank("u2", i)[0:NCH, q * P:(q + 1) * P],
                              dims(Ug[:, 8 * (i // 2), :], [TAU, NCH], off=4 * (i % 2) + q), ident[:, :])
                last.then_inc(fsem("u2", i), 1)
            for g in range(G5):
                if g % 8 == 0:
                    wait_bank(pe, "ut", g // 8)
                    pe.wait_ge(S["uk_ready"], 8)
                last = tr(bank("ut", g // 8)[:, (g % 8) * NCH:(g % 8 + 1) * NCH],
                          uk[0:NCH, g].rearrange("p a b -> p (a b)"), ident[0:NCH, 0:NCH])
                if g % 8 == 7:
                    last.then_inc(fsem("ut", g // 8), 1)
            for s in range(2):
                wait_bank(pe, "gates", s)
                for k in range(KD):
                    last = mm(bank("gates", s)[0:4, :], wif[:, k, 4 * s:4 * s + 4], hT[:, k, :],
                              start=(k == 0), stop=(k == KD - 1))
                last.then_inc(fsem("gates", s), 1)
            ch_proj("qk", "ain", 0, (0, 1))
            for g in range(G5):
                if g % 8 == 0:
                    wait_bank(pe, "s5_e1", g // 8)
                    pe.wait_ge(S["ug_ready"], 4)
                    pe.wait_ge(S["et_ready"], 8)
                last = mm(bank("s5_e1", g // 8)[:, (g % 8) * NCH:(g % 8 + 1) * NCH], ET[:, g, :], Ug[:, g, :],
                          start=True, stop=True)
                if g % 8 == 7:
                    last.then_inc(fsem("s5_e1", g // 8), 1)
            for i in range(4):
                wait_bank(pe, "s5_eb", i)
                pe.wait_ge(S["ea_ready"], i + 1)
                mm(bank("s5_eb", i)[:, :], perm[:, :], ea[:, 8 * i:8 * i + 8, :].rearrange("p a b -> p (a b)"),
                   start=True, stop=True).then_inc(fsem("s5_eb", i), 1)
            ch_proj("qk2", "ain", 0, (2, 3))
            for i in range(4):
                wait_bank(pe, "s5_zb", i)
                pe.wait_ge(S["za_ready"], 1)
                mm(bank("s5_zb", i)[:, :], perm[:, :], za[:, 8 * i:8 * i + 8, :].rearrange("p a b -> p (a b)"),
                   start=True, stop=True).then_inc(fsem("s5_zb", i), 1)
            pe.wait_ge(S["m_in"], 16 * TAU)
            pe.wait_ge(S["xs_ready"], 4)
            for g in range(G5):
                if g % 8 == 0:
                    wait_bank(pe, "s5_y", g // 8)
                o = bank("s5_y", g // 8)[:, (g % 8) * NCH:(g % 8 + 1) * NCH]
                mm(o, Mt[:, g, :], Ug[:, g, :], start=True, stop=False)
                last = mm(o[:, 1:NCH], F9f[:, g, S5C:S5C + P], ea[:, g, 0:NCH - 1], start=False, stop=True)
                if g % 8 == 7:
                    last.then_inc(fsem("s5_y", g // 8), 1)
            tok_proj("v", "ain", 0, (4, 5), lambda k, t: hT[:, k, t * P:(t + 1) * P])
            for g in range(G5):
                if g % 8 == 0:
                    wait_bank(pe, "s5_glu", g // 8)
                    pe.wait_ge(S["y_ready"], g // 8 + 1)
                if g % 4 == 0:
                    pe.wait_ge(S["glu_in"], 16 * TAU * (g // 4 + 1))
                last = mm(bank("s5_glu", g // 8)[:, (g % 8) * NCH:(g % 8 + 1) * NCH], gluw[:, g % 4, :],
                          za[:, g, :], start=True, stop=True)
                if g % 8 == 7:
                    last.then_inc(fsem("s5_glu", g // 8), 1)
                elif g % 4 == 3:
                    last.then_inc(S["glu_used"], 1)
            tok_proj("o", "ain", 0, (6, 7), lambda k, t: hT[:, k, t * P:(t + 1) * P])
            for i in range(8):
                st, ii = ("s5_k", i) if i < 4 else ("s5_t", i - 4)
                wait_bank(pe, st, ii)
                pe.wait_ge(S["ys_ready"], 4)
                for g in range(4 * i, 4 * i + 4):
                    last = tr(bank(st, ii)[0:NCH, (g % 4) * P:(g % 4 + 1) * P], Ug[:, g, :], ident[:, :])
                last.then_inc(fsem(st, ii), 1)
            wait_bank(pe, "gcol")
            pe.wait_ge(S["gates_ready"], 1)
            for s in range(2):
                for t in range(NT):
                    last = tr(bank("gcol")[:, (s * NT + t) * MH:(s * NT + t + 1) * MH],
                              grow[:, s, t * P:(t + 1) * P], ident[0:4, 0:4])
            last.then_inc(fsem("gcol"), 1)
            n = BASE["ml_h"]
            for i in range(KD // 2):
                pe.wait_ge(S["sk_ready"], 8)
                wait_bank(pe, "ml_h", i)
                for tau in range(TAU):
                    last = tr(bank("ml_h", i)[:, tau * NCH:(tau + 1) * NCH], skv(tau, i), ident[0:NCH, 0:NCH])
                last.then_inc(fsem("ml_h", i), 1)
            n = 4
            for h in range(MH):
                wait_bank(pe, "ml_h", n)
                mm(bank("ml_h", n)[:, :], dims(ident[0:MH, h:h + 1], [0, P]), rstd[0:MH, :], start=True, stop=True).then_inc(fsem("ml_h", n), 1)
                n += 1
                pe.wait_ge(S["qk_ready"], KD)
                for j in range(NT):
                    wait_bank(pe, "ml_h", n)
                    mm(bank("ml_h", n)[:, j * P:], qkT[:, MH + h, j * P:(j + 1) * P], qkT[:, h, j * P:],
                       start=True, stop=True).then_inc(fsem("ml_h", n), 1)
                    n += 1
                pe.wait_ge(S["w_ready"], h + 1)
                pe.wait_ge(S["v_ready"], 8)
                for i in range(0, NT, 2):
                    wait_bank(pe, "ml_h", n)
                    for ii in range(i, i + 2):
                        for j in range(ii + 1):
                            last = mm(bank("ml_h", n)[:, (ii - i) * 129:(ii - i + 1) * 129],
                                      Wb[h % 2][:, j, ii * P:(ii + 1) * P], Vaug[:, j, h, :],
                                      start=(j == 0), stop=(j == ii))
                    last.then_inc(fsem("ml_h", n), 1)
                    n += 1
            for h in range(MH):
                wait_bank(pe, "ml_t", h)
                pe.wait_ge(S["hm_ready"], 1)
                for t in range(NT):
                    last = tr(bank("ml_t", h)[:, t * P:(t + 1) * P], hmx[:, t, h, :], ident[:, :])
                last.then_inc(fsem("ml_t", h), 1)

            def out_proj(stage, kind):
                for c in range(4):
                    wait_chunk(pe, kind, 0, c)
                    for j in range(2):
                        i = 2 * c + j
                        wait_bank(pe, stage, i)
                        for k in range(KD):
                            last = mm(bank(stage, i)[:, :], chunk(kind, 0, c)[:, k, j * P:(j + 1) * P],
                                      mixT[:, k, :], start=(k == 0), stop=(k == KD - 1))
                        last.then_inc(fsem(stage, i), 1)

            ada(1)
            pe.wait_ge(S["mixh_ready"], MH)
            pe.wait_ge(S["mix_ready"], 4)
            out_proj("aout", "aout")

            def moe(l):
                wait_bank(pe, f"route{l}")
                pe.wait_ge(S["wr_in"], 16 * 6)
                pe.wait_ge(S["h_ready"], KD * (2 * l + 2))
                for t in range(NT):
                    for k in range(KD):
                        last = mm(bank(f"route{l}")[:, 20 * t:20 * t + 20], hT[:, k, t * P:(t + 1) * P], wr[:, l, k, :],
                                  start=(k == 0), stop=(k == KD - 1))
                last.then_inc(fsem(f"route{l}"), 1)
                wait_bank(pe, f"gt{l}")
                pe.wait_ge(S["gate_t"], 2 * l + 1)
                for t in range(NT):
                    last = tr(bank(f"gt{l}")[0:NE, t * P:(t + 1) * P], rt[:, 192 + NE * t:192 + NE * t + NE], ident[:, :])
                last.then_inc(fsem(f"gt{l}"), 1)
                stg = f"moe{l}"

                def down(e):
                    wait_chunk(pe, "ed", l, e)
                    pe.wait_ge(S["hid_ready"], 2 * (NE * l + e) + 2)
                    w = chunk("ed", l, e).rearrange("p k c -> p (k c)").rearrange("p (k c) -> p k c", c=D)
                    for j in range(KD):
                        i = EM * e + 5 + j
                        wait_bank(pe, stg, i)
                        for f in range(2):
                            last = mm(bank(stg, i)[:, :], w[:, f, j * P:(j + 1) * P], hid[:, e % 2, f, :],
                                      start=(f == 0), stop=(f == 1))
                        last.then_inc(fsem(stg, i), 1)

                for e in range(NE):
                    i = EM * e
                    wait_bank(pe, stg, i)
                    if e == 0:
                        pe.wait_ge(S["gate_t"], 2 * l + 2)
                    mm(bank(stg, i)[:, :], dims(ident[0:NE, e:e + 1], [0, P]), gT[:, :], start=True,
                       stop=True).then_inc(fsem(stg, i), 1)
                    for n, kind in enumerate(("eg", "eu")):
                        wait_chunk(pe, kind, l, e)
                        for j in range(2):
                            i = EM * e + 1 + 2 * n + j
                            wait_bank(pe, stg, i)
                            for k in range(KD):
                                last = mm(bank(stg, i)[:, :], chunk(kind, l, e)[:, k, j * P:(j + 1) * P], hT[:, k, :],
                                          start=(k == 0), stop=(k == KD - 1))
                            last.then_inc(fsem(stg, i), 1)
                    down(e)

            norm(1)
            moe(0)
            ada(2)
            norm(2)
            pe.wait_ge(S["h_ready"], KD * 3)
            ch_proj("nq", "nin", 0, (0, 1, 2, 3))
            ch_proj("nkc", "nin", 0, (4, 5))
            ch_proj("nks", "nin", 0, (6,))
            tok_proj("nvs", "nin", 0, (7,), lambda k, t: hT[:, k, t * P:(t + 1) * P])
            ch_proj("nkw", "nin", 0, (8,))
            tok_proj("nvw", "nin", 0, (9,), lambda k, t: hT[:, k, t * P:(t + 1) * P])
            wait_bank(pe, "ngate")
            pe.wait_ge(S["nsa_in"], NSA_IN)
            for t in range(NT):
                for k in range(KD):
                    last = mm(bank("ngate")[:, 48 * t:48 * t + 48], hT[:, k, t * P:(t + 1) * P], wng[:, k, :],
                              start=(k == 0), stop=(k == KD - 1))
            last.then_inc(fsem("ngate"), 1)
            for i in range(2):
                wait_bank(pe, "fvec", i)
                mm(bank("fvec", i)[0:NH, :], tab[:, :], oh[:, T * i:T * i + T], start=True,
                   stop=True).then_inc(fsem("fvec", i), 1)
            for i in range(NT):
                wait_bank(pe, "biasc", i)
                for n in range(NCMP):
                    last = mm(bank("biasc", i)[:, NH * n:NH * n + NH], oh[:, T + P * i - CS * n - CL + 1:T + P * i - CS * n - CL + 1 + P],
                              tab[:, :], start=True, stop=True)
                last.then_inc(fsem("biasc", i), 1)
            for j in range(2):
                for f in range(2):
                    wait_bank(pe, "cpos", 2 * j + f)
                pe.wait_ge(S["kc_ready"], 8 * (j + 1))
                for c in range(2):
                    wait_chunk(pe, "cw", j, c)
                    w = chunk("cw", j, c)
                    for f in range(2):
                        if c == 0:
                            wait_bank(pe, "chid", 2 * j + f)
                        for k in range(8):
                            lp = 8 * c + k
                            wf = w[:, k, f * P:(f + 1) * P]
                            first, stop = lp == 0, lp == 15
                            a1 = mm(bank("chid", 2 * j + f)[:, 0:NKV * NCMP], wf,
                                    dims(kc2[:, j, 0, :], [T + 1, NKV], [CS, NCMP], off=2 * lp), start=first, stop=stop)
                            a2 = mm(bank("cpos", 2 * j + f)[:, 0:1], wf, par[:, 96 + 16 * j + lp:97 + 16 * j + lp],
                                    start=first, stop=stop)
                        if c == 1 and f == 0:
                            a1.then_inc(fsem("chid", 2 * j), 1)
                            a2.then_inc(fsem("cpos", 2 * j), 1)
                        elif c == 1:
                            a1.then_inc(fsem("chid", 2 * j + 1), 1)
                            a2.then_inc(fsem("cpos", 2 * j + 1), 1)
                        elif f == 1:
                            a2.then_inc(S["cw_used"], 1)
                mm(bank("cpos", 2 * j + 1)[:, 8:9], ones[:, :], par[:, 0:1], start=True, stop=True).then_inc(S["cw_used"], 1)
            wait_bank(pe, "kcmp")
            pe.wait_ge(S["chid_ready"], 4)
            for f in range(2):
                last = mm(bank("kcmp")[:, 0:P], w2k[:, f, :], chid[:, 0, f, :, :].rearrange("p a b -> p (a b)"), start=(f == 0), stop=(f == 1))
            last.then_inc(fsem("kcmp"), 1)
            wait_bank(pe, "vcmp")
            for g in range(NKV):
                for r in range(R):
                    for f in range(2):
                        last = mm(bank("vcmp")[32 * r:32 * r + 32, DH * g:DH * g + DH], chid[:, 1, f, g, :], w2v[:, f, :],
                                  start=(f == 0), stop=(f == 1))
            last.then_inc(fsem("vcmp"), 1)
            pe.wait_ge(S["q_ready"], KD)
            pe.wait_ge(S["kcmp_ready"], 1)
            for i in range(NT):
                for odd in range(2):
                    wait_bank(pe, "cmpa", 5 * i + odd)
                    for h in range(odd, NH, 2):
                        lo = 64 * odd
                        last = mm(bank("cmpa", 5 * i + odd)[:, 16 * (h - odd):16 * (h - odd) + 32],
                                  qT[lo:lo + 64, h // 2, i * P:(i + 1) * P], kcT[lo:lo + 64, h // R, :], start=True, stop=True)
                    last.then_inc(fsem("cmpa", 5 * i + odd), 1)
                wait_bank(pe, "cmpa", 5 * i + 2)
                pe.wait_ge(S["cp_ready"], i + 1)
                for g in range(NKV):
                    last = tr(bank("cmpa", 5 * i + 2)[:, g * P:(g + 1) * P], Pw[:, i % 4, g * P:(g + 1) * P], ident[:, :])
                last.then_inc(fsem("cmpa", 5 * i + 2), 1)
                pe.wait_ge(S["pct_ready"], i + 1)
                pe.wait_ge(S["vcmp_ready"], 1)
                for s in range(2):
                    wait_bank(pe, "cmpa", 5 * i + 3 + s)
                    for g in (2 * s, 2 * s + 1):
                        last = mm(bank("cmpa", 5 * i + 3 + s)[:, CC * (g % 2):CC * (g % 2) + CC],
                                  PT[:, i % 4, g * P:(g + 1) * P], Vc[:, g, :], start=True, stop=True)
                    last.then_inc(fsem("cmpa", 5 * i + 3 + s), 1)
            pe.wait_ge(S["ktd_ready"], 16)
            pe.wait_ge(S["vn_ready"], 8)
            for kind, n in ATT_ORDER:
                i, h, b = ITEMS[n]
                tile = ATT[(kind, n)]
                lo, g = 64 * (h % 2), h // R
                wait_bank(pe, "att", tile)
                o = bank("att", tile)
                if kind == "s":
                    last = mm(o[:, 0:(i + 1) * P], qT[lo:lo + 64, h // 2, i * P:(i + 1) * P],
                              kTd[lo:lo + 64, b, g, 0:(i + 1) * P], start=True, stop=True)
                elif kind == "t":
                    pe.wait_ge(S["e_done"], n + 1)
                    for j in range(i + 1):
                        last = tr(o[:, j * P:(j + 1) * P], Pw[:, n % 4, j * P:(j + 1) * P], ident[:, :])
                else:
                    pe.wait_ge(S["pt_ready"], n + 1)
                    for j in range(i + 1):
                        last = mm(o[:, 0:DH], PT[:, n % 4, j * P:(j + 1) * P], vN[:, b, j, DH * g:DH * g + DH],
                                  start=(j == 0), stop=(j == i))
                last.then_inc(fsem("att", tile), 1)
            pe.wait_ge(S["o_ready"], NI)
            for j in range(KD):
                wait_bank(pe, "ot", j)
                for t in range(NT):
                    last = tr(bank("ot", j)[:, t * P:(t + 1) * P], on[:, t, j * P:(j + 1) * P], ident[:, :])
                last.then_inc(fsem("ot", j), 1)
            ada(3)
            pe.wait_ge(S["ot_ready"], KD)
            out_proj("nout", "nout")
            norm(3)
            moe(1)
            norm(4)
            for i in range(8):
                wait_bank(pe, "xo", i)
                pe.wait_ge(S["h_part"], KD * 5)
                for j in range(4):
                    last = tr(bank("xo", i)[:, j * P:(j + 1) * P], hT[:, 4 * (i % 2) + j, (i // 2) * P:(i // 2 + 1) * P], ident[:, :])
                last.then_inc(fsem("xo", i), 1)

        @block.scalar
        def _(act):
            AC = nc.scalar.activation
            cnt = [0]

            def link(ins):
                cnt[0] += 1
                ins.then_inc(S["act_chain"], 1)
                act.wait_ge(S["act_chain"], cnt[0])

            d = act.dma_start
            rows = [(0, 96, a["n_cmp_pos"][0].rearrange("j (l s) d -> (j l) (s d)", s=2)), (0, 0, a["ada_b"].rearrange("l k (j p) -> (l k j) p", p=P)),
                    (1, 0, a["c"].rearrange("o (j p) -> (o j) p", p=P)),
                    (1, 8, a["norm_g"].rearrange("l k (j p) -> (l k j) p", p=P)),
                    (1, 40, a["final_g"].rearrange("(j p) -> j p", p=P)),
                    (1, 48, a["a_conv"][0].rearrange("t (j p) -> (t j) p", p=P)),
                    (1, 80, a["n_cmp_b1"][0].rearrange("t (j p) -> (t j) p", p=P)),
                    ]
            act.wait_ge(S["const_ready"], 1)
            for s, r, ap in rows:
                d(raw[r:r + ap.shape[0], s, :], ap).then_inc(S["raw_in"], 16)
            for half in range(2):
                d(raw[84:85, 1, 64 * half:64 * half + 64], a["n_cmp_b2"][0, 0:1, :]).then_inc(S["raw_in"], 16)
                for s, key in enumerate(("s5_lam_re", "s5_lam_im")):
                    d(lrow[:, s, 64 * half:64 * half + 64], a[key][0]).then_inc(S["raw_in"], 16)
                for s in range(2):
                    key = ("s5_c_re", "s5_c_im")[(half + s) % 2]
                    d(crow[:, s, :, 64 * half:64 * half + 64],
                      a[key][0].rearrange("(t g) c p -> (g c) t p", g=8)).then_inc(S["raw_in"], 16)
            assert RAW_IN == 16 * (7 + 2 * 5)
            for half in range(2):
                for s, dst in enumerate((Ba, Bb)):
                    key = ("s5_b_re", "s5_b_im")[(half + s) % 2]
                    d(dst[64 * half:64 * half + 64], a[key][0].rearrange("g p c -> p g c")).then_inc(S["small_in"], 16)
            d(s5s[:, 0, :], a["s5_log_dt"].rearrange("o g -> (o g)").partition_broadcast(P)).then_inc(S["small_in"], 16)
            d(wif[:, :, :], a["a_w_in"][0, :, 2048:2056].rearrange("(k p) c -> p k c", p=P)).then_inc(S["small_in"], 16)
            d(d5[:, :], a["s5_d"][0].rearrange("g c -> c g"), allow_slow_non_contiguous=True).then_inc(S["small_in"], 16)
            d(vecs[0:4, 0:1], a["a_b_i"].rearrange("o h -> h o")).then_inc(S["small_in"], 16)
            d(vecs[0:4, 1:2], a["a_b_f"].rearrange("o h -> h o")).then_inc(S["small_in"], 16)
            for tau in range(TAU):
                d(glub[16 * tau:16 * tau + 16, :], a["s5_glu_b"][0].rearrange("g c -> c g"),
                  allow_slow_non_contiguous=True).then_inc(S["small_in"], 16)
            assert SMALL_IN == 16 * (4 + 5 + TAU)

            for j in range(KD):
                wait_full(act, "x", j)
                AC(xT[:, j, :], bank("x", j)[:, :], ACT.Copy).then_inc(rsem("x", j), 1)
            nc.scalar.nop().then_inc(S["x_ready"], 1)
            act.wait_ge(S["par_ready"], 1)
            AC(small[:, 0:KD], par[:, PB:PB + 8], ACT.Sigmoid).then_inc(S["act_gate"], 1)
            act.wait_ge(S["small_in"], SMALL_IN)
            AC(s5s[:, 1, :], s5s[:, 0, :], ACT.Exp).then_inc(S["act_s5"], 1)
            act.wait_ge(S["dve_s5"], 1)
            AC(ps[:, :, :], pc[:, :, :], ACT.Exp).then_inc(S["act_s5"], 1)
            act.wait_ge(S["dve_s5"], 2)
            AC(F9[:, :, :, 0], F9[:, :, :, 0], ACT.Sin).then_inc(S["act_s5"], 1)
            AC(F9[:, :, :, 1], F9[:, :, :, 1], ACT.Sin).then_inc(S["act_s5"], 1)
            act.wait_ge(S["dve_s5"], 3)
            AC(tws[:, :, :], tws[:, :, :], ACT.Sin).then_inc(S["act_s5"], 1)
            AC(twc[:, :, :], twc[:, :, :], ACT.Sin).then_inc(S["act_s5"], 1)
            for i in range(8):
                wait_full(act, "s5_e", i)
                AC(ET[:, 4 * i:4 * i + 4, :].rearrange("p a b -> p (a b)"), bank("s5_e", i)[:, :],
                   ACT.Copy).then_inc(rsem("s5_e", i), 1)
            nc.scalar.nop().then_inc(S["et_ready"], 8)

            def norm(m):
                if m:
                    act.wait_ge(S["x_upd"], KD * m)
                for k in range(KD):
                    AC(hT[:, k, :], xT[:, k, :], ACT.Square).then_inc(S["sq_ready"], 1)
                act.wait_ge(S["var_ready"], m + 1)
                AC(rstd[:, :], rstd[:, :], ACT.Sqrt).then_inc(S["sqrt_ready"], 1)
                for k in range(KD if m < 4 else 0):
                    act.wait_ge(S["h_part"], KD * m + k + 1)
                    AC(hT[:, k, :], hT[:, k, :], ACT.Identity, bias=mod[:, m, k:k + 1]).then_inc(S["h_ready"], 1)

            norm(0)
            for i in range(4):
                wait_full(act, "u", i)
                AC(Ug[:, 8 * i:8 * i + 8, :].rearrange("p a b -> p (a b)"), bank("u", i)[:, :],
                   ACT.Copy).then_inc(S["ut_ready"], 1)
                act.wait_ge(S["ut_ready"], i + 1)
                nc.scalar.nop().then_inc(rsem("u", i), 1)
            for i in range(4):
                wait_full(act, "ut", i)
                AC(Ug[:, 8 * i:8 * i + 8, :].rearrange("p a b -> p (a b)"), bank("ut", i)[:, :],
                   ACT.Copy).then_inc(rsem("ut", i), 1)
            nc.scalar.nop().then_inc(S["ug_ready"], 4)
            act.wait_ge(S["arg_ready"], 1)
            AC(grow[:, 2, :], grow[:, 2, :], ACT.Exp).then_inc(S["act_gate"], 1)
            act.wait_ge(S["act_gate"], 2)
            AC(grow[:, 2, :], grow[:, 2, :], ACT.Ln, bias=1.0).then_inc(S["act_gate"], 1)
            act.wait_ge(S["arg_ready"], 2)
            AC(grow[:, 1, :], grow[:, 1, :], ACT.Exp).then_inc(S["act_gate"], 1)

            def conv_tile(st, i, n):
                wait_full(act, st, i)
                if n >= 2:
                    act.wait_ge(S["conv_ready"], n - 1)
                AC(cpad[:, n % 2, 3:], bank(st, i)[:, :], ACT.Copy).then_inc(S["cpad_ready"], 1)
                act.wait_ge(S["cpad_ready"], n + 1)
                nc.scalar.nop().then_inc(rsem(st, i), 1)

            def conv_sig(n):
                act.wait_ge(S["conv_ready"], n + 1)
                if n:
                    act.wait_ge(S["qk_ready"], n)
                AC(ct1[:, :], qkT[:, n, :], ACT.Sigmoid).then_inc(S["sig_ready"], 1)

            for n in range(4):
                conv_tile("qk", n, n)
                conv_sig(n)
            for i in range(4):
                wait_full(act, "s5_e1", i)
                AC(ea[:, 8 * i:8 * i + 8, :].rearrange("p a b -> p (a b)"), bank("s5_e1", i)[:, :],
                   ACT.Copy).then_inc(S["ea_ready"], 1)
                act.wait_ge(S["ea_ready"], i + 1)
                nc.scalar.nop().then_inc(rsem("s5_e1", i), 1)
            for n in range(4, 8):
                conv_tile("qk2", n - 4, n)
                conv_sig(n)
            for i in range(4):
                wait_full(act, "s5_y", i)
                AC(za[:, 8 * i:8 * i + 8, :].rearrange("p a b -> p (a b)"), bank("s5_y", i)[:, :],
                   ACT.Gelu_apprx_tanh).then_inc(S["y_ready"], 1)
                act.wait_ge(S["y_ready"], i + 1)
                nc.scalar.nop().then_inc(rsem("s5_y", i), 1)
            act.wait_ge(S["st_ready"], 1)
            for n in range(8):
                wait_full(act, "v", n)
                c, t = n // 4, n % 4
                AC(Vaug[:, t, 2 * c:2 * c + 2, 0:P], bank("v", n)[:, 0:CC].rearrange("p (h d) -> p h d", h=2),
                   ACT.Copy).then_inc(S["v_ready"], 1)
                act.wait_ge(S["v_ready"], n + 1)
                nc.scalar.nop().then_inc(rsem("v", n), 1)
            for i in range(4):
                wait_full(act, "s5_glu", i)
                act.wait_ge(S["rs_ready"], i + 1)
                AC(ea[:, 8 * i:8 * i + 8, :].rearrange("p a b -> p (a b)"),
                   ea[:, 8 * i:8 * i + 8, :].rearrange("p a b -> p (a b)"), ACT.Sigmoid).then_inc(S["act_s5"], 1)
            for n in range(8):
                wait_full(act, "o", n)
                if n == 0:
                    act.wait_ge(S["et_ready"], 8)
                c, t = n // 4, n % 4
                AC(so[:, t, c * CC:(c + 1) * CC], bank("o", n)[:, 0:CC], ACT.Sigmoid).then_inc(S["so_ready"], 1)
                act.wait_ge(S["so_ready"], n + 1)
                nc.scalar.nop().then_inc(rsem("o", n), 1)
            for i in range(4):
                wait_full(act, "ml_h", i)
                AC(mixT[:, 4 + i, :].rearrange("p (k t) -> p t k", t=TAU), bank("ml_h", i)[:, :].rearrange("p (t k) -> p t k", t=TAU),
                   ACT.Copy).then_inc(S["mix_ready"], 1)
                act.wait_ge(S["mix_ready"], i + 1)
                nc.scalar.nop().then_inc(rsem("ml_h", i), 1)
            for h in range(MH):
                act.wait_ge(S["arg_ready"], 2 + h + 1)
                AC(Wb[h % 2].rearrange("p a b -> p (a b)"), Wb[h % 2].rearrange("p a b -> p (a b)"),
                   ACT.Exp).then_inc(S["dexp_ready"], 1)
            act.wait_ge(S["diag_ready"], 1)
            AC(small[:, 64:80], small[:, 64:80], ACT.Sqrt).then_inc(S["act_gate"], 1)
            for h in range(MH):
                wait_full(act, "ml_t", h)
                AC(mixT[:, h, :], bank("ml_t", h)[:, :], ACT.Copy).then_inc(S["mixh_ready"], 1)
                act.wait_ge(S["mixh_ready"], h + 1)
                nc.scalar.nop().then_inc(rsem("ml_t", h), 1)

            def evict(st, i, dst, ready, src=None, func=ACT.Copy, **kw):
                wait_full(act, st, i)
                AC(dst, bank(st, i)[:, :] if src is None else src, func, **kw).then_inc(rsem(st, i), 1)
                n = BASE[st] + i
                act.wait_ge(free[n % 8], n // 8 + 1)
                nc.scalar.nop().then_inc(ready, 1)

            def moe(l):
                act.wait_ge(S["route_e"], l + 1)
                AC(rt[:, 80:160], rt[:, 80:160], ACT.Exp).then_inc(S["route_s"], 1)
                for e in range(NE):
                    for f in range(2):
                        n = 2 * (NE * l + e) + f
                        wait_full(act, f"moe{l}", EM * e + 1 + f)
                        if n >= 2:
                            act.wait_ge(S["hid_ready"], n - 1)
                        AC(sg[:, f, :], bank(f"moe{l}", EM * e + 1 + f)[:, :], ACT.Sigmoid).then_inc(S["esig"], 1)

            norm(1)
            moe(0)
            norm(2)
            for i in range(8):
                wait_full(act, "nq", i)
                AC(qT[:, i, :], bank("nq", i)[:, :], ACT.Copy, scale=DH ** -0.5).then_inc(S["q_ready"], 1)
                act.wait_ge(S["q_ready"], i + 1)
                nc.scalar.nop().then_inc(rsem("nq", i), 1)
            for j in range(2):
                for half in range(2):
                    i = 2 * j + half
                    wait_full(act, "nkc", i)
                    for gg in range(2):
                        g = 2 * half + gg
                        src = bank("nkc", i)[64 * gg:64 * gg + 64, :]
                        AC(kc2[0:64, j, g, 0:T], src, ACT.Copy).then_inc(S["kc_ready"], 1)
                        AC(kc2[64:128, j, g, 0:T - 1], src[:, 1:T], ACT.Copy).then_inc(S["kc_ready"], 1)
                    act.wait_ge(S["kc_ready"], 4 * i + 4)
                    nc.scalar.nop().then_inc(rsem("nkc", i), 1)
            for b, (st_k, st_v) in enumerate((("nks", "nvs"), ("nkw", "nvw"))):
                for i in range(2):
                    wait_full(act, st_k, i)
                    for gg in range(2):
                        src = bank(st_k, i)[64 * gg:64 * gg + 64, :]
                        for lo in (0, 64):
                            AC(kTd[lo:lo + 64, b, 2 * i + gg, :], src, ACT.Copy).then_inc(S["ktd_ready"], 1)
                    act.wait_ge(S["ktd_ready"], 8 * b + 4 * i + 4)
                    nc.scalar.nop().then_inc(rsem(st_k, i), 1)
                for t in range(NT):
                    wait_full(act, st_v, t)
                    AC(vN[:, b, t, :], bank(st_v, t)[:, 0:CC], ACT.Copy).then_inc(S["vn_ready"], 1)
                    act.wait_ge(S["vn_ready"], 4 * b + t + 1)
                    nc.scalar.nop().then_inc(rsem(st_v, t), 1)
            act.wait_ge(S["ng_ready"], 1)
            AC(gts.rearrange("p a b -> p (a b)"), gts.rearrange("p a b -> p (a b)"), ACT.Sigmoid).then_inc(S["gsig"], 1)
            for j in range(2):
                act.wait_ge(S["cb_ready"], j + 1)
                for f in range(2):
                    wait_full(act, "chid", 2 * j + f)
                    if j == 0 and f == 0:
                        act.wait_ge(S["cpre"], 1)
                    AC(chid[:, j, f, :, 0:NCMP], bank("chid", 2 * j + f)[:, 0:NKV * NCMP].rearrange("p (g n) -> p g n", g=NKV),
                       ACT.Gelu_apprx_tanh, bias=cb[:, j, f:f + 1]).then_inc(S["chid_ready"], 1)
                    act.wait_ge(S["chid_ready"], 2 * j + f + 1)
                    nc.scalar.nop().then_inc(rsem("chid", 2 * j + f), 1)
            act.wait_ge(S["f_out"], 16)
            for i in range(NT):
                act.wait_ge(S["cs_ready"], i + 1)
                AC(Pw[:, i % 4, :], Pw[:, i % 4, :], ACT.Exp).then_inc(S["ce_ready"], 1)
                wait_full(act, "cmpa", 5 * i + 2)
                AC(PT[:, i % 4, :], bank("cmpa", 5 * i + 2)[:, :], ACT.Copy).then_inc(S["pct_ready"], 1)
                act.wait_ge(S["pct_ready"], i + 1)
                nc.scalar.nop().then_inc(rsem("cmpa", 5 * i + 2), 1)
            for n in range(NI + 2):
                if n < NI:
                    w = (ITEMS[n][0] + 1) * P
                    act.wait_ge(S["p_ready"], n + 1)
                    AC(Pw[:, n % 4, 0:w], Pw[:, n % 4, 0:w], ACT.Exp, bias=stat[:, n % 8:n % 8 + 1],
                       accum_out=stat[:, 8 + n % 8:9 + n % 8]).then_inc(S["e_done"], 1)
                if n >= 2:
                    m = n - 2
                    w = (ITEMS[m][0] + 1) * P
                    tile = ATT[("t", m)]
                    wait_full(act, "att", tile)
                    if m >= 4:
                        wait_full(act, "att", ATT[("o", m - 4)])
                    AC(PT[:, m % 4, 0:w], bank("att", tile)[:, 0:w], ACT.Copy).then_inc(S["pt_ready"], 1)
                    act.wait_ge(S["pt_ready"], m + 1)
                    nc.scalar.nop().then_inc(rsem("att", tile), 1)
            for j in range(KD):
                wait_full(act, "ot", j)
                AC(mixT[:, j, :], bank("ot", j)[:, :], ACT.Copy).then_inc(S["ot_ready"], 1)
                act.wait_ge(S["ot_ready"], j + 1)
                nc.scalar.nop().then_inc(rsem("ot", j), 1)
            norm(3)
            moe(1)
            norm(4)
            for i in range(8):
                wait_full(act, "xo", i)
                AC(osb[:, i // 2, (i % 2) * T:(i % 2 + 1) * T], bank("xo", i)[:, :], ACT.Copy).then_inc(S["out_ready"], 1)

        @block.vector
        def _(dve):
            V = nc.vector
            cnt = [0]

            def link(ins):
                cnt[0] += 1
                ins.then_inc(S["dve_chain"], 1)
                dve.wait_ge(S["dve_chain"], cnt[0])

            def signal(s, n=1):
                V.nop().then_inc(s, n)

            wait_full(dve, "param")
            link(V.tensor_copy(par[:, :], bank("param")[:, 0:224]))
            lre, lim = s5s[:, 2, :], s5s[:, 3, :]
            link(V.tensor_copy(s5s[:, 2:4, :].rearrange("p a b -> p (a b)"), bank("param")[:, 224:288]))
            V.nop().then_inc(rsem("param"), 1)
            signal(S["par_ready"])
            wait_full(dve, "ct", 0)
            dve.wait_ge(S["const_ready"], 1)
            link(V.tensor_scalar(Ca.rearrange("p a b -> p (a b)"), bank("ct", 0)[:, :], sgn[:, 0:1], None, ALU.mult))
            signal(rsem("ct", 0))
            wait_full(dve, "ct", 1)
            link(V.tensor_scalar(Cb.rearrange("p a b -> p (a b)"), bank("ct", 1)[:, :], -1.0, None, ALU.mult))
            signal(rsem("ct", 1))
            dve.wait_ge(S["act_gate"], 1)
            link(V.tensor_tensor(sil[:, :], small[:, 0:KD], par[:, PB:PB + 8], ALU.mult))
            signal(S["sil_ready"])
            dve.wait_ge(S["small_in"], SMALL_IN)
            link(V.tensor_scalar(Bb[0:64].rearrange("p a b -> p (a b)"), Bb[0:64].rearrange("p a b -> p (a b)"), -1.0, None, ALU.mult))
            dve.wait_ge(S["act_s5"], 1)
            are, ang = s5s[:, 4, :], s5s[:, 5, :]
            link(V.tensor_tensor(are, lre, s5s[:, 1, :], ALU.mult))
            link(V.tensor_tensor(ang, lim, s5s[:, 1, :], ALU.mult))

            def outer(o, x, n):
                link(V.tensor_tensor(o, dims(x, [1, G5], [0, n]), dims(jj[:, :], [0, G5], [1, n]), ALU.mult))

            def reduce_angle(x, t, c):
                link(V.tensor_scalar(t, x, 1.0 / (2 * PI), MAGIC, ALU.mult, ALU.add))
                link(V.tensor_scalar(t, t, MAGIC, None, ALU.subtract))
                for part in (C1, C2, C3):
                    link(V.tensor_scalar(c, t, -part, None, ALU.mult))
                    link(V.tensor_tensor(x, x, c, ALU.add))
                link(V.tensor_scalar(x, x, 3.1415925, -3.1415925, ALU.min, ALU.max))
                link(V.tensor_scalar(c, x, -1.0, None, ALU.mult))
                link(V.tensor_tensor(c, x, c, ALU.max))
                link(V.tensor_scalar(c, c, -1.0, PI / 2, ALU.mult, ALU.add))

            outer(pc[:, :, :], are, NPW)
            signal(S["dve_s5"])
            sx, cx = F9[:, :, :, 0], F9[:, :, :, 1]
            outer(sx, ang, NPW)
            reduce_angle(sx, pt[:, :, :], cx)
            signal(S["dve_s5"])
            dve.wait_ge(S["act_s5"], 4)
            link(V.tensor_copy(r8[:, :], ps[:, :, TAU]))
            link(V.tensor_tensor(pc[:, :, :], ps[:, :, :], cx, ALU.mult))
            link(V.tensor_tensor(ps[:, :, :], ps[:, :, :], sx, ALU.mult))
            nr, t1, t2, kr, ki, iv = (s5s[:, i, :] for i in range(6, 12))
            link(V.tensor_scalar(nr, pc[:, :, 1], -1.0, None, ALU.add))
            ni = s5s[:, 12, :]
            link(V.tensor_copy(ni, ps[:, :, 1]))
            link(V.tensor_tensor(t1, lre, lre, ALU.mult))
            link(V.tensor_tensor(t2, lim, lim, ALU.mult))
            link(V.tensor_tensor(t1, t1, t2, ALU.add))
            link(V.reciprocal(iv, t1))
            link(V.tensor_tensor(t1, nr, lre, ALU.mult))
            link(V.tensor_tensor(t2, ni, lim, ALU.mult))
            link(V.tensor_tensor(t1, t1, t2, ALU.add))
            link(V.tensor_tensor(kr, t1, iv, ALU.mult))
            link(V.tensor_tensor(t1, ni, lre, ALU.mult))
            link(V.tensor_tensor(t2, nr, lim, ALU.mult))
            link(V.tensor_tensor(t1, t1, t2, ALU.subtract))
            link(V.tensor_tensor(ki, t1, iv, ALU.mult))
            krb, kib = dims(kr, [1, G5], [0, S5C]), dims(ki, [1, G5], [0, S5C])
            tmp = Ea[:, :, 0, :]
            link(V.tensor_tensor(Bba, Ba, krb, ALU.mult))
            link(V.tensor_tensor(tmp, Bb, kib, ALU.mult))
            link(V.tensor_tensor(Bba, Bba, tmp, ALU.add))
            link(V.tensor_tensor(Bbb, Bb, krb, ALU.mult))
            link(V.tensor_tensor(tmp, Ba, kib, ALU.mult))
            link(V.tensor_tensor(Bbb, Bbb, tmp, ALU.subtract))
            pcr = dims(pc[:, 0, :], [NPW, G5], [-1, TAU], [0, S5C], off=TAU - 1)
            psr = dims(ps[:, 0, :], [NPW, G5], [-1, TAU], [0, S5C], off=TAU - 1)
            bA = dims(Bba[:, 0, :], [S5C, G5], [0, TAU], [1, S5C])
            bB = dims(Bbb[:, 0, :], [S5C, G5], [0, TAU], [1, S5C])
            t4 = Mt.rearrange("p g (t c) -> p g t c", t=TAU)
            link(V.tensor_tensor(Ea, pcr, bA, ALU.mult))
            link(V.tensor_tensor(t4, psr, bB, ALU.mult))
            link(V.tensor_tensor(Ea, Ea, t4, ALU.add))
            signal(S["e_ready"])
            cA = dims(Ca[:, 0, :], [S5C, G5], [0, NPW], [1, S5C])
            cB = dims(Cb[:, 0, :], [S5C, G5], [0, NPW], [1, S5C])
            pcf = dims(pc[:, 0, :], [NPW, G5], [1, NPW], [0, S5C])
            psf = dims(ps[:, 0, :], [NPW, G5], [1, NPW], [0, S5C])
            tf = region(12800, [G5, NPW, S5C])
            link(V.tensor_tensor(F9, pcf, cA, ALU.mult))
            link(V.tensor_tensor(tf, psf, cB, ALU.mult))
            link(V.tensor_tensor(F9, F9, tf, ALU.add))
            signal(S["pow_ready"])
            link(V.tensor_scalar(ang, ang, float(TAU), None, ALU.mult))
            outer(tws, ang, NCH)
            reduce_angle(tws, za, twc)
            signal(S["dve_s5"])
            def ada_out(m):
                wait_full(dve, f"ada{m}")
                link(V.tensor_tensor(mod[:, m, :], bank(f"ada{m}")[:, 0:24], par[:, 24 * m:24 * m + 24], ALU.add))
                signal(rsem(f"ada{m}"))

            ada_out(0)
            link(V.memset(Mt, 0.0))
            for i in range(8):
                wait_full(dve, "s5_g", i)
                link(V.tensor_copy(Gk[:, 4 * i:4 * i + 4, :].rearrange("p a b -> p (a b)"), bank("s5_g", i)[0:16, :]))
                signal(rsem("s5_g", i))
            dd = ct1[0:16, :].rearrange("p (g c) -> p g c", g=G5)
            link(V.tensor_tensor(dd, dims(ident[0:16, :], [0, G5], [1, S5C]), dims(d5[:, :], [1, G5], [0, S5C]), ALU.mult))
            link(V.tensor_tensor(Gk[:, :, 0:S5C], Gk[:, :, 0:S5C], dd, ALU.add))
            signal(S["g_ready"])

            def norm(m):
                if m == 4:
                    link(V.tensor_copy(amul[:, :], par[:, PB + 40:PB + 48]))
                else:
                    link(V.scalar_tensor_tensor(out=amul[:, :], in0=mod[:, m, 8:16], scalar=1.0,
                                                in1=par[:, PB + 8 + 8 * m:PB + 16 + 8 * m], op0=ALU.add, op1=ALU.mult))
                st = f"norm{m}"
                wait_full(dve, st)
                link(V.tensor_scalar(rstd[:, :], bank(st)[:, :], 1.0 / D, EPS, ALU.mult, ALU.add))
                signal(rsem(st))
                signal(S["var_ready"])
                dve.wait_ge(S["sqrt_ready"], m + 1)
                link(V.reciprocal(rstd[:, :], rstd[:, :]))
                for k in range(KD):
                    V.scalar_tensor_tensor(out=hT[:, k, :], in0=xT[:, k, :], scalar=amul[:, k:k + 1],
                                           in1=rstd[:, :], op0=ALU.mult, op1=ALU.mult).then_inc(S["h_part"], 1)

            dve.wait_ge(S["x_ready"], 1)
            norm(0)
            dve.wait_ge(S["m_in"], 16 * TAU)
            for n in range(8):
                wait_full(dve, "u2", n)
                g0, q = 8 * (n // 2), 4 * (n % 2)
                link(V.tensor_copy(uk[0:NCH, g0:g0 + 8, q:q + 4, :],
                                   bank("u2", n)[0:NCH, :].rearrange("p (t g c) -> p g t c", t=4, c=S5C)))
                signal(rsem("u2", n))
                signal(S["uk_ready"])
            wait_full(dve, "gates", 0)
            li, lf, sc = (grow[:, i, :] for i in range(3))
            A, E5, nM = li, lf, rstd[0:MH, :]
            link(V.tensor_scalar(li, bank("gates", 0)[0:4, :], vecs[0:4, 0:1], None, ALU.add))
            signal(rsem("gates", 0))
            wait_full(dve, "gates", 1)
            link(V.tensor_scalar(lf, bank("gates", 1)[0:4, :], vecs[0:4, 1:2], None, ALU.add))
            signal(rsem("gates", 1))
            link(V.tensor_scalar(sc, lf, -1.0, None, ALU.mult))
            link(V.tensor_tensor(sc, lf, sc, ALU.min))
            signal(S["arg_ready"])
            dve.wait_ge(S["act_gate"], 3)
            link(V.scalar_tensor_tensor(out=lf, in0=lf, scalar=0.0, in1=sc, op0=ALU.min, op1=ALU.subtract))
            link(V.memset(nM, 1.0))
            link(V.tensor_tensor_scan(sc, nM, lf, 0.0, ALU.mult, ALU.add))
            link(V.tensor_tensor(A, li, sc, ALU.subtract))
            link(V.tensor_tensor_scan(lf, A, A, 0.0, ALU.max, ALU.max))
            link(V.tensor_scalar(nM, lf, -1.0, None, ALU.mult))
            link(V.tensor_tensor(E5, nM, sc, ALU.subtract))
            signal(S["arg_ready"])
            dve.wait_ge(S["act_gate"], 4)
            signal(S["gates_ready"])

            def conv(n):
                dve.wait_ge(S["cpad_ready"], n + 1)
                w = lambda t: par[:, PB + 48 + 8 * t + n:PB + 49 + 8 * t + n]
                o = qkT[:, n, :]
                link(V.tensor_scalar(o, cpad[:, n % 2, 0:T], w(0), None, ALU.mult))
                for t in range(1, 4):
                    i = V.scalar_tensor_tensor(out=o, in0=cpad[:, n % 2, t:t + T], scalar=w(t), in1=o, op0=ALU.mult, op1=ALU.add)
                    link(i)
                signal(S["conv_ready"])
                dve.wait_ge(S["sig_ready"], n + 1)
                link(V.tensor_tensor(o, o, ct1[:, :], ALU.mult))
                signal(S["qk_ready"])

            for n in range(4):
                conv(n)
            f2 = lambda t: t.rearrange("p a b -> p (a b)")
            dve.wait_ge(S["act_s5"], 6)
            for i in range(4):
                wait_full(dve, "s5_eb", i)
                sl = slice(8 * i, 8 * i + 8)
                link(V.tensor_tensor(f2(za[:, sl]), bank("s5_eb", i)[:, :], f2(tws[:, sl]), ALU.mult))
                signal(rsem("s5_eb", i))
                link(V.tensor_tensor(f2(ea[:, sl]), f2(ea[:, sl]), f2(twc[:, sl]), ALU.mult))
                link(V.tensor_tensor(f2(ea[:, sl]), f2(ea[:, sl]), f2(za[:, sl]), ALU.add))
            decay = Ug2 = region(4096, [G5, NCH])
            link(V.tensor_copy(decay, dims(r8[:, :], [1, G5], [0, NCH])))
            link(V.memset(decay[:, :, 0:1], 0.0))
            link(V.tensor_tensor_scan(f2(za), f2(decay), f2(ea), 0.0, ALU.mult, ALU.add))
            signal(S["za_ready"])
            for n in range(4, 8):
                conv(n)
            for i in range(4):
                wait_full(dve, "s5_zb", i)
                sl = slice(8 * i, 8 * i + 8)
                link(V.tensor_tensor(f2(ea[:, sl]), bank("s5_zb", i)[:, :], f2(tws[:, sl]), ALU.mult))
                signal(rsem("s5_zb", i))
                link(V.tensor_tensor(f2(za[:, sl]), f2(za[:, sl]), f2(twc[:, sl]), ALU.mult))
                link(V.tensor_tensor(f2(ea[:, sl]), f2(za[:, sl]), f2(ea[:, sl]), ALU.subtract))
                signal(S["xs_ready"])
            link(V.memset(Vaug[:, :, :, P:P + 1].rearrange("p a b c -> p (a b c)"), 1.0))
            signal(S["st_ready"])
            for i in range(4):
                wait_full(dve, "s5_glu", i)
                for g in range(8 * i, 8 * i + 8):
                    V.tensor_scalar(ea[:, g, :], bank("s5_glu", i)[:, (g % 8) * NCH:(g % 8 + 1) * NCH],
                                    glub[:, g:g + 1], None, ALU.add).then_inc(S["dve_s5"], 1)
                dve.wait_ge(S["dve_s5"], 3 + 8 * i + 8)
                signal(rsem("s5_glu", i))
                signal(S["rs_ready"])
                dve.wait_ge(S["act_s5"], 6 + i + 1)
                sl = slice(8 * i, 8 * i + 8)
                link(V.tensor_tensor(f2(Ug[:, sl]), f2(za[:, sl]), f2(ea[:, sl]), ALU.mult))
                signal(S["ys_ready"])
            for i in range(8):
                st, ii = ("s5_k", i) if i < 4 else ("s5_t", i - 4)
                wait_full(dve, st, ii)
                link(V.tensor_copy(uk2[:, :, 64 * i:64 * i + 64].rearrange("p t (g c) -> p g t c", c=S5C),
                                   bank(st, ii)[0:NCH, :].rearrange("p (g t c) -> p g t c", t=TAU, c=S5C)))
                signal(rsem(st, ii))
                signal(S["sk_ready"])
            wait_full(dve, "gcol")
            link(V.tensor_copy(gcol[:, :, :, :].rearrange("p a b c -> p (a b c)"), bank("gcol")[:, 0:32]))
            signal(rsem("gcol"))
            n = 4
            ssq = small[:, 64:80]
            for h in range(MH):
                wait_full(dve, "ml_h", n)
                if h == 0:
                    wait_full(dve, "ml_h", 3)
                W = Wb[h % 2]
                if h >= 2:
                    wait_full(dve, "ml_h", 4 + 7 * (h - 2) + 6)
                link(V.memset(W, 0.0)) if h < 2 else None
                for j in range(NT):
                    link(V.tensor_scalar(W[:, j, j * P:], bank("ml_h", n)[:, j * P:], gcol[:, 0, j, h:h + 1], 0.0,
                                         ALU.add, ALU.min))
                signal(rsem("ml_h", n))
                signal(S["arg_ready"])
                n += 1
                dve.wait_ge(S["dexp_ready"], h + 1)
                for j in range(NT):
                    wait_full(dve, "ml_h", n)
                    dg = W[:, j, j * P:(j + 1) * P]
                    link(V.tensor_tensor(dg, dg, cmask[:, :], ALU.mult))
                    link(V.scalar_tensor_tensor(out=W[:, j, j * P:], in0=bank("ml_h", n)[:, j * P:], scalar=P ** -0.5,
                                                in1=W[:, j, j * P:], op0=ALU.mult, op1=ALU.mult))
                    signal(rsem("ml_h", n))
                    n += 1
                signal(S["w_ready"])
                for i in range(0, NT, 2):
                    wait_full(dve, "ml_h", n)
                    for ii in range(i, i + 2):
                        b = bank("ml_h", n)[:, (ii - i) * 129:(ii - i + 1) * 129]
                        dn = small[:, 80:81]
                        link(V.tensor_scalar(dn, b[:, P:P + 1], -1.0, None, ALU.mult))
                        link(V.tensor_tensor(dn, dn, b[:, P:P + 1], ALU.max))
                        link(V.tensor_tensor(dn, dn, gcol[:, 1, ii, h:h + 1], ALU.max))
                        link(V.reciprocal(dn, dn))
                        link(V.tensor_scalar(hmx[:, ii, h, :], b[:, 0:P], dn, None, ALU.mult))
                        link(V.scalar_tensor_tensor(out=ct1[:, 0:P], in0=hmx[:, ii, h, :], scalar=1.0,
                                                    in1=hmx[:, ii, h, :], op0=ALU.mult, op1=ALU.mult,
                                                    accum_out=ssq[:, 4 * ii + h:4 * ii + h + 1]))
                    signal(rsem("ml_h", n))
                    n += 1
            link(V.tensor_scalar(ssq, ssq, 1.0 / P, EPS, ALU.mult, ALU.add))
            signal(S["diag_ready"])
            dve.wait_ge(S["act_gate"], 5)
            link(V.reciprocal(ssq, ssq))
            dve.wait_ge(S["headg_in"], 16)
            hf = hmx.rearrange("p a b c -> p (a b) c")
            link(V.tensor_tensor(hf, hf, dims(ssq, [1, 16], [0, P]), ALU.mult))
            link(V.tensor_tensor(hmx.rearrange("p a b c -> p a (b c)"), hmx.rearrange("p a b c -> p a (b c)"),
                                 dims(headg[:, :], [0, NT], [1, MA]), ALU.mult))
            dve.wait_ge(S["so_ready"], 8)
            link(V.tensor_tensor(hmx.rearrange("p a b c -> p (a b c)"), hmx.rearrange("p a b c -> p (a b c)"),
                                 so.rearrange("p a b -> p (a b)"), ALU.mult))
            signal(S["hm_ready"])
            ada_out(1)

            def residual(stage, m):
                for j in range(KD):
                    wait_full(dve, stage, j)
                    link(V.scalar_tensor_tensor(out=xT[:, j, :], in0=bank(stage, j)[:, :], scalar=mod[:, m, 16 + j:17 + j],
                                                in1=xT[:, j, :], op0=ALU.mult, op1=ALU.add))
                    signal(rsem(stage, j))
                    signal(S["x_upd"])

            residual("aout", 0)

            def moe(l):
                wait_full(dve, f"route{l}")
                dve.wait_ge(S["wr_in"], 16 * 6)
                lg = rt[:, 0:80].rearrange("p (t e) -> p t e", t=NT)
                ex = rt[:, 80:160].rearrange("p (t e) -> p t e", t=NT)
                link(V.tensor_tensor(lg, bank(f"route{l}")[:, 0:80].rearrange("p (t e) -> p t e", t=NT),
                                     dims(rb[:, l, :], [0, NT], [1, 20]), ALU.add))
                signal(rsem(f"route{l}"))
                gl, el = lg[:, :, 0:NG], lg[:, :, NG:]
                m1 = rt[:, 160:164]
                b4 = lambda x: dims(x, [1, NT], [0, NG])
                b16 = lambda x: dims(x, [1, NT], [0, NE])
                ix = lambda n: dims(jj[:, 0:1], [0, NT], [1, n])
                gate = rt[:, 192:256].rearrange("p (t e) -> p t e", t=NT)
                o1 = rt[:, 256:320].rearrange("p (t e) -> p t e", t=NT)
                o2 = rt[:, 320:384].rearrange("p (t e) -> p t e", t=NT)
                og = rt[:, 384:400].rearrange("p (t e) -> p t e", t=NT)
                ms = rt[:, 400:464].rearrange("p (t e) -> p t e", t=NT)
                mg, v1, v2, wa, wb, pg = (rt[:, 164 + 4 * i:168 + 4 * i] for i in range(6))

                def first_max(o, x, mx, n):
                    bx = dims(mx, [1, NT], [0, n])
                    link(V.tensor_reduce(mx, x, AX.X, ALU.max))
                    link(V.tensor_tensor(o, x, bx, ALU.is_equal))
                    link(V.scalar_tensor_tensor(out=gate[:, :, 0:n], in0=ix(n), scalar=-64.0, in1=o, op0=ALU.add, op1=ALU.mult))
                    link(V.tensor_reduce(m1, gate[:, :, 0:n], AX.X, ALU.min))
                    link(V.tensor_scalar(gate[:, :, 0:n], ix(n), -64.0, None, ALU.add))
                    link(V.tensor_tensor(o, gate[:, :, 0:n], dims(m1, [1, NT], [0, n]), ALU.is_equal))

                first_max(og, gl, mg, NG)
                link(V.tensor_tensor(ex[:, :, 0:NG], gl, b4(mg), ALU.subtract))
                link(V.memset(ex[:, :, NG:], 0.0))
                og16 = dims(og[:, 0, :], [NG, NT], [1, NG], [0, NPG])
                four = lambda x: x.rearrange("p t (g e) -> p t g e", g=NG)
                link(V.tensor_copy(four(o2), og16))
                link(V.tensor_tensor(ms, el, o2, ALU.mult))
                link(V.tensor_scalar(o2, o2, -1.0, 1e30, ALU.add, ALU.mult))
                link(V.tensor_tensor(ms, ms, o2, ALU.add))
                first_max(o1, ms, v1, NE)
                link(V.scalar_tensor_tensor(out=ms, in0=o1, scalar=-2e30, in1=ms, op0=ALU.mult, op1=ALU.add))
                first_max(o2, ms, v2, NE)
                link(V.tensor_tensor(dims(ex[:, 0, :], [20, NT], off=NG), v2, v1, ALU.subtract))
                signal(S["route_e"])
                dve.wait_ge(S["route_s"], l + 1)
                link(V.tensor_reduce(pg, ex[:, :, 0:NG], AX.X, ALU.add))
                e2 = dims(ex[:, 0, :], [20, NT], off=NG)
                link(V.tensor_scalar(wa, e2, 1.0, None, ALU.add))
                link(V.tensor_tensor(wa, wa, pg, ALU.mult))
                link(V.reciprocal(wa, wa))
                link(V.tensor_tensor(wb, wa, e2, ALU.mult))
                link(V.tensor_tensor(o1, o1, b16(wa), ALU.mult))
                link(V.tensor_tensor(o2, o2, b16(wb), ALU.mult))
                link(V.tensor_tensor(gate, o1, o2, ALU.add))
                signal(S["gate_t"])
                wait_full(dve, f"gt{l}")
                link(V.tensor_copy(gT[:, :], bank(f"gt{l}")[0:NE, :]))
                signal(rsem(f"gt{l}"))
                signal(S["gate_t"])
                stg = f"moe{l}"
                for e in range(NE):
                    i = EM * e
                    for f in range(2):
                        n = 2 * (NE * l + e) + f
                        dve.wait_ge(S["esig"], n + 1)
                        h = hid[:, e % 2, f, :]
                        link(V.tensor_tensor(h, bank(stg, i + 1 + f)[:, :], sg[:, f, :], ALU.mult))
                        signal(rsem(stg, i + 1 + f))
                        if f == 0:
                            wait_full(dve, stg, i)
                        link(V.tensor_tensor(h, bank(stg, i)[:, :], h, ALU.mult))
                        if f == 1:
                            signal(rsem(stg, i))
                        wait_full(dve, stg, i + 3 + f)
                        link(V.tensor_tensor(h, bank(stg, i + 3 + f)[:, :], h, ALU.mult))
                        signal(rsem(stg, i + 3 + f))
                        signal(S["hid_ready"])
                    for j in range(KD):
                        wait_full(dve, stg, i + 5 + j)
                        b = bank(stg, i + 5 + j)[:, :]
                        if e == 0:
                            link(V.tensor_copy(acc[:, j, :], b))
                        else:
                            link(V.tensor_tensor(acc[:, j, :], acc[:, j, :], b, ALU.add))
                        signal(rsem(stg, i + 5 + j))
                m = 2 * l + 1
                for j in range(KD):
                    link(V.scalar_tensor_tensor(out=xT[:, j, :], in0=acc[:, j, :], scalar=mod[:, m, 16 + j:17 + j],
                                                in1=xT[:, j, :], op0=ALU.mult, op1=ALU.add))
                    signal(S["x_upd"])

            norm(1)
            moe(0)
            ada_out(2)
            norm(2)
            link(V.memset(chid.rearrange("p a b c d -> p (a b c d)"), 0.0))
            signal(S["cpre"])
            link(V.memset(Vc.rearrange("p a b -> p (a b)"), 0.0))
            link(V.memset(biasC.rearrange("p a b c -> p (a b c)"), NEG))
            wait_full(dve, "ngate")
            dve.wait_ge(S["nsa_in"], NSA_IN)
            link(V.tensor_tensor(gts, bank("ngate")[:, 0:192].rearrange("p (t e) -> p t e", t=NT),
                                 dims(bng[:, :], [0, NT], [1, 48]), ALU.add))
            signal(rsem("ngate"))
            signal(S["ng_ready"])
            for i in range(2):
                wait_full(dve, "fvec", i)
                link(V.tensor_copy(frs[:, T * (1 - i):T * (1 - i) + T], dims(bank("fvec", i)[0:NH, :], [-1, T], off=T - 1)))
                signal(rsem("fvec", i))
            signal(S["f_ready"])
            for i in range(NT):
                wait_full(dve, "biasc", i)
                link(V.tensor_copy(biasC[:, i, :, 0:NCMP], bank("biasc", i)[:, 0:NH * NCMP].rearrange("p (n h) -> p h n", h=NH)))
                signal(rsem("biasc", i))
            for j in range(2):
                for f in range(2):
                    wait_full(dve, "cpos", 2 * j + f)
                    if f:
                        dve.wait_ge(S["cw_used"], 2 * j + 2)
                    link(V.tensor_tensor(cb[:, j, f:f + 1], bank("cpos", 2 * j + f)[:, 0:1],
                                         par[:, PB + 80 + 2 * j + f:PB + 81 + 2 * j + f], ALU.add))
                    signal(rsem("cpos", 2 * j + f))
                signal(S["cb_ready"])
            wait_full(dve, "kcmp")
            link(V.tensor_scalar(kcT.rearrange("p a b -> p (a b)"), bank("kcmp")[:, 0:P], par[:, PB + 84:PB + 85], None, ALU.add))
            signal(rsem("kcmp"))
            signal(S["kcmp_ready"])
            wait_full(dve, "vcmp")
            for r in range(R):
                sl = slice(32 * r, 32 * r + 32)
                link(V.tensor_tensor(Vc[sl, :, DH * r:DH * r + DH], bank("vcmp")[sl, 0:CC].rearrange("p (g d) -> p g d", g=NKV),
                                     dims(b2v[sl, :], [0, NKV], [1, DH]), ALU.add))
            signal(rsem("vcmp"))
            signal(S["vcmp_ready"])
            dve.wait_ge(S["gsig"], 1)
            for i in range(NT):
                p = Pw[:, i % 4, :]
                p3 = p.rearrange("p (h n) -> p h n", h=NH)
                mx, sm = stat[:, 16:32], stat[:, 32:48]
                for odd in range(2):
                    wait_full(dve, "cmpa", 5 * i + odd)
                    link(V.tensor_tensor(p3.rearrange("p (a two) n -> p two a n", two=2)[:, odd],
                                         bank("cmpa", 5 * i + odd)[:, 0:256].rearrange("p (a n) -> p a n", n=32),
                                         biasC[:, i, :, :].rearrange("p (a two) n -> p two a n", two=2)[:, odd], ALU.add))
                    signal(rsem("cmpa", 5 * i + odd))
                link(V.tensor_reduce(mx, p3, AX.X, ALU.max))
                link(V.tensor_tensor(p3, p3, dims(mx, [1, NH], [0, 32]), ALU.subtract))
                signal(S["cs_ready"])
                dve.wait_ge(S["ce_ready"], i + 1)
                link(V.tensor_reduce(sm, p3, AX.X, ALU.add))
                link(V.reciprocal(sm, sm))
                link(V.tensor_tensor(sm, sm, dims(gts[:, i, :], [3, NH]), ALU.mult))
                if i == 0:
                    link(V.memset(sm[0:CL - 1, :], 0.0))
                link(V.tensor_tensor(p3, p3, dims(sm, [1, NH], [0, 32]), ALU.mult))
                signal(S["cp_ready"])
                for s in range(2):
                    wait_full(dve, "cmpa", 5 * i + 3 + s)
                    link(V.tensor_copy(on[:, i, T * s:T * s + T], bank("cmpa", 5 * i + 3 + s)[:, :]))
                    signal(rsem("cmpa", 5 * i + 3 + s))
            dve.wait_ge(S["bias_in"], 16 * P // REP)
            for n in range(NI + 3):
                if n < NI:
                    i, h, b = ITEMS[n]
                    w = (i + 1) * P
                    tile = ATT[("s", n)]
                    wait_full(dve, "att", tile)
                    if n >= 4:
                        wait_full(dve, "att", ATT[("t", n - 4)])
                    link(V.tensor_tensor_reduce(Pw[:, n % 4, 0:w], bank("att", tile)[:, 0:w], biasT[:, h, T - w:T], 1.0, NEG * 10,
                                                ALU.add, ALU.max, stat[:, 48:49]))
                    signal(rsem("att", tile))
                    link(V.tensor_scalar(stat[:, n % 8:n % 8 + 1], stat[:, 48:49], -1.0, None, ALU.mult))
                    signal(S["p_ready"])
                if n >= 3:
                    m = n - 3
                    i, h, b = ITEMS[m]
                    tile = ATT[("o", m)]
                    sc = stat[:, 50:51]
                    dve.wait_ge(S["e_done"], m + 1)
                    link(V.reciprocal(sc, stat[:, 8 + m % 8:9 + m % 8]))
                    link(V.tensor_tensor(sc, sc, gts[:, i, 3 * h + 1 + b:3 * h + 2 + b], ALU.mult))
                    wait_full(dve, "att", tile)
                    o = on[:, i, DH * h:DH * h + DH]
                    link(V.scalar_tensor_tensor(out=o, in0=bank("att", tile)[:, 0:DH], scalar=sc, in1=o, op0=ALU.mult, op1=ALU.add))
                    signal(rsem("att", tile))
                    signal(S["o_ready"])
            ada_out(3)
            residual("nout", 2)
            norm(3)
            moe(1)
            norm(4)

        @block.gpsimd
        def _(pool):
            G = nc.gpsimd
            cnt = [0]

            def link(ins):
                cnt[0] += 1
                ins.then_inc(S["pool_chain"], 1)
                pool.wait_ge(S["pool_chain"], cnt[0])

            link(G.memset(ident[:, :], 0.0))
            link(G.affine_select(out=ident[:, :], in_=ident[:, :], compare_op=ALU.not_equal, fill=1.0, base=0,
                                 pattern=[[-1, P]], channel_multiplier=1))
            link(G.memset(ones[:, :], 1.0))
            link(G.memset(raw[:, :, :], 0.0))
            link(G.memset(cpad[:, :, 0:3], 0.0))
            link(G.memset(sgn[0:64, :], 1.0))
            link(G.memset(sgn[64:128, :], -1.0))
            link(G.memset(cmask[:, :], 1.0))
            link(G.affine_select(out=cmask[:, :], in_=cmask[:, :], compare_op=ALU.is_ge, fill=0.0, base=0,
                                 pattern=[[1, P]], channel_multiplier=-1))
            link(G.memset(perm[:, :], 0.0))
            link(G.affine_select(out=perm[:, :], in_=perm[:, :], compare_op=ALU.not_equal, fill=1.0, base=-64,
                                 pattern=[[-1, P]], channel_multiplier=1))
            link(G.affine_select(out=perm[:, :], in_=perm[:, :], compare_op=ALU.not_equal, fill=-1.0, base=64,
                                 pattern=[[-1, P]], channel_multiplier=1))
            link(G.iota(jj[:, :], pattern=[[1, NCH]], base=0, channel_multiplier=0,
                        allow_small_or_imprecise_dtypes=True))
            G.nop().then_inc(S["const_ready"], 1)
            pool.wait_ge(S["g_ready"], 1)
            for tau in range(TAU):
                pool.dma_start(Mt[16 * tau:16 * tau + 16, :, 16 * tau:P], Gk[:, :, 0:P - 16 * tau]).then_inc(S["m_in"], 16)
            pool.wait_ge(S["st_ready"], 1)
            link(G.memset(gluw[:, :, :], 0.0))
            pool.dma_start(headg[:, :], a["a_head_g"].rearrange("o g -> (o g)").partition_broadcast(P)).then_inc(S["headg_in"], 16)
            for i in range(8):
                if i % 2:
                    pool.wait_ge(S["glu_used"], (i + 1) // 2)
                elif i:
                    wait_full(pool, "s5_glu", i // 2 - 1)
                for tau in range(TAU):
                    pool.dma_start(gluw[16 * tau:16 * tau + 16, :, 16 * tau:16 * tau + 16],
                                   a["s5_glu_w"][0, 4 * i:4 * i + 4].rearrange("g c e -> c g e")).then_inc(S["glu_in"], 16)
            for l in range(2):
                pool.dma_start(wr[:, l, :, 0:NG], a["r_grp_w"][l].rearrange("(k p) g -> p k g", p=P)).then_inc(S["wr_in"], 16)
                pool.dma_start(wr[:, l, :, NG:], a["r_exp_w"][l].rearrange("(k p) g e -> p k (g e)", p=P)).then_inc(S["wr_in"], 16)
            pool.dma_start(rb[:, :, 0:NG], a["r_grp_b"].partition_broadcast(P)).then_inc(S["wr_in"], 16)
            pool.dma_start(rb[:, :, NG:], a["r_exp_b"].rearrange("l g e -> l (g e)").partition_broadcast(P)).then_inc(S["wr_in"], 16)
            pool.wait_ge(S["x_upd"], KD)
            pool.dma_start(wng[:, :, :], a["n_w_in"][0, :, 2560:2608].rearrange("(k p) c -> p k c", p=P)).then_inc(S["nsa_in"], 16)
            for half in range(2):
                pool.dma_start(w2k[:, :, 64 * half:64 * half + 64],
                               a["n_cmp_w2"][0, 0].rearrange("(f p) d -> p f d", p=P)).then_inc(S["nsa_in"], 16)
            pool.dma_start(w2v[:, :, :], a["n_cmp_w2"][0, 1].rearrange("(f p) d -> p f d", p=P)).then_inc(S["nsa_in"], 16)
            pool.dma_start(b2v[:, :], a["n_cmp_b2"][0, 1].partition_broadcast(P)).then_inc(S["nsa_in"], 16)
            pool.dma_start(bng[:, :], a["n_b_gate"][0].partition_broadcast(P)).then_inc(S["nsa_in"], 16)
            link(G.memset(tab[32:33, :], NEG))
            pool.dma_start(tab[0:32, :], a["rel_bias"]).then_inc(S["nsa_in"], 16)
            pool.dma_start(oh[:, :], onehot).then_inc(S["nsa_in"], 16)
            pool.wait_ge(S["nsa_in"], NSA_IN)
            pool.wait_ge(S["f_ready"], 1)
            pool.dma_start(bias_d, dims(frs[:, 0:1], [0, REP], [1, 1024])).then_inc(S["f_out"], 16)
            pool.wait_ge(S["f_out"], 16)
            pool.wait_ge(S["x_upd"], 2 * KD)
            for p in range(0, P, REP):
                pool.dma_start(biasT[p:p + REP, :, :],
                               bass.AP(tensor=bias_d.tensor, offset=bias_d.offset + P - 1 - p,
                                       ap=[[1023, REP], [REP * 1024, NH], [1, T]])).then_inc(S["bias_in"], 16)


NSA_IN = 16 * 8
RAW_IN = 16 * 17
SMALL_IN = 16 * 17


def bucket_rows():
    dist = np.arange(2 * T) - T
    exact = BUCKETS // 2
    ratio = np.log(np.maximum(dist, 1).astype(np.float32) / np.float32(exact)) / np.float32(np.log(MAXD / exact))
    large = np.minimum(exact + (ratio * np.float32(BUCKETS - exact)).astype(np.int32), BUCKETS - 1)
    bucket = np.where(dist < 0, BUCKETS, np.where(dist < exact, dist, large))
    return (np.arange(BUCKETS + 1)[:, None] == bucket[None, :]).astype(np.float32)


def kernel(**inputs):
    import concourse.bacc as _bacc
    from concourse.bass_utils import run_bass_kernel_spmd as _run

    nc = _bacc.Bacc("TRN2", target_bir_lowering=False, num_devices=1)
    arrays, args = {}, {}
    for name in NAMES:
        v = np.ascontiguousarray(inputs[name])
        arrays[f"in_{name}"] = v
        args[name] = nc.dram_tensor(f"in_{name}", v.shape, mybir.dt.from_np(v.dtype), kind="ExternalInput").ap()
    arrays["in_onehot"] = bucket_rows()
    onehot = nc.dram_tensor("in_onehot", [33, 1024], F32, kind="ExternalInput").ap()
    out = nc.dram_tensor("out0", [1, T, D], F32, kind="ExternalOutput").ap()
    build(nc, args, onehot, out)
    r = _run(nc, [arrays], core_ids=[0])
    return r.results[0]["out0"]
```

```python
from contextlib import ExitStack

import numpy as np

import concourse.bass as bass
from concourse import mybir

F32 = mybir.dt.float32
U32 = mybir.dt.uint32
ALU = mybir.AluOpType
ACT = mybir.ActivationFunctionType
AX = mybir.AxisListType

P = 128
T = 512
D = 1024
KD = D // P
NT = T // P
MA = 512
MH = 4
G5, S5P, S5C = 32, 64, 16
TAU = 8
NCH = T // TAU
NPW = TAU + 1
NH, NKV, R, DH = 16, 4, 4, 64
NCMP, CL, CS = 31, 32, 16
CH = 256
NE, NG, NPG, FH = 16, 4, 4, 256
NX = 2 * T // P - 1
NI2 = NE + NX
EPS = 1e-6
NEG = -1e30
REP = 8
BUCKETS, MAXD = 32, 128
ADA_PARTS = 6
NSLOT = 4
NXS = 3
PB = 128
CC = 256
PI = float(np.pi)
C1 = 6.28125
C2 = float(np.float32(2 * np.pi - C1))
C3 = float(2 * np.pi - C1 - C2)
MAGIC = 12582912.0

STAGES = [("x", KD), ("param", 1), ("ct", 2), ("ada0", 1), ("s5_e", 8), ("s5_g", 8), ("norm0", 1),
          ("u", 4), ("u2", 8), ("ut", 4), ("gates", 2), ("qk", 4), ("s5_e1", 4), ("s5_eb", 4), ("qk2", 4),
          ("s5_zb", 4), ("s5_y", 4), ("v", 8), ("ada1_0", 1), ("s5_glu", 4), ("o", 8), ("s5_k", 4), ("s5_t", 4),
          ("gcol", 1)]
STAGES += [("ml_h", 4)]
for _h in range(MH):
    STAGES += [("ml_h", 1 + NT + 2)] + [(f"ada1_{_h + 1}", 1)]
STAGES += [("ml_t", MH), ("ada1_5", 1), ("aout", 4), ("ada2_0", 1), ("aout", 4), ("ada2_1", 1), ("norm1", 1), ("ada2_2", 1)]


NPRE = 8
PAIRS = -(-(NI2 - NPRE) // 2)
MOE_ORDER = [("x0", 0), ("x1", 0)]
for _e in range(NI2 + 1):
    MOE_ORDER += [("i", _e - 1)] * (1 <= _e <= PAIRS)
    MOE_ORDER += [(k, _e + 1) for k in ("x0", "x1") if _e + 1 < NI2] + [("ht", _e - 1)] * (_e > 0)
    MOE_ORDER += [("gu", _e)] * (_e < NI2) + [(k, _e - 1) for k in ("y0", "y1") if _e]
MT = {x: i for i, x in enumerate(MOE_ORDER)}
LISTS = NPRE // 4 + PAIRS
G_USED = NPRE - NPRE // 4 + NI2 - NPRE - PAIRS


def moe_stages(l):
    return ([(f"hx{l}", KD), (f"route{l}", 1), (f"pos{l}", 1), (f"idx{l}", NPRE // 4)]
            + [(f"ada2_{q}", 1) for q in (3, 4, 5) if l == 0])


def moe_stages2(l):
    return [(f"moe{l}", len(MOE_ORDER)), (f"yt{l}", KD)]


STAGES += moe_stages(0) + moe_stages2(0)
ITEMS = [(i, h, b) for i in range(NT) for h in range(NH) for b in range(2)]
NI = len(ITEMS)
ADA_AT = {20 * (q + 1): q for q in range(ADA_PARTS)}
ATT_ORDER = []
for _n in range(NI + 3):
    ATT_ORDER += [(k, _n - lag) for k, lag in (("s", 0), ("t", 2), ("o", 3)) if 0 <= _n - lag < NI]
    ATT_ORDER += [("a", ADA_AT[_n])] if _n in ADA_AT else []
ATT = {x: i for i, x in enumerate(ATT_ORDER)}
STAGES += [("norm2", 1), ("nq", 8), ("nkc", 4), ("nks", 2), ("nvs", 4), ("nkw", 2),
           ("nvw", 4), ("ngate", 1), ("fvec", 2), ("cpos", 4), ("chid", 4), ("kcmp", 1), ("vcmp", 1),
           ("cmpa", 5 * NT), ("att", len(ATT_ORDER)), ("ot", KD), ("nout", KD), ("norm3", 1)]
STAGES += moe_stages(1) + moe_stages2(1)
STAGES += [("norm4", 1), ("xo", 8)]
TILE = {}
for _name, _count in STAGES:
    _first = sum(1 for x in TILE if x[0] == _name)
    for _i in range(_first, _first + _count):
        TILE[(_name, _i)] = len(TILE)

def expert_chunks(l):
    out = []
    for e in range(NI2 + 1):
        out += [(w, l, e) for w in ("eg", "eu") if e < NI2] + [("ed", l, e - 1)] * (e > 0)
    return out


CHUNKS = ([("ada", 0, c) for c in range(12)] + [("ain", 0, c) for c in (8, 9, 0, 1, 2, 3, 4, 5)]
          + [("ada", 1, 0), ("ada", 1, 1), ("ain", 0, 6), ("ain", 0, 7)] + [("ada", 1, c) for c in range(2, 12)]
          + [("aout", 0, 0), ("aout", 0, 1), ("ada", 2, 0), ("ada", 2, 1), ("aout", 0, 2), ("aout", 0, 3)]
          + [("ada", 2, c) for c in range(2, 12)]
          + expert_chunks(0) + [("nin", 0, c) for c in range(10)]
          + [("cw", j, c) for j in range(2) for c in range(2)]
          + [("ada", 3, c) for c in range(12)] + [("nout", 0, c) for c in range(4)]
          + expert_chunks(1))
PLACE, LAST = {}, {}
for _i, _c in enumerate(CHUNKS):
    _slot = min(range(NSLOT + (NXS if _c[0] in ("eg", "eu", "ed") else 0)), key=lambda s: LAST.get(s, (-1,))[0])
    _former = LAST.get(_slot, (-1, 0, None))
    PLACE[_c] = (_slot, _former[1] + 1, _former[2])
    LAST[_slot] = (_i, _former[1] + 1, _c)
LAST_TILE = {("ain", 0, 8): ("u", 1), ("ain", 0, 9): ("u", 3), ("ain", 0, 0): ("qk", 1), ("ain", 0, 1): ("qk", 3),
             ("ain", 0, 2): ("qk2", 1), ("ain", 0, 3): ("qk2", 3), ("ain", 0, 4): ("v", 3), ("ain", 0, 5): ("v", 7),
             ("ain", 0, 6): ("o", 3), ("ain", 0, 7): ("o", 7)}
LAST_TILE.update({("aout", 0, c): ("aout", 2 * c + 1) for c in range(4)})
LAST_TILE.update({("nin", 0, c): ("nq", 2 * c + 1) for c in range(4)})
LAST_TILE.update({("nin", 0, 4): ("nkc", 1), ("nin", 0, 5): ("nkc", 3), ("nin", 0, 6): ("nks", 1),
                  ("nin", 0, 7): ("nvs", 3), ("nin", 0, 8): ("nkw", 1), ("nin", 0, 9): ("nvw", 3)})
LAST_TILE.update({(w, l, e): (f"moe{l}", MT[(k, e)]) for l in range(2) for e in range(NI2)
                  for w, k in (("eg", "gu"), ("eu", "gu"), ("ed", "y1"))})
LAST_TILE.update({("nout", 0, c): ("nout", 2 * c + 1) for c in range(4)})


NAMES = ["x", "c", "rel_bias", "ada_w", "ada_b", "norm_g", "final_g", "a_w_in", "a_conv", "a_b_i", "a_b_f",
         "a_head_g", "s5_lam_re", "s5_lam_im", "s5_log_dt", "s5_b_re", "s5_b_im", "s5_c_re", "s5_c_im", "s5_d",
         "s5_glu_w", "s5_glu_b", "a_w_out", "n_w_in", "n_b_gate", "n_cmp_pos", "n_cmp_w1", "n_cmp_b1",
         "n_cmp_w2", "n_cmp_b2", "n_w_out", "r_grp_w", "r_grp_b", "r_exp_w", "r_exp_b", "e_w_gate", "e_w_up",
         "e_w_down"]


def dims(ap, *free, off=0):
    return bass.AP(tensor=ap.tensor, offset=ap.offset + off, ap=[list(ap.ap[0])] + [list(f) for f in free])


def build(nc, a, onehot, out):
    bias_d = nc.dram_tensor("bias_rev", [NH, REP, 1024], F32, kind="Internal").ap()
    h_d = nc.dram_tensor("h_tokens", [T, D], F32, kind="Internal").ap()
    y_d = nc.dram_tensor("expert_rows", [NI2 * P, D], F32, kind="Internal").ap()
    with ExitStack() as ctx:
        def sb(name, shape):
            return ctx.enter_context(nc.sbuf_tensor(name, shape, F32))

        def sem(name):
            return ctx.enter_context(nc.semaphore(name))

        banks = [ctx.enter_context(nc.psum_tensor(f"bank{i}", [P, 512], F32)) for i in range(8)]
        ring = sb("ring", [P, NSLOT, KD, CC])
        xT = sb("xT", [P, KD, T])
        hT = sb("hT", [P, KD, T])
        mixT = sb("mixT", [P, KD, T])
        arena = sb("arena", [P, 27136])
        ident = sb("ident", [P, P])
        ones = sb("ones", [P, P])
        par = sb("par", [P, 128 + 96])
        mod = sb("mod", [P, 4, 24])
        amul = sb("amul", [P, KD])
        sil = sb("sil", [P, KD])
        rstd = sb("rstd", [P, T])
        small = sb("small", [P, 96])

        def region(start, shape, parts=P, of=arena):
            n = int(np.prod(shape))
            ap = of[0:parts, start:start + n]
            if len(shape) == 1:
                return ap
            letters = "abcde"[:len(shape)]
            return ap.rearrange(f"p ({' '.join(letters)}) -> p {' '.join(letters)}",
                                **{x: s for x, s in zip(letters[1:], shape[1:])})

        Mt = region(0, [G5, P])
        ET = region(4096, [G5, P])
        Vaug = region(4096, [NT, MH, 129])
        F9 = region(8192, [G5, NPW, S5C])
        twc = region(12800, [G5, NCH])
        tws = region(14848, [G5, NCH])
        hmx = region(12800, [NT, MH, P])
        uk = region(16896, [G5, TAU, S5C])
        uk2 = region(16896, [TAU, MA], parts=NCH)
        Gk = region(16896, [G5, P], parts=16)
        ea = region(16896, [G5, NCH])
        za = region(18944, [G5, NCH])
        Wb = [region(16896 + 2048 * i, [NT, T]) for i in range(2)]
        qkT = region(20992, [KD, T])
        Ug = region(25088, [G5, NCH])
        Ba = region(20992, [G5, S5C])
        Bb = region(21504, [G5, S5C])
        Ca = region(22016, [G5, S5C])
        Cb = region(22528, [G5, S5C])
        Bba = region(23040, [G5, S5C])
        Bbb = region(23552, [G5, S5C])
        pc = region(24064, [G5, NPW])
        ps = region(24352, [G5, NPW])
        pt = region(24640, [G5, NPW])
        crow = region(25088, [2, 4, P])
        lrow = region(26112, [2, P], parts=32)
        s5s = region(26368, [16, G5])
        Ea = region(0, [G5, TAU, S5C], of=mixT[:, :, :].rearrange("p a b -> p (a b)"))
        so = region(0, [NT, MA], of=mixT[:, :, :].rearrange("p a b -> p (a b)"))
        F9f = region(8192, [G5, NPW * S5C])

        xg = region(0, [4, D])
        xgT = region(4096, [2, KD, P])
        hid = region(6144, [2, CC])
        hidT = region(6656, [2, 2, P])
        ya = region(0, [2, NT, D])
        ysb = region(8192, [2, D])
        Gm = region(10240, [2, NT, P])
        rt = region(11264, [512])
        posx = region(11776, [NT, NI2])
        vt = region(11868, [NT, NI2, 2])
        gc = region(12052, [NI2])
        idx = region(12075, [NI2]).bitcast(U32)
        idx2 = region(12098, [2 * NT]).bitcast(U32)
        ixf = region(12106, [16])
        tmp64 = region(12122, [NT, NE])
        nE, Sx, Si = (region(12186 + 16 * i, [NE]) for i in range(3))
        sel = region(12234, [NX, NE])
        xk = region(12346, [NX]).bitcast(U32)
        xkf, bk, ck = (region(12353 + 7 * i, [NX]) for i in range(3))
        tmx = region(12376, [NX, NE])
        htok = region(12544, [NT, D])
        xring = [region(16640 + i * KD * CC, [KD, CC]) for i in range(NXS)]
        wr = sb("wr", [P, 2, KD, NG + NE])
        rb = sb("rb", [P, 2, NG + NE])
        biasT = region(0, [NH, T])
        biasC = region(8192, [NT, NH, 32])
        kTd = region(10240, [2, NKV, T])
        vN = region(14336, [2, NT, CC])
        kc2 = region(16384, [2, NKV, T + 1])
        on = region(16384, [NT, D])
        Pw = region(20488, [4, T])
        PT = region(22536, [4, T])
        oh = region(20488, [1024], parts=33)
        chid = region(22536, [2, 2, NKV, 32])
        wng = region(24584, [KD, 48])
        w2k = region(24968, [2, P])
        w2v = region(25224, [2, DH])
        b2v = region(25352, [DH])
        bng = region(25416, [48])
        gts = region(25464, [NT, 48])
        tab = region(25656, [NH], parts=33)
        kcT = region(25672, [NKV, 32])
        Vc = region(25800, [NKV, CC])
        cb = region(26824, [2, 2])
        stat = region(26832, [128])
        qT = mixT
        frs = region(23560, [1024], parts=NH)
        osb = region(8192, [NT, D])

        wif = sb("wif", [P, KD, 8])
        gluc = region(7184, [G5, S5C])
        blk = region(7696, [TAU])
        vecs = sb("vecs", [P, 8])
        d5 = sb("d5", [16, G5])
        glub = sb("glub", [P, G5])
        headg = region(6672, [MA])
        perm = sb("perm", [P, P])
        cpad = sb("cpad", [P, 2, T + 3])
        ct1 = sb("ct1", [P, T])
        gluw = [region(6160, [4, TAU, S5C]), ct1[:, :].rearrange("p (g t e) -> p g t e", g=4, t=TAU)]
        grow = sb("grow", [4, 3, T])
        gcol = sb("gcol", [P, 2, NT, MH])
        sgn = sb("sgn", [P, 1])
        tokn = sb("tokn", [P, NT])
        jj = sb("jj", [P, P])
        cmask = sb("cmask", [P, P])
        r8 = sb("r8", [P, G5])
        raw = sb("raw", [P, 2, P])

        wsem = [sem(f"chunk_in{i}") for i in range(NSLOT + NXS)]
        ada_used = sem("ada_used")
        full = [sem(f"bank_full{i}") for i in range(8)]
        free = [sem(f"bank_free{i}") for i in range(8)]
        names = ["x_in", "raw_in", "small_in", "const_ready", "x_ready", "par_ready", "sil_ready", "mod_ready",
                 "pow_ready", "e_ready", "et_ready", "g_ready", "m_in", "sq_ready", "h_part", "h_ready",
                 "uk_ready", "ug_ready", "act_s5", "dve_s5", "ea_ready", "za_ready", "xs_ready", "y_ready",
                 "ys_ready", "glu_in", "glu_ready", "gates_ready", "gcol_ready", "cpad_ready", "conv_ready", "sig_ready",
                 "qk_ready", "v_ready", "so_ready", "arg_ready", "dexp_ready", "w_ready", "hm_ready",
                 "mixh_ready", "mix_ready", "x_upd", "dve_chain", "act_chain", "pool_chain", "dbg_out",
                 "sqrt_ready", "rs_ready", "sk_ready", "st_ready", "diag_ready", "var_ready", "act_gate",
                 "uk_free", "out_sem", "headg_in", "ut_ready", "cw_used", "out_ready", "wr_in", "gate_t", "esig", "hid_ready", "acc_chain",
                 "nsa_in", "oh_in", "q_ready", "kc_ready", "ktd_ready", "vn_ready", "f_ready", "f_out", "bias_in",
                 "biasc_ready", "cb_ready", "chid_ready", "kcmp_ready", "vcmp_ready", "cs_ready", "ce_ready", "cp_ready",
                 "pct_ready", "p_ready", "e_done", "pt_ready", "o_ready", "ot_ready", "ng_ready", "gsig", "route_e", "route_s", "cpre", "hx_ready", "h_out", "mask_ready", "lists_ready", "g_part", "g_used",
                 "idx_ready", "row_ready", "xt_ready", "ht_ready", "y0_ready", "y1_ready", "y_out0", "y_out1", "ya_in0", "ya_in1", "ya_in2", "ya_in3", "yt_ready", "tok_ready", "xk_ready", "ada_sum"]
        S = {n: sem(n) for n in names}
        xg_in = [sem(f"xg_in{i}") for i in range(4)]

        def bank(stage, i=0):
            return banks[TILE[(stage, i)] % 8]

        def wait_full(eng, stage, i=0):
            n = TILE[(stage, i)]
            eng.wait_ge(full[n % 8], n // 8 + 1)

        def wait_bank(eng, stage, i=0):
            n = TILE[(stage, i)]
            if n // 8:
                eng.wait_ge(free[n % 8], n // 8)

        def fsem(stage, i=0):
            return full[TILE[(stage, i)] % 8]

        def rsem(stage, i=0):
            return free[TILE[(stage, i)] % 8]

        block = ctx.enter_context(nc.Block())

        def chunk(kind, m, c):
            s = PLACE[(kind, m, c)][0]
            return ring[:, s, :, :] if s < NSLOT else xring[s - NSLOT]

        @block.sync
        def _(sp):
            for t in range(NT):
                sp.dma_start(hT[:, 2 * t:2 * t + 2, :].rearrange("p a b -> p (a b)"),
                             a["x"][0, t * P:(t + 1) * P, :]).then_inc(S["x_in"], 16)
            ain_cols = [0, 256, 512, 768, 1024, 1280, 1536, 1792, 2056, 2312]
            chosen = {}

            def expert(w, l, e):
                if e < NE:
                    return w[l, e]
                if (l, e) not in chosen:
                    if e == NE:
                        sp.wait_ge(S["xk_ready"], l + 1)
                    chosen[l, e] = sp.value_load(xk[0:1, e - NE:e - NE + 1], min_val=0, max_val=NE - 1)
                return w[l, bass.ds(chosen[l, e], 1)].rearrange("o d f -> (o d) f")

            src = {
                "ada": lambda m, c: a["ada_w"][m // 2, m % 2, :, c * CC:(c + 1) * CC],
                "ain": lambda m, c: a["a_w_in"][0, :, ain_cols[c]:ain_cols[c] + CC],
                "aout": lambda m, c: a["a_w_out"][0, :, c * CC:(c + 1) * CC],
                "nin": lambda m, c: a["n_w_in"][0, :, c * CC:(c + 1) * CC],
                "nout": lambda m, c: a["n_w_out"][0, :, c * CC:(c + 1) * CC],
                "cw": lambda j, c: a["n_cmp_w1"][0, j, c * 1024:(c + 1) * 1024, :],
                "eg": lambda l, e: expert(a["e_w_gate"], l, e),
                "eu": lambda l, e: expert(a["e_w_up"], l, e),
                "ed": lambda l, e: expert(a["e_w_down"], l, e),
            }
            in_arena = set()
            for kind, m, c in CHUNKS:
                s, count, former = PLACE[(kind, m, c)]
                if s >= NSLOT and (m, s) not in in_arena:
                    in_arena.add((m, s))
                    sp.wait_ge(S["x_upd"], KD * (2 * m + 1))
                if former:
                    k0, m0, c0 = former
                    if k0 == "cw":
                        sp.wait_ge(S["cw_used"], 2 * m0 + c0 + 1)
                    elif k0 == "ada":
                        sp.wait_ge(ada_used, 12 * m0 + c0 + 1)
                    else:
                        wait_full(sp, *LAST_TILE[(k0, m0, c0)])
                dst = chunk(kind, m, c)
                w = src[kind](m, c)
                if kind == "ed":
                    dst = dst.rearrange("p k c -> p (k c)").rearrange("p (k c) -> p k c", c=D)
                w = w.rearrange("(p k) c -> p k c" if kind in ("eg", "eu") else "(k p) c -> p k c", p=P)
                sp.dma_start(dst, w).then_inc(wsem[s], 16)
            for t in range(NT):
                sp.wait_ge(S["out_ready"], 2 * t + 2)
                sp.dma_start(out[0, t * P:(t + 1) * P, :], osb[:, t, :]).then_inc(S["out_sem"], 16)
            sp.wait_ge(S["out_sem"], 16 * NT)

        def wait_chunk(eng, kind, m, c):
            s, count, _ = PLACE[(kind, m, c)]
            eng.wait_ge(wsem[s], 16 * count)

        small_loads = []

        def skv(tau, i):
            return uk2[:, tau, i * P:(i + 1) * P]

        @block.tensor
        def _(pe):
            mm, tr = nc.tensor.matmul, nc.tensor.transpose
            pe.wait_ge(S["const_ready"], 1)
            pe.wait_ge(S["x_in"], 16 * NT)
            for j in range(KD):
                for t in range(NT):
                    xin = hT[:, 2 * t:2 * t + 2, :].rearrange("p a b -> p (a b)")
                    last = tr(bank("x", j)[:, t * P:(t + 1) * P], xin[:, j * P:(j + 1) * P], ident[:, :])
                last.then_inc(fsem("x", j), 1)
            wait_bank(pe, "param")
            pe.wait_ge(S["raw_in"], RAW_IN)
            b = bank("param")
            tr(b[:, 0:128], raw[:, 0, :], ident[:, :])
            tr(b[:, 128:224], raw[0:96, 1, :], ident[0:96, 0:96])
            tr(b[:, 224:256], lrow[:, 0, :], ident[0:32, 0:32])
            tr(b[:, 256:288], lrow[:, 1, :], ident[0:32, 0:32]).then_inc(fsem("param"), 1)
            for s in range(2):
                wait_bank(pe, "ct", s)
                for t in range(4):
                    last = tr(bank("ct", s)[:, t * P:(t + 1) * P], crow[:, s, t, :], ident[:, :])
                last.then_inc(fsem("ct", s), 1)

            def ada(m, chunks, stage, i=0):
                wait_bank(pe, stage, i)
                pe.wait_ge(S["sil_ready"], 1)
                for c in chunks:
                    w = chunk("ada", m, c)
                    if m:
                        pe.wait_ge(S["ada_sum"], 12 * (m - 1) + c + 1)
                        for j in range(2):
                            last = mm(bank(stage, i)[:, 2 * c + j:2 * c + j + 1], w[:, 0, j * P:(j + 1) * P],
                                      ones[:, 0:1], start=True, stop=True)
                        last.then_inc(ada_used, 1)
                        continue
                    wait_chunk(pe, "ada", m, c)
                    for j in range(2):
                        for k in range(KD):
                            last = mm(bank(stage, i)[:, 2 * c + j:2 * c + j + 1], w[:, k, j * P:(j + 1) * P],
                                      sil[:, k:k + 1], start=(k == 0), stop=(k == KD - 1))
                    last.then_inc(ada_used, 1)
                mm(bank(stage, i)[:, 32:33], ones[:, :], sil[:, 0:1], start=True, stop=True).then_inc(fsem(stage, i), 1)

            def ada_part(m, q):
                ada(m, (2 * q, 2 * q + 1), f"ada{m}_{q}")

            def norm(m):
                wait_bank(pe, f"norm{m}")
                b = bank(f"norm{m}")
                for k in range(KD):
                    pe.wait_ge(S["sq_ready"], KD * m + k + 1)
                    last = mm(b[:, :], ones[:, :], hT[:, k, :], start=(k == 0), stop=(k == KD - 1))
                last.then_inc(fsem(f"norm{m}"), 1)

            ada(0, range(12), "ada0")
            for g in range(G5):
                if g % 4 == 0:
                    wait_bank(pe, "s5_e", g // 4)
                    pe.wait_ge(S["e_ready"], 1)
                last = tr(bank("s5_e", g // 4)[:, (g % 4) * P:(g % 4 + 1) * P],
                          Ea[:, g].rearrange("p a b -> p (a b)"), ident[:, :])
                if g % 4 == 3:
                    last.then_inc(fsem("s5_e", g // 4), 1)
            for g in range(G5):
                if g % 4 == 0:
                    wait_bank(pe, "s5_g", g // 4)
                    pe.wait_ge(S["pow_ready"], 1)
                last = mm(bank("s5_g", g // 4)[0:16, (g % 4) * P:(g % 4 + 1) * P], Bba[:, g, :],
                          F9f[:, g, 0:P], start=True, stop=True)
                if g % 4 == 3:
                    last.then_inc(fsem("s5_g", g // 4), 1)
            norm(0)

            def tok_proj(stage, kind, m, cs, lhs, nwait=False):
                for n, c in enumerate(cs):
                    wait_chunk(pe, kind, m, c)
                    for t in range(NT):
                        wait_bank(pe, stage, 4 * n + t)
                        for k in range(KD):
                            last = mm(bank(stage, 4 * n + t)[:, 0:CC], lhs(k, t), chunk(kind, m, c)[:, k, :],
                                      start=(k == 0), stop=(k == KD - 1))
                        last.then_inc(fsem(stage, 4 * n + t), 1)

            def ch_proj(stage, kind, m, cs, first=0):
                for n, c in enumerate(cs):
                    wait_chunk(pe, kind, m, c)
                    for j in range(2):
                        i = first + 2 * n + j
                        wait_bank(pe, stage, i)
                        for k in range(KD):
                            last = mm(bank(stage, i)[:, :], chunk(kind, m, c)[:, k, j * P:(j + 1) * P], hT[:, k, :],
                                      start=(k == 0), stop=(k == KD - 1))
                        last.then_inc(fsem(stage, i), 1)

            pe.wait_ge(S["h_ready"], KD)
            ch_proj("u", "ain", 0, (8, 9))
            for i in range(8):
                wait_bank(pe, "u2", i)
                pe.wait_ge(S["ut_ready"], 4)
                for q in range(4):
                    last = tr(bank("u2", i)[0:NCH, q * P:(q + 1) * P],
                              dims(Ug[:, 8 * (i // 2), :], [TAU, NCH], off=4 * (i % 2) + q), ident[:, :])
                last.then_inc(fsem("u2", i), 1)
            for g in range(G5):
                if g % 8 == 0:
                    wait_bank(pe, "ut", g // 8)
                    pe.wait_ge(S["uk_ready"], 8)
                last = tr(bank("ut", g // 8)[:, (g % 8) * NCH:(g % 8 + 1) * NCH],
                          uk[0:NCH, g].rearrange("p a b -> p (a b)"), ident[0:NCH, 0:NCH])
                if g % 8 == 7:
                    last.then_inc(fsem("ut", g // 8), 1)
            for s in range(2):
                wait_bank(pe, "gates", s)
                for k in range(KD):
                    last = mm(bank("gates", s)[0:4, :], wif[:, k, 4 * s:4 * s + 4], hT[:, k, :],
                              start=(k == 0), stop=(k == KD - 1))
                last.then_inc(fsem("gates", s), 1)
            ch_proj("qk", "ain", 0, (0, 1))
            for g in range(G5):
                if g % 8 == 0:
                    wait_bank(pe, "s5_e1", g // 8)
                    pe.wait_ge(S["ug_ready"], 4)
                    pe.wait_ge(S["et_ready"], 8)
                last = mm(bank("s5_e1", g // 8)[:, (g % 8) * NCH:(g % 8 + 1) * NCH], ET[:, g, :], Ug[:, g, :],
                          start=True, stop=True)
                if g % 8 == 7:
                    last.then_inc(fsem("s5_e1", g // 8), 1)
            for i in range(4):
                wait_bank(pe, "s5_eb", i)
                pe.wait_ge(S["ea_ready"], i + 1)
                mm(bank("s5_eb", i)[:, :], perm[:, :], ea[:, 8 * i:8 * i + 8, :].rearrange("p a b -> p (a b)"),
                   start=True, stop=True).then_inc(fsem("s5_eb", i), 1)
            ch_proj("qk2", "ain", 0, (2, 3))
            for i in range(4):
                wait_bank(pe, "s5_zb", i)
                pe.wait_ge(S["za_ready"], 1)
                mm(bank("s5_zb", i)[:, :], perm[:, :], za[:, 8 * i:8 * i + 8, :].rearrange("p a b -> p (a b)"),
                   start=True, stop=True).then_inc(fsem("s5_zb", i), 1)
            pe.wait_ge(S["m_in"], 16 * TAU)
            pe.wait_ge(S["xs_ready"], 4)
            for g in range(G5):
                if g % 8 == 0:
                    wait_bank(pe, "s5_y", g // 8)
                o = bank("s5_y", g // 8)[:, (g % 8) * NCH:(g % 8 + 1) * NCH]
                mm(o, Mt[:, g, :], Ug[:, g, :], start=True, stop=False)
                last = mm(o[:, 1:NCH], F9f[:, g, S5C:S5C + P], ea[:, g, 0:NCH - 1], start=False, stop=True)
                if g % 8 == 7:
                    last.then_inc(fsem("s5_y", g // 8), 1)
            tok_proj("v", "ain", 0, (4, 5), lambda k, t: hT[:, k, t * P:(t + 1) * P])
            ada_part(1, 0)
            for g in range(G5):
                if g % 8 == 0:
                    wait_bank(pe, "s5_glu", g // 8)
                    pe.wait_ge(S["y_ready"], g // 8 + 1)
                if g % 4 == 0:
                    pe.wait_ge(S["glu_ready"], g // 4 + 1)
                last = mm(bank("s5_glu", g // 8)[:, (g % 8) * NCH:(g % 8 + 1) * NCH], gluw[g // 4 % 2][:, g % 4].rearrange("p t e -> p (t e)"),
                          za[:, g, :], start=True, stop=True)
                if g % 8 == 7:
                    last.then_inc(fsem("s5_glu", g // 8), 1)
            tok_proj("o", "ain", 0, (6, 7), lambda k, t: hT[:, k, t * P:(t + 1) * P])
            for i in range(8):
                st, ii = ("s5_k", i) if i < 4 else ("s5_t", i - 4)
                wait_bank(pe, st, ii)
                pe.wait_ge(S["ys_ready"], 4)
                for g in range(4 * i, 4 * i + 4):
                    last = tr(bank(st, ii)[0:NCH, (g % 4) * P:(g % 4 + 1) * P], Ug[:, g, :], ident[:, :])
                last.then_inc(fsem(st, ii), 1)
            wait_bank(pe, "gcol")
            pe.wait_ge(S["gates_ready"], 1)
            for s in range(2):
                for t in range(NT):
                    last = tr(bank("gcol")[:, (s * NT + t) * MH:(s * NT + t + 1) * MH],
                              grow[:, s, t * P:(t + 1) * P], ident[0:4, 0:4])
            last.then_inc(fsem("gcol"), 1)
            for i in range(KD // 2):
                pe.wait_ge(S["sk_ready"], 8)
                wait_bank(pe, "ml_h", i)
                for tau in range(TAU):
                    last = tr(bank("ml_h", i)[:, tau * NCH:(tau + 1) * NCH], skv(tau, i), ident[0:NCH, 0:NCH])
                last.then_inc(fsem("ml_h", i), 1)
            n = 4
            for h in range(MH):
                wait_bank(pe, "ml_h", n)
                mm(bank("ml_h", n)[:, :], dims(ident[0:MH, h:h + 1], [0, P]), rstd[0:MH, :], start=True, stop=True).then_inc(fsem("ml_h", n), 1)
                n += 1
                pe.wait_ge(S["qk_ready"], KD)
                for j in range(NT):
                    wait_bank(pe, "ml_h", n)
                    mm(bank("ml_h", n)[:, j * P:], qkT[:, MH + h, j * P:(j + 1) * P], qkT[:, h, j * P:],
                       start=True, stop=True).then_inc(fsem("ml_h", n), 1)
                    n += 1
                pe.wait_ge(S["w_ready"], h + 1)
                pe.wait_ge(S["v_ready"], 8)
                for i in range(0, NT, 2):
                    wait_bank(pe, "ml_h", n)
                    for ii in range(i, i + 2):
                        for j in range(ii + 1):
                            last = mm(bank("ml_h", n)[:, (ii - i) * 129:(ii - i + 1) * 129],
                                      Wb[h % 2][:, j, ii * P:(ii + 1) * P], Vaug[:, j, h, :],
                                      start=(j == 0), stop=(j == ii))
                    last.then_inc(fsem("ml_h", n), 1)
                    n += 1
                ada_part(1, h + 1)
            for h in range(MH):
                wait_bank(pe, "ml_t", h)
                pe.wait_ge(S["hm_ready"], 1)
                for t in range(NT):
                    last = tr(bank("ml_t", h)[:, t * P:(t + 1) * P], hmx[:, t, h, :], ident[:, :])
                last.then_inc(fsem("ml_t", h), 1)

            def out_proj(stage, kind):
                for c in range(4):
                    wait_chunk(pe, kind, 0, c)
                    for j in range(2):
                        i = 2 * c + j
                        wait_bank(pe, stage, i)
                        for k in range(KD):
                            last = mm(bank(stage, i)[:, :], chunk(kind, 0, c)[:, k, j * P:(j + 1) * P],
                                      mixT[:, k, :], start=(k == 0), stop=(k == KD - 1))
                        last.then_inc(fsem(stage, i), 1)
                    if stage == "aout" and c % 2:
                        ada_part(2, c // 2)

            ada_part(1, 5)
            pe.wait_ge(S["mixh_ready"], MH)
            pe.wait_ge(S["mix_ready"], 4)
            out_proj("aout", "aout")

            def slot_list(l, e, b, col):
                pe.wait_ge(S["g_part"], NI2 * l + e + 1)
                for t in range(NT):
                    last = mm(b[:, col:col + 2], Gm[:, e % 2, t, :], vt[:, t, e, :], start=(t == 0), stop=(t == NT - 1))
                return last

            def route(l):
                pe.wait_ge(S["wr_in"], 16 * 6)
                pe.wait_ge(S["h_ready"], KD * (2 * l + 2))
                for i in range(KD):
                    wait_bank(pe, f"hx{l}", i)
                    t, half = i // 2, i % 2
                    for j in range(4):
                        last = tr(bank(f"hx{l}", i)[:, j * P:(j + 1) * P], hT[:, 4 * half + j, t * P:(t + 1) * P], ident[:, :])
                    last.then_inc(fsem(f"hx{l}", i), 1)
                wait_bank(pe, f"route{l}")
                for t in range(NT):
                    for k in range(KD):
                        last = mm(bank(f"route{l}")[:, 20 * t:20 * t + 20], hT[:, k, t * P:(t + 1) * P], wr[:, l, k, :],
                                  start=(k == 0), stop=(k == KD - 1))
                last.then_inc(fsem(f"route{l}"), 1)
                wait_bank(pe, f"pos{l}")
                pe.wait_ge(S["mask_ready"], l + 1)
                for t in range(NT):
                    for tt in range(t + 1):
                        last = mm(bank(f"pos{l}")[:, NE * t:NE * t + NE], cmask[:, :] if tt == t else ones[:, :],
                                  rt[:, 256 + NE * tt:256 + NE * tt + NE], start=(tt == 0), stop=(tt == t))
                for t in range(NT):
                    last = mm(bank(f"pos{l}")[:, NE * NT:NE * NT + NE], ones[:, :], rt[:, 256 + NE * t:256 + NE * t + NE],
                              start=(t == 0), stop=(t == NT - 1))
                last.then_inc(fsem(f"pos{l}"), 1)
                for e in range(NPRE):
                    if e % 4 == 0:
                        wait_bank(pe, f"idx{l}", e // 4)
                    slot_list(l, e, bank(f"idx{l}", e // 4), 2 * (e % 4)).then_inc(
                        S["g_used"] if e % 4 < 3 else fsem(f"idx{l}", e // 4), 1)
                if l == 0:
                    for q in (3, 4, 5):
                        ada_part(2, q)

            def moe(l):
                stg = f"moe{l}"
                for kind, e in MOE_ORDER:
                    i = MT[(kind, e)]
                    wait_bank(pe, stg, i)
                    b = bank(stg, i)
                    if kind == "i":
                        first = NPRE + 2 * e
                        last = slot_list(l, first, b, 0)
                        if first + 1 < NI2:
                            last.then_inc(S["g_used"], 1)
                            last = slot_list(l, first + 1, b, 2)
                    elif kind in ("x0", "x1"):
                        half = int(kind[1])
                        if half == 0:
                            pe.wait_ge(xg_in[e % 4], 16 * (len(range(e % 4, NI2, 4)) * l + e // 4 + 1))
                        for j in range(4):
                            last = tr(b[:, j * P:(j + 1) * P], xg[:, e % 4, 4 * half + j:D:KD], ident[:, :])
                    elif kind == "gu":
                        pe.wait_ge(S["xt_ready"], 2 * (NI2 * l + e) + 2)
                        for n, w in enumerate(("eg", "eu")):
                            wait_chunk(pe, w, l, e)
                            for k in range(KD):
                                last = mm(b[:, CC * n:CC * n + CC], xgT[:, e % 2, k, :], chunk(w, l, e)[:, k, :],
                                          start=(k == 0), stop=(k == KD - 1))
                    elif kind == "ht":
                        pe.wait_ge(S["hid_ready"], NI2 * l + e + 1)
                        for f in range(2):
                            last = tr(b[:, f * P:(f + 1) * P], hid[:, e % 2, f * P:(f + 1) * P], ident[:, :])
                    else:
                        half = int(kind[1])
                        pe.wait_ge(S["ht_ready"], NI2 * l + e + 1)
                        wait_chunk(pe, "ed", l, e)
                        w = chunk("ed", l, e).rearrange("p k c -> p (k c)").rearrange("p (k c) -> p k c", c=D)
                        for f in range(2):
                            last = mm(b[:, :], hidT[:, e % 2, f, :], w[:, f, T * half:T * half + T], start=(f == 0), stop=(f == 1))
                    last.then_inc(fsem(stg, i), 1)
                pe.wait_ge(S["yt_ready"], NT * (l + 1))
                for j in range(KD):
                    wait_bank(pe, f"yt{l}", j)
                    for t in range(NT):
                        last = tr(bank(f"yt{l}", j)[:, t * P:(t + 1) * P], ya[:, 0, t, j * P:(j + 1) * P], ident[:, :])
                    last.then_inc(fsem(f"yt{l}", j), 1)

            norm(1)
            ada_part(2, 2)
            route(0)
            moe(0)
            norm(2)
            pe.wait_ge(S["h_ready"], KD * 3)
            ch_proj("nq", "nin", 0, (0, 1, 2, 3))
            ch_proj("nkc", "nin", 0, (4, 5))
            ch_proj("nks", "nin", 0, (6,))
            tok_proj("nvs", "nin", 0, (7,), lambda k, t: hT[:, k, t * P:(t + 1) * P])
            ch_proj("nkw", "nin", 0, (8,))
            tok_proj("nvw", "nin", 0, (9,), lambda k, t: hT[:, k, t * P:(t + 1) * P])
            wait_bank(pe, "ngate")
            pe.wait_ge(S["nsa_in"], NSA_IN)
            for t in range(NT):
                for k in range(KD):
                    last = mm(bank("ngate")[:, 48 * t:48 * t + 48], hT[:, k, t * P:(t + 1) * P], wng[:, k, :],
                              start=(k == 0), stop=(k == KD - 1))
            last.then_inc(fsem("ngate"), 1)
            for i in range(2):
                wait_bank(pe, "fvec", i)
                if i == 0:
                    pe.wait_ge(S["oh_in"], 16)
                mm(bank("fvec", i)[0:NH, :], tab[:, :], oh[:, T * i:T * i + T], start=True,
                   stop=True).then_inc(fsem("fvec", i), 1)
            for j in range(2):
                for f in range(2):
                    wait_bank(pe, "cpos", 2 * j + f)
                pe.wait_ge(S["kc_ready"], 8 * (j + 1))
                for c in range(2):
                    wait_chunk(pe, "cw", j, c)
                    w = chunk("cw", j, c)
                    for f in range(2):
                        if c == 0:
                            wait_bank(pe, "chid", 2 * j + f)
                        for k in range(8):
                            lp = 8 * c + k
                            wf = w[:, k, f * P:(f + 1) * P]
                            first, stop = lp == 0, lp == 15
                            a1 = mm(bank("chid", 2 * j + f)[:, 0:NKV * NCMP], wf,
                                    dims(kc2[:, j, 0, :], [T + 1, NKV], [CS, NCMP], off=2 * lp), start=first, stop=stop)
                            a2 = mm(bank("cpos", 2 * j + f)[:, 0:1], wf, par[:, 96 + 16 * j + lp:97 + 16 * j + lp],
                                    start=first, stop=stop)
                        if c == 1 and f == 0:
                            a1.then_inc(fsem("chid", 2 * j), 1)
                            a2.then_inc(fsem("cpos", 2 * j), 1)
                        elif c == 1:
                            a1.then_inc(fsem("chid", 2 * j + 1), 1)
                            a2.then_inc(fsem("cpos", 2 * j + 1), 1)
                        elif f == 1:
                            a2.then_inc(S["cw_used"], 1)
                mm(bank("cpos", 2 * j + 1)[:, 8:9], ones[:, :], par[:, 0:1], start=True, stop=True).then_inc(S["cw_used"], 1)
            wait_bank(pe, "kcmp")
            pe.wait_ge(S["chid_ready"], 4)
            for f in range(2):
                last = mm(bank("kcmp")[:, 0:P], w2k[:, f, :], chid[:, 0, f, :, :].rearrange("p a b -> p (a b)"), start=(f == 0), stop=(f == 1))
            last.then_inc(fsem("kcmp"), 1)
            wait_bank(pe, "vcmp")
            for g in range(NKV):
                for r in range(R):
                    for f in range(2):
                        last = mm(bank("vcmp")[32 * r:32 * r + 32, DH * g:DH * g + DH], chid[:, 1, f, g, :], w2v[:, f, :],
                                  start=(f == 0), stop=(f == 1))
            last.then_inc(fsem("vcmp"), 1)
            pe.wait_ge(S["q_ready"], KD)
            pe.wait_ge(S["kcmp_ready"], 1)
            for i in range(NT):
                for odd in range(2):
                    wait_bank(pe, "cmpa", 5 * i + odd)
                    for h in range(odd, NH, 2):
                        lo = 64 * odd
                        last = mm(bank("cmpa", 5 * i + odd)[:, 16 * (h - odd):16 * (h - odd) + 32],
                                  qT[lo:lo + 64, h // 2, i * P:(i + 1) * P], kcT[lo:lo + 64, h // R, :], start=True, stop=True)
                    last.then_inc(fsem("cmpa", 5 * i + odd), 1)
                wait_bank(pe, "cmpa", 5 * i + 2)
                pe.wait_ge(S["cp_ready"], i + 1)
                for g in range(NKV):
                    last = tr(bank("cmpa", 5 * i + 2)[:, g * P:(g + 1) * P], Pw[:, i % 4, g * P:(g + 1) * P], ident[:, :])
                last.then_inc(fsem("cmpa", 5 * i + 2), 1)
                pe.wait_ge(S["pct_ready"], i + 1)
                pe.wait_ge(S["vcmp_ready"], 1)
                for s in range(2):
                    wait_bank(pe, "cmpa", 5 * i + 3 + s)
                    for g in (2 * s, 2 * s + 1):
                        last = mm(bank("cmpa", 5 * i + 3 + s)[:, CC * (g % 2):CC * (g % 2) + CC],
                                  PT[:, i % 4, g * P:(g + 1) * P], Vc[:, g, :], start=True, stop=True)
                    last.then_inc(fsem("cmpa", 5 * i + 3 + s), 1)
            pe.wait_ge(S["ktd_ready"], 16)
            pe.wait_ge(S["vn_ready"], 8)
            for kind, n in ATT_ORDER:
                i, h, b = ITEMS[n]
                tile = ATT[(kind, n)]
                if kind == "a":
                    ada(3, (2 * n, 2 * n + 1), "att", tile)
                    continue
                lo, g = 64 * (h % 2), h // R
                wait_bank(pe, "att", tile)
                o = bank("att", tile)
                if kind == "s":
                    last = mm(o[:, 0:(i + 1) * P], qT[lo:lo + 64, h // 2, i * P:(i + 1) * P],
                              kTd[lo:lo + 64, b, g, 0:(i + 1) * P], start=True, stop=True)
                elif kind == "t":
                    pe.wait_ge(S["e_done"], n + 1)
                    for j in range(i + 1):
                        last = tr(o[:, j * P:(j + 1) * P], Pw[:, n % 4, j * P:(j + 1) * P], ident[:, :])
                else:
                    pe.wait_ge(S["pt_ready"], n + 1)
                    for j in range(i + 1):
                        last = mm(o[:, 0:DH], PT[:, n % 4, j * P:(j + 1) * P], vN[:, b, j, DH * g:DH * g + DH],
                                  start=(j == 0), stop=(j == i))
                last.then_inc(fsem("att", tile), 1)
            pe.wait_ge(S["o_ready"], NI)
            for j in range(KD):
                wait_bank(pe, "ot", j)
                for t in range(NT):
                    last = tr(bank("ot", j)[:, t * P:(t + 1) * P], on[:, t, j * P:(j + 1) * P], ident[:, :])
                last.then_inc(fsem("ot", j), 1)
            pe.wait_ge(S["ot_ready"], KD)
            out_proj("nout", "nout")
            norm(3)
            route(1)
            moe(1)
            norm(4)
            for i in range(8):
                wait_bank(pe, "xo", i)
                pe.wait_ge(S["h_part"], KD * 5)
                for j in range(4):
                    last = tr(bank("xo", i)[:, j * P:(j + 1) * P], hT[:, 4 * (i % 2) + j, (i // 2) * P:(i // 2 + 1) * P], ident[:, :])
                last.then_inc(fsem("xo", i), 1)

        @block.scalar
        def _(act):
            AC = nc.scalar.activation
            cnt = [0]

            def link(ins):
                cnt[0] += 1
                ins.then_inc(S["act_chain"], 1)
                act.wait_ge(S["act_chain"], cnt[0])

            d = act.dma_start
            rows = [(0, 96, a["n_cmp_pos"][0].rearrange("j (l s) d -> (j l) (s d)", s=2)), (0, 0, a["ada_b"].rearrange("l k (j p) -> (l k j) p", p=P)),
                    (1, 0, a["c"].rearrange("o (j p) -> (o j) p", p=P)),
                    (1, 8, a["norm_g"].rearrange("l k (j p) -> (l k j) p", p=P)),
                    (1, 40, a["final_g"].rearrange("(j p) -> j p", p=P)),
                    (1, 48, a["a_conv"][0].rearrange("t (j p) -> (t j) p", p=P)),
                    (1, 80, a["n_cmp_b1"][0].rearrange("t (j p) -> (t j) p", p=P)),
                    ]
            act.wait_ge(S["const_ready"], 1)
            for s, r, ap in rows:
                d(raw[r:r + ap.shape[0], s, :], ap).then_inc(S["raw_in"], 16)
            for half in range(2):
                d(raw[84:85, 1, 64 * half:64 * half + 64], a["n_cmp_b2"][0, 0:1, :]).then_inc(S["raw_in"], 16)
                for s, key in enumerate(("s5_lam_re", "s5_lam_im")):
                    d(lrow[:, s, 64 * half:64 * half + 64], a[key][0]).then_inc(S["raw_in"], 16)
                for s in range(2):
                    key = ("s5_c_re", "s5_c_im")[(half + s) % 2]
                    d(crow[:, s, :, 64 * half:64 * half + 64],
                      a[key][0].rearrange("(t g) c p -> (g c) t p", g=8)).then_inc(S["raw_in"], 16)
            assert RAW_IN == 16 * (7 + 2 * 5)
            for half in range(2):
                for s, dst in enumerate((Ba, Bb)):
                    key = ("s5_b_re", "s5_b_im")[(half + s) % 2]
                    d(dst[64 * half:64 * half + 64], a[key][0].rearrange("g p c -> p g c")).then_inc(S["small_in"], 16)
            d(s5s[:, 0, :], a["s5_log_dt"].rearrange("o g -> (o g)").partition_broadcast(P)).then_inc(S["small_in"], 16)
            d(wif[:, :, :], a["a_w_in"][0, :, 2048:2056].rearrange("(k p) c -> p k c", p=P)).then_inc(S["small_in"], 16)
            d(d5[:, :], a["s5_d"][0].rearrange("g c -> c g"), allow_slow_non_contiguous=True).then_inc(S["small_in"], 16)
            d(vecs[0:4, 0:1], a["a_b_i"].rearrange("o h -> h o")).then_inc(S["small_in"], 16)
            d(vecs[0:4, 1:2], a["a_b_f"].rearrange("o h -> h o")).then_inc(S["small_in"], 16)
            for tau in range(TAU):
                d(glub[16 * tau:16 * tau + 16, :], a["s5_glu_b"][0].rearrange("g c -> c g"),
                  allow_slow_non_contiguous=True).then_inc(S["small_in"], 16)
            assert SMALL_IN == 16 * (4 + 5 + TAU)

            for j in range(KD):
                wait_full(act, "x", j)
                AC(xT[:, j, :], bank("x", j)[:, :], ACT.Copy).then_inc(rsem("x", j), 1)
            nc.scalar.nop().then_inc(S["x_ready"], 1)
            act.wait_ge(S["par_ready"], 1)
            AC(small[:, 0:KD], par[:, PB:PB + 8], ACT.Sigmoid).then_inc(S["act_gate"], 1)
            act.wait_ge(S["small_in"], SMALL_IN)
            AC(s5s[:, 1, :], s5s[:, 0, :], ACT.Exp).then_inc(S["act_s5"], 1)
            act.wait_ge(S["dve_s5"], 1)
            AC(ps[:, :, :], pc[:, :, :], ACT.Exp).then_inc(S["act_s5"], 1)
            act.wait_ge(S["dve_s5"], 2)
            AC(F9[:, :, :, 0], F9[:, :, :, 0], ACT.Sin).then_inc(S["act_s5"], 1)
            AC(F9[:, :, :, 1], F9[:, :, :, 1], ACT.Sin).then_inc(S["act_s5"], 1)
            act.wait_ge(S["dve_s5"], 3)
            AC(tws[:, :, :], tws[:, :, :], ACT.Sin).then_inc(S["act_s5"], 1)
            AC(twc[:, :, :], twc[:, :, :], ACT.Sin).then_inc(S["act_s5"], 1)
            for i in range(8):
                wait_full(act, "s5_e", i)
                AC(ET[:, 4 * i:4 * i + 4, :].rearrange("p a b -> p (a b)"), bank("s5_e", i)[:, :],
                   ACT.Copy).then_inc(rsem("s5_e", i), 1)
            nc.scalar.nop().then_inc(S["et_ready"], 8)

            def norm(m):
                if m:
                    act.wait_ge(S["x_upd"], KD * m)
                for k in range(KD):
                    AC(hT[:, k, :], xT[:, k, :], ACT.Square).then_inc(S["sq_ready"], 1)
                act.wait_ge(S["var_ready"], m + 1)
                AC(rstd[:, :], rstd[:, :], ACT.Sqrt).then_inc(S["sqrt_ready"], 1)
                for k in range(KD if m < 4 else 0):
                    act.wait_ge(S["h_part"], KD * m + k + 1)
                    AC(hT[:, k, :], hT[:, k, :], ACT.Identity, bias=mod[:, m, k:k + 1]).then_inc(S["h_ready"], 1)

            norm(0)
            for i in range(4):
                wait_full(act, "u", i)
                AC(Ug[:, 8 * i:8 * i + 8, :].rearrange("p a b -> p (a b)"), bank("u", i)[:, :],
                   ACT.Copy).then_inc(S["ut_ready"], 1)
                act.wait_ge(S["ut_ready"], i + 1)
                nc.scalar.nop().then_inc(rsem("u", i), 1)
            for i in range(4):
                wait_full(act, "ut", i)
                AC(Ug[:, 8 * i:8 * i + 8, :].rearrange("p a b -> p (a b)"), bank("ut", i)[:, :],
                   ACT.Copy).then_inc(rsem("ut", i), 1)
            nc.scalar.nop().then_inc(S["ug_ready"], 4)
            act.wait_ge(S["arg_ready"], 1)
            AC(grow[:, 2, :], grow[:, 2, :], ACT.Exp).then_inc(S["act_gate"], 1)
            act.wait_ge(S["act_gate"], 2)
            AC(grow[:, 2, :], grow[:, 2, :], ACT.Ln, bias=1.0).then_inc(S["act_gate"], 1)
            act.wait_ge(S["arg_ready"], 2)
            AC(grow[:, 1, :], grow[:, 1, :], ACT.Exp).then_inc(S["act_gate"], 1)

            def conv_tile(st, i, n):
                wait_full(act, st, i)
                if n >= 2:
                    act.wait_ge(S["conv_ready"], n - 1)
                AC(cpad[:, n % 2, 3:], bank(st, i)[:, :], ACT.Copy).then_inc(S["cpad_ready"], 1)
                act.wait_ge(S["cpad_ready"], n + 1)
                nc.scalar.nop().then_inc(rsem(st, i), 1)

            def conv_sig(n):
                act.wait_ge(S["conv_ready"], n + 1)
                if n:
                    act.wait_ge(S["qk_ready"], n)
                AC(ct1[:, :], qkT[:, n, :], ACT.Sigmoid).then_inc(S["sig_ready"], 1)

            for n in range(4):
                conv_tile("qk", n, n)
                conv_sig(n)
            for i in range(4):
                wait_full(act, "s5_e1", i)
                AC(ea[:, 8 * i:8 * i + 8, :].rearrange("p a b -> p (a b)"), bank("s5_e1", i)[:, :],
                   ACT.Copy).then_inc(S["ea_ready"], 1)
                act.wait_ge(S["ea_ready"], i + 1)
                nc.scalar.nop().then_inc(rsem("s5_e1", i), 1)
            for n in range(4, 8):
                conv_tile("qk2", n - 4, n)
                conv_sig(n)
            for i in range(4):
                wait_full(act, "s5_y", i)
                AC(za[:, 8 * i:8 * i + 8, :].rearrange("p a b -> p (a b)"), bank("s5_y", i)[:, :],
                   ACT.Gelu_apprx_tanh).then_inc(S["y_ready"], 1)
                act.wait_ge(S["y_ready"], i + 1)
                nc.scalar.nop().then_inc(rsem("s5_y", i), 1)
            act.wait_ge(S["st_ready"], 1)
            for n in range(8):
                wait_full(act, "v", n)
                c, t = n // 4, n % 4
                AC(Vaug[:, t, 2 * c:2 * c + 2, 0:P], bank("v", n)[:, 0:CC].rearrange("p (h d) -> p h d", h=2),
                   ACT.Copy).then_inc(S["v_ready"], 1)
                act.wait_ge(S["v_ready"], n + 1)
                nc.scalar.nop().then_inc(rsem("v", n), 1)
            for i in range(4):
                wait_full(act, "s5_glu", i)
                act.wait_ge(S["rs_ready"], i + 1)
                AC(ea[:, 8 * i:8 * i + 8, :].rearrange("p a b -> p (a b)"),
                   ea[:, 8 * i:8 * i + 8, :].rearrange("p a b -> p (a b)"), ACT.Sigmoid).then_inc(S["act_s5"], 1)
            for n in range(8):
                wait_full(act, "o", n)
                if n == 0:
                    act.wait_ge(S["et_ready"], 8)
                c, t = n // 4, n % 4
                AC(so[:, t, c * CC:(c + 1) * CC], bank("o", n)[:, 0:CC], ACT.Sigmoid).then_inc(S["so_ready"], 1)
                act.wait_ge(S["so_ready"], n + 1)
                nc.scalar.nop().then_inc(rsem("o", n), 1)
            for i in range(4):
                wait_full(act, "ml_h", i)
                AC(mixT[:, 4 + i, :].rearrange("p (k t) -> p t k", t=TAU), bank("ml_h", i)[:, :].rearrange("p (t k) -> p t k", t=TAU),
                   ACT.Copy).then_inc(S["mix_ready"], 1)
                act.wait_ge(S["mix_ready"], i + 1)
                nc.scalar.nop().then_inc(rsem("ml_h", i), 1)
            for h in range(MH):
                act.wait_ge(S["arg_ready"], 2 + h + 1)
                AC(Wb[h % 2].rearrange("p a b -> p (a b)"), Wb[h % 2].rearrange("p a b -> p (a b)"),
                   ACT.Exp).then_inc(S["dexp_ready"], 1)
            act.wait_ge(S["diag_ready"], 1)
            AC(small[:, 64:80], small[:, 64:80], ACT.Sqrt).then_inc(S["act_gate"], 1)
            for h in range(MH):
                wait_full(act, "ml_t", h)
                AC(mixT[:, h, :], bank("ml_t", h)[:, :], ACT.Copy).then_inc(S["mixh_ready"], 1)
                act.wait_ge(S["mixh_ready"], h + 1)
                nc.scalar.nop().then_inc(rsem("ml_t", h), 1)

            def evict(st, i, dst, ready, src=None, func=ACT.Copy, **kw):
                wait_full(act, st, i)
                AC(dst, bank(st, i)[:, :] if src is None else src, func, **kw).then_inc(rsem(st, i), 1)
                n = TILE[(st, i)]
                act.wait_ge(free[n % 8], n // 8 + 1)
                nc.scalar.nop().then_inc(ready, 1)

            def moe(l):
                for i in range(KD):
                    wait_full(act, f"hx{l}", i)
                    AC(htok[:, i // 2, T * (i % 2):T * (i % 2) + T], bank(f"hx{l}", i)[:, :], ACT.Copy).then_inc(S["hx_ready"], 1)
                    act.wait_ge(S["hx_ready"], KD * l + i + 1)
                    nc.scalar.nop().then_inc(rsem(f"hx{l}", i), 1)
                    if i % 2:
                        act.dma_start(h_d[(i // 2) * P:(i // 2 + 1) * P, :], htok[:, i // 2, :]).then_inc(S["h_out"], 16)
                act.wait_ge(S["route_e"], l + 1)
                AC(rt[:, 80:160], rt[:, 80:160], ACT.Exp).then_inc(S["route_s"], 1)
                stg = f"moe{l}"
                for kind, e in MOE_ORDER:
                    i = MT[(kind, e)]
                    n = NI2 * l + e
                    if kind == "i":
                        continue
                    if kind in ("x0", "x1"):
                        half = int(kind[1])
                        wait_full(act, stg, i)
                        if e >= 2:
                            wait_full(act, stg, MT[("gu", e - 2)])
                        AC(xgT[:, e % 2, 4 * half:4 * half + 4, :].rearrange("p a b -> p (a b)"), bank(stg, i)[:, :],
                           ACT.Copy).then_inc(S["xt_ready"], 1)
                        act.wait_ge(S["xt_ready"], 2 * n + half + 1)
                        nc.scalar.nop().then_inc(rsem(stg, i), 1)
                    elif kind == "gu":
                        wait_full(act, stg, i)
                        if e >= 2:
                            wait_full(act, stg, MT[("ht", e - 2)])
                        AC(hid[:, e % 2, :], bank(stg, i)[:, 0:CC], ACT.Sigmoid).then_inc(S["esig"], 1)
                    elif kind == "ht":
                        wait_full(act, stg, i)
                        if e >= 2:
                            wait_full(act, stg, MT[("y1", e - 2)])
                        AC(hidT[:, e % 2, :, :].rearrange("p a b -> p (a b)"), bank(stg, i)[:, 0:CC], ACT.Copy).then_inc(S["ht_ready"], 1)
                        act.wait_ge(S["ht_ready"], n + 1)
                        nc.scalar.nop().then_inc(rsem(stg, i), 1)
                    elif kind == "y0":
                        wait_full(act, stg, i)
                        if e >= 2:
                            act.wait_ge(S[f"y_out{e % 2}"], 16 * (len(range(e % 2, NI2, 2)) * l + e // 2))
                        AC(ysb[:, e % 2, 0:T], bank(stg, i)[:, :], ACT.Copy).then_inc(S["y0_ready"], 1)
                        act.wait_ge(S["y0_ready"], n + 1)
                        nc.scalar.nop().then_inc(rsem(stg, i), 1)
                    else:
                        act.wait_ge(S["y1_ready"], n + 1)
                        act.dma_start(y_d[e * P:e * P + P, :], ysb[:, e % 2, :]).then_inc(S[f"y_out{e % 2}"], 16)

            norm(1)
            moe(0)
            norm(2)
            for i in range(8):
                wait_full(act, "nq", i)
                AC(qT[:, i, :], bank("nq", i)[:, :], ACT.Copy, scale=DH ** -0.5).then_inc(S["q_ready"], 1)
                act.wait_ge(S["q_ready"], i + 1)
                nc.scalar.nop().then_inc(rsem("nq", i), 1)
            for j in range(2):
                for half in range(2):
                    i = 2 * j + half
                    wait_full(act, "nkc", i)
                    for gg in range(2):
                        g = 2 * half + gg
                        src = bank("nkc", i)[64 * gg:64 * gg + 64, :]
                        AC(kc2[0:64, j, g, 0:T], src, ACT.Copy).then_inc(S["kc_ready"], 1)
                        AC(kc2[64:128, j, g, 0:T - 1], src[:, 1:T], ACT.Copy).then_inc(S["kc_ready"], 1)
                    act.wait_ge(S["kc_ready"], 4 * i + 4)
                    nc.scalar.nop().then_inc(rsem("nkc", i), 1)
            for b, (st_k, st_v) in enumerate((("nks", "nvs"), ("nkw", "nvw"))):
                for i in range(2):
                    wait_full(act, st_k, i)
                    for gg in range(2):
                        src = bank(st_k, i)[64 * gg:64 * gg + 64, :]
                        for lo in (0, 64):
                            AC(kTd[lo:lo + 64, b, 2 * i + gg, :], src, ACT.Copy).then_inc(S["ktd_ready"], 1)
                    act.wait_ge(S["ktd_ready"], 8 * b + 4 * i + 4)
                    nc.scalar.nop().then_inc(rsem(st_k, i), 1)
                for t in range(NT):
                    wait_full(act, st_v, t)
                    AC(vN[:, b, t, :], bank(st_v, t)[:, 0:CC], ACT.Copy).then_inc(S["vn_ready"], 1)
                    act.wait_ge(S["vn_ready"], 4 * b + t + 1)
                    nc.scalar.nop().then_inc(rsem(st_v, t), 1)
            act.wait_ge(S["ng_ready"], 1)
            AC(gts.rearrange("p a b -> p (a b)"), gts.rearrange("p a b -> p (a b)"), ACT.Sigmoid).then_inc(S["gsig"], 1)
            for j in range(2):
                act.wait_ge(S["cb_ready"], j + 1)
                for f in range(2):
                    wait_full(act, "chid", 2 * j + f)
                    if j == 0 and f == 0:
                        act.wait_ge(S["cpre"], 1)
                    AC(chid[:, j, f, :, 0:NCMP], bank("chid", 2 * j + f)[:, 0:NKV * NCMP].rearrange("p (g n) -> p g n", g=NKV),
                       ACT.Gelu_apprx_tanh, bias=cb[:, j, f:f + 1]).then_inc(S["chid_ready"], 1)
                    act.wait_ge(S["chid_ready"], 2 * j + f + 1)
                    nc.scalar.nop().then_inc(rsem("chid", 2 * j + f), 1)
            act.wait_ge(S["f_out"], 16)
            for i in range(NT):
                act.wait_ge(S["cs_ready"], i + 1)
                AC(Pw[:, i % 4, :], Pw[:, i % 4, :], ACT.Exp).then_inc(S["ce_ready"], 1)
                wait_full(act, "cmpa", 5 * i + 2)
                AC(PT[:, i % 4, :], bank("cmpa", 5 * i + 2)[:, :], ACT.Copy).then_inc(S["pct_ready"], 1)
                act.wait_ge(S["pct_ready"], i + 1)
                nc.scalar.nop().then_inc(rsem("cmpa", 5 * i + 2), 1)
            for n in range(NI + 2):
                if n < NI:
                    w = (ITEMS[n][0] + 1) * P
                    act.wait_ge(S["p_ready"], n + 1)
                    AC(Pw[:, n % 4, 0:w], Pw[:, n % 4, 0:w], ACT.Exp, bias=stat[:, n % 8:n % 8 + 1],
                       accum_out=stat[:, 8 + n % 8:9 + n % 8]).then_inc(S["e_done"], 1)
                if n >= 2:
                    m = n - 2
                    w = (ITEMS[m][0] + 1) * P
                    tile = ATT[("t", m)]
                    wait_full(act, "att", tile)
                    if m >= 4:
                        wait_full(act, "att", ATT[("o", m - 4)])
                    AC(PT[:, m % 4, 0:w], bank("att", tile)[:, 0:w], ACT.Copy).then_inc(S["pt_ready"], 1)
                    act.wait_ge(S["pt_ready"], m + 1)
                    nc.scalar.nop().then_inc(rsem("att", tile), 1)
            for j in range(KD):
                wait_full(act, "ot", j)
                AC(mixT[:, j, :], bank("ot", j)[:, :], ACT.Copy).then_inc(S["ot_ready"], 1)
                act.wait_ge(S["ot_ready"], j + 1)
                nc.scalar.nop().then_inc(rsem("ot", j), 1)
            norm(3)
            moe(1)
            norm(4)
            for i in range(8):
                wait_full(act, "xo", i)
                AC(osb[:, i // 2, (i % 2) * T:(i % 2 + 1) * T], bank("xo", i)[:, :], ACT.Copy).then_inc(S["out_ready"], 1)

        @block.vector
        def _(dve):
            V = nc.vector
            cnt = [0]

            def link(ins):
                cnt[0] += 1
                ins.then_inc(S["dve_chain"], 1)
                dve.wait_ge(S["dve_chain"], cnt[0])

            def signal(s, n=1):
                V.nop().then_inc(s, n)

            wait_full(dve, "param")
            link(V.tensor_copy(par[:, :], bank("param")[:, 0:224]))
            lre, lim = s5s[:, 2, :], s5s[:, 3, :]
            link(V.tensor_copy(s5s[:, 2:4, :].rearrange("p a b -> p (a b)"), bank("param")[:, 224:288]))
            V.nop().then_inc(rsem("param"), 1)
            signal(S["par_ready"])
            wait_full(dve, "ct", 0)
            dve.wait_ge(S["const_ready"], 1)
            link(V.tensor_scalar(Ca.rearrange("p a b -> p (a b)"), bank("ct", 0)[:, :], sgn[:, 0:1], None, ALU.mult))
            signal(rsem("ct", 0))
            wait_full(dve, "ct", 1)
            link(V.tensor_scalar(Cb.rearrange("p a b -> p (a b)"), bank("ct", 1)[:, :], -1.0, None, ALU.mult))
            signal(rsem("ct", 1))
            dve.wait_ge(S["act_gate"], 1)
            link(V.tensor_tensor(sil[:, :], small[:, 0:KD], par[:, PB:PB + 8], ALU.mult))
            signal(S["sil_ready"])
            dve.wait_ge(S["small_in"], SMALL_IN)
            link(V.tensor_scalar(Bb[0:64].rearrange("p a b -> p (a b)"), Bb[0:64].rearrange("p a b -> p (a b)"), -1.0, None, ALU.mult))
            dve.wait_ge(S["act_s5"], 1)
            are, ang = s5s[:, 4, :], s5s[:, 5, :]
            link(V.tensor_tensor(are, lre, s5s[:, 1, :], ALU.mult))
            link(V.tensor_tensor(ang, lim, s5s[:, 1, :], ALU.mult))

            def outer(o, x, n):
                link(V.tensor_tensor(o, dims(x, [1, G5], [0, n]), dims(jj[:, :], [0, G5], [1, n]), ALU.mult))

            def reduce_angle(x, t, c):
                link(V.tensor_scalar(t, x, 1.0 / (2 * PI), MAGIC, ALU.mult, ALU.add))
                link(V.tensor_scalar(t, t, MAGIC, None, ALU.subtract))
                for part in (C1, C2, C3):
                    link(V.tensor_scalar(c, t, -part, None, ALU.mult))
                    link(V.tensor_tensor(x, x, c, ALU.add))
                link(V.tensor_scalar(x, x, 3.1415925, -3.1415925, ALU.min, ALU.max))
                link(V.tensor_scalar(c, x, -1.0, None, ALU.mult))
                link(V.tensor_tensor(c, x, c, ALU.max))
                link(V.tensor_scalar(c, c, -1.0, PI / 2, ALU.mult, ALU.add))

            outer(pc[:, :, :], are, NPW)
            signal(S["dve_s5"])
            sx, cx = F9[:, :, :, 0], F9[:, :, :, 1]
            outer(sx, ang, NPW)
            reduce_angle(sx, pt[:, :, :], cx)
            signal(S["dve_s5"])
            dve.wait_ge(S["act_s5"], 4)
            link(V.tensor_copy(r8[:, :], ps[:, :, TAU]))
            link(V.tensor_tensor(pc[:, :, :], ps[:, :, :], cx, ALU.mult))
            link(V.tensor_tensor(ps[:, :, :], ps[:, :, :], sx, ALU.mult))
            nr, t1, t2, kr, ki, iv = (s5s[:, i, :] for i in range(6, 12))
            link(V.tensor_scalar(nr, pc[:, :, 1], -1.0, None, ALU.add))
            ni = s5s[:, 12, :]
            link(V.tensor_copy(ni, ps[:, :, 1]))
            link(V.tensor_tensor(t1, lre, lre, ALU.mult))
            link(V.tensor_tensor(t2, lim, lim, ALU.mult))
            link(V.tensor_tensor(t1, t1, t2, ALU.add))
            link(V.reciprocal(iv, t1))
            link(V.tensor_tensor(t1, nr, lre, ALU.mult))
            link(V.tensor_tensor(t2, ni, lim, ALU.mult))
            link(V.tensor_tensor(t1, t1, t2, ALU.add))
            link(V.tensor_tensor(kr, t1, iv, ALU.mult))
            link(V.tensor_tensor(t1, ni, lre, ALU.mult))
            link(V.tensor_tensor(t2, nr, lim, ALU.mult))
            link(V.tensor_tensor(t1, t1, t2, ALU.subtract))
            link(V.tensor_tensor(ki, t1, iv, ALU.mult))
            krb, kib = dims(kr, [1, G5], [0, S5C]), dims(ki, [1, G5], [0, S5C])
            tmp = Ea[:, :, 0, :]
            link(V.tensor_tensor(Bba, Ba, krb, ALU.mult))
            link(V.tensor_tensor(tmp, Bb, kib, ALU.mult))
            link(V.tensor_tensor(Bba, Bba, tmp, ALU.add))
            link(V.tensor_tensor(Bbb, Bb, krb, ALU.mult))
            link(V.tensor_tensor(tmp, Ba, kib, ALU.mult))
            link(V.tensor_tensor(Bbb, Bbb, tmp, ALU.subtract))
            pcr = dims(pc[:, 0, :], [NPW, G5], [-1, TAU], [0, S5C], off=TAU - 1)
            psr = dims(ps[:, 0, :], [NPW, G5], [-1, TAU], [0, S5C], off=TAU - 1)
            bA = dims(Bba[:, 0, :], [S5C, G5], [0, TAU], [1, S5C])
            bB = dims(Bbb[:, 0, :], [S5C, G5], [0, TAU], [1, S5C])
            t4 = Mt.rearrange("p g (t c) -> p g t c", t=TAU)
            link(V.tensor_tensor(Ea, pcr, bA, ALU.mult))
            link(V.tensor_tensor(t4, psr, bB, ALU.mult))
            link(V.tensor_tensor(Ea, Ea, t4, ALU.add))
            signal(S["e_ready"])
            cA = dims(Ca[:, 0, :], [S5C, G5], [0, NPW], [1, S5C])
            cB = dims(Cb[:, 0, :], [S5C, G5], [0, NPW], [1, S5C])
            pcf = dims(pc[:, 0, :], [NPW, G5], [1, NPW], [0, S5C])
            psf = dims(ps[:, 0, :], [NPW, G5], [1, NPW], [0, S5C])
            tf = region(12800, [G5, NPW, S5C])
            link(V.tensor_tensor(F9, pcf, cA, ALU.mult))
            link(V.tensor_tensor(tf, psf, cB, ALU.mult))
            link(V.tensor_tensor(F9, F9, tf, ALU.add))
            signal(S["pow_ready"])
            link(V.tensor_scalar(ang, ang, float(TAU), None, ALU.mult))
            outer(tws, ang, NCH)
            reduce_angle(tws, za, twc)
            signal(S["dve_s5"])
            def ada_out(m, lo, n, stage, i=0):
                wait_full(dve, stage, i)
                link(V.tensor_tensor(mod[:, m, lo:lo + n], bank(stage, i)[:, lo:lo + n], par[:, 24 * m + lo:24 * m + lo + n], ALU.add))
                signal(rsem(stage, i))

            def ada_part(m, q):
                ada_out(m, 4 * q, 4, f"ada{m}_{q}")

            ada_out(0, 0, 24, "ada0")
            link(V.memset(Mt, 0.0))
            for i in range(8):
                wait_full(dve, "s5_g", i)
                link(V.tensor_copy(Gk[:, 4 * i:4 * i + 4, :].rearrange("p a b -> p (a b)"), bank("s5_g", i)[0:16, :]))
                signal(rsem("s5_g", i))
            dd = ct1[0:16, :].rearrange("p (g c) -> p g c", g=G5)
            link(V.tensor_tensor(dd, dims(ident[0:16, :], [0, G5], [1, S5C]), dims(d5[:, :], [1, G5], [0, S5C]), ALU.mult))
            link(V.tensor_tensor(Gk[:, :, 0:S5C], Gk[:, :, 0:S5C], dd, ALU.add))
            signal(S["g_ready"])

            def norm(m):
                if m == 4:
                    link(V.tensor_copy(amul[:, :], par[:, PB + 40:PB + 48]))
                else:
                    link(V.scalar_tensor_tensor(out=amul[:, :], in0=mod[:, m, 8:16], scalar=1.0,
                                                in1=par[:, PB + 8 + 8 * m:PB + 16 + 8 * m], op0=ALU.add, op1=ALU.mult))
                st = f"norm{m}"
                wait_full(dve, st)
                link(V.tensor_scalar(rstd[:, :], bank(st)[:, :], 1.0 / D, EPS, ALU.mult, ALU.add))
                signal(rsem(st))
                signal(S["var_ready"])
                dve.wait_ge(S["sqrt_ready"], m + 1)
                link(V.reciprocal(rstd[:, :], rstd[:, :]))
                for k in range(KD):
                    V.scalar_tensor_tensor(out=hT[:, k, :], in0=xT[:, k, :], scalar=amul[:, k:k + 1],
                                           in1=rstd[:, :], op0=ALU.mult, op1=ALU.mult).then_inc(S["h_part"], 1)

            dve.wait_ge(S["x_ready"], 1)
            norm(0)
            dve.wait_ge(S["m_in"], 16 * TAU)
            for n in range(8):
                wait_full(dve, "u2", n)
                g0, q = 8 * (n // 2), 4 * (n % 2)
                link(V.tensor_copy(uk[0:NCH, g0:g0 + 8, q:q + 4, :],
                                   bank("u2", n)[0:NCH, :].rearrange("p (t g c) -> p g t c", t=4, c=S5C)))
                signal(rsem("u2", n))
                signal(S["uk_ready"])
            wait_full(dve, "gates", 0)
            li, lf, sc = (grow[:, i, :] for i in range(3))
            A, E5, nM = li, lf, rstd[0:MH, :]
            link(V.tensor_scalar(li, bank("gates", 0)[0:4, :], vecs[0:4, 0:1], None, ALU.add))
            signal(rsem("gates", 0))
            wait_full(dve, "gates", 1)
            link(V.tensor_scalar(lf, bank("gates", 1)[0:4, :], vecs[0:4, 1:2], None, ALU.add))
            signal(rsem("gates", 1))
            link(V.tensor_scalar(sc, lf, -1.0, None, ALU.mult))
            link(V.tensor_tensor(sc, lf, sc, ALU.min))
            signal(S["arg_ready"])
            dve.wait_ge(S["act_gate"], 3)
            link(V.scalar_tensor_tensor(out=lf, in0=lf, scalar=0.0, in1=sc, op0=ALU.min, op1=ALU.subtract))
            link(V.memset(nM, 1.0))
            link(V.tensor_tensor_scan(sc, nM, lf, 0.0, ALU.mult, ALU.add))
            link(V.tensor_tensor(A, li, sc, ALU.subtract))
            link(V.tensor_tensor_scan(lf, A, A, 0.0, ALU.max, ALU.max))
            link(V.tensor_scalar(nM, lf, -1.0, None, ALU.mult))
            link(V.tensor_tensor(E5, nM, sc, ALU.subtract))
            signal(S["arg_ready"])
            dve.wait_ge(S["act_gate"], 4)
            signal(S["gates_ready"])

            def conv(n):
                dve.wait_ge(S["cpad_ready"], n + 1)
                w = lambda t: par[:, PB + 48 + 8 * t + n:PB + 49 + 8 * t + n]
                o = qkT[:, n, :]
                link(V.tensor_scalar(o, cpad[:, n % 2, 0:T], w(0), None, ALU.mult))
                for t in range(1, 4):
                    i = V.scalar_tensor_tensor(out=o, in0=cpad[:, n % 2, t:t + T], scalar=w(t), in1=o, op0=ALU.mult, op1=ALU.add)
                    link(i)
                signal(S["conv_ready"])
                dve.wait_ge(S["sig_ready"], n + 1)
                link(V.tensor_tensor(o, o, ct1[:, :], ALU.mult))
                signal(S["qk_ready"])

            for n in range(4):
                conv(n)
            f2 = lambda t: t.rearrange("p a b -> p (a b)")
            dve.wait_ge(S["act_s5"], 6)
            for i in range(4):
                wait_full(dve, "s5_eb", i)
                sl = slice(8 * i, 8 * i + 8)
                link(V.tensor_tensor(f2(za[:, sl]), bank("s5_eb", i)[:, :], f2(tws[:, sl]), ALU.mult))
                signal(rsem("s5_eb", i))
                link(V.tensor_tensor(f2(ea[:, sl]), f2(ea[:, sl]), f2(twc[:, sl]), ALU.mult))
                link(V.tensor_tensor(f2(ea[:, sl]), f2(ea[:, sl]), f2(za[:, sl]), ALU.add))
            decay = Ug2 = region(4096, [G5, NCH])
            link(V.tensor_copy(decay, dims(r8[:, :], [1, G5], [0, NCH])))
            link(V.memset(decay[:, :, 0:1], 0.0))
            link(V.tensor_tensor_scan(f2(za), f2(decay), f2(ea), 0.0, ALU.mult, ALU.add))
            signal(S["za_ready"])
            for n in range(4, 8):
                conv(n)
            for i in range(4):
                wait_full(dve, "s5_zb", i)
                sl = slice(8 * i, 8 * i + 8)
                link(V.tensor_tensor(f2(ea[:, sl]), bank("s5_zb", i)[:, :], f2(tws[:, sl]), ALU.mult))
                signal(rsem("s5_zb", i))
                link(V.tensor_tensor(f2(za[:, sl]), f2(za[:, sl]), f2(twc[:, sl]), ALU.mult))
                link(V.tensor_tensor(f2(ea[:, sl]), f2(za[:, sl]), f2(ea[:, sl]), ALU.subtract))
                signal(S["xs_ready"])
            link(V.memset(Vaug[:, :, :, P:P + 1].rearrange("p a b c -> p (a b c)"), 1.0))
            signal(S["st_ready"])
            dve.wait_ge(S["glu_in"], 16 * TAU)
            for i in range(4):
                for q in range(2):
                    link(V.tensor_tensor(gluw[q], dims(gluc[:, 8 * i + 4 * q, :], [S5C, 4], [0, TAU], [1, S5C]),
                                         dims(blk, [0, 4], [1, TAU], [0, S5C]), ALU.mult))
                    signal(S["glu_ready"])
                if i == 0:
                    ada_part(1, 0)
                wait_full(dve, "s5_glu", i)
                for g in range(8 * i, 8 * i + 8):
                    V.tensor_scalar(ea[:, g, :], bank("s5_glu", i)[:, (g % 8) * NCH:(g % 8 + 1) * NCH],
                                    glub[:, g:g + 1], None, ALU.add).then_inc(S["dve_s5"], 1)
                dve.wait_ge(S["dve_s5"], 3 + 8 * i + 8)
                signal(rsem("s5_glu", i))
                signal(S["rs_ready"])
                dve.wait_ge(S["act_s5"], 6 + i + 1)
                sl = slice(8 * i, 8 * i + 8)
                link(V.tensor_tensor(f2(Ug[:, sl]), f2(za[:, sl]), f2(ea[:, sl]), ALU.mult))
                signal(S["ys_ready"])
            for i in range(8):
                st, ii = ("s5_k", i) if i < 4 else ("s5_t", i - 4)
                wait_full(dve, st, ii)
                link(V.tensor_copy(uk2[:, :, 64 * i:64 * i + 64].rearrange("p t (g c) -> p g t c", c=S5C),
                                   bank(st, ii)[0:NCH, :].rearrange("p (g t c) -> p g t c", t=TAU, c=S5C)))
                signal(rsem(st, ii))
                signal(S["sk_ready"])
            wait_full(dve, "gcol")
            link(V.tensor_copy(gcol[:, :, :, :].rearrange("p a b c -> p (a b c)"), bank("gcol")[:, 0:32]))
            signal(rsem("gcol"))
            n = 4
            ssq = small[:, 64:80]
            for h in range(MH):
                wait_full(dve, "ml_h", n)
                if h == 0:
                    wait_full(dve, "ml_h", 3)
                W = Wb[h % 2]
                if h >= 2:
                    wait_full(dve, "ml_h", 4 + 7 * (h - 2) + 6)
                link(V.memset(W, 0.0)) if h < 2 else None
                for j in range(NT):
                    link(V.tensor_scalar(W[:, j, j * P:], bank("ml_h", n)[:, j * P:], gcol[:, 0, j, h:h + 1], 0.0,
                                         ALU.add, ALU.min))
                signal(rsem("ml_h", n))
                signal(S["arg_ready"])
                n += 1
                dve.wait_ge(S["dexp_ready"], h + 1)
                for j in range(NT):
                    wait_full(dve, "ml_h", n)
                    dg = W[:, j, j * P:(j + 1) * P]
                    link(V.tensor_tensor(dg, dg, cmask[:, :], ALU.mult))
                    link(V.scalar_tensor_tensor(out=W[:, j, j * P:], in0=bank("ml_h", n)[:, j * P:], scalar=P ** -0.5,
                                                in1=W[:, j, j * P:], op0=ALU.mult, op1=ALU.mult))
                    signal(rsem("ml_h", n))
                    n += 1
                signal(S["w_ready"])
                for i in range(0, NT, 2):
                    wait_full(dve, "ml_h", n)
                    for ii in range(i, i + 2):
                        b = bank("ml_h", n)[:, (ii - i) * 129:(ii - i + 1) * 129]
                        dn = small[:, 80:81]
                        link(V.tensor_scalar(dn, b[:, P:P + 1], -1.0, None, ALU.mult))
                        link(V.tensor_tensor(dn, dn, b[:, P:P + 1], ALU.max))
                        link(V.tensor_tensor(dn, dn, gcol[:, 1, ii, h:h + 1], ALU.max))
                        link(V.reciprocal(dn, dn))
                        link(V.tensor_scalar(hmx[:, ii, h, :], b[:, 0:P], dn, None, ALU.mult))
                        link(V.scalar_tensor_tensor(out=ct1[:, 0:P], in0=hmx[:, ii, h, :], scalar=1.0,
                                                    in1=hmx[:, ii, h, :], op0=ALU.mult, op1=ALU.mult,
                                                    accum_out=ssq[:, 4 * ii + h:4 * ii + h + 1]))
                    signal(rsem("ml_h", n))
                    n += 1
                ada_part(1, h + 1)
            link(V.tensor_scalar(ssq, ssq, 1.0 / P, EPS, ALU.mult, ALU.add))
            signal(S["diag_ready"])
            dve.wait_ge(S["act_gate"], 5)
            link(V.reciprocal(ssq, ssq))
            dve.wait_ge(S["headg_in"], 16)
            hf = hmx.rearrange("p a b c -> p (a b) c")
            link(V.tensor_tensor(hf, hf, dims(ssq, [1, 16], [0, P]), ALU.mult))
            link(V.tensor_tensor(hmx.rearrange("p a b c -> p a (b c)"), hmx.rearrange("p a b c -> p a (b c)"),
                                 dims(headg[:, :], [0, NT], [1, MA]), ALU.mult))
            dve.wait_ge(S["so_ready"], 8)
            link(V.tensor_tensor(hmx.rearrange("p a b c -> p (a b c)"), hmx.rearrange("p a b c -> p (a b c)"),
                                 so.rearrange("p a b -> p (a b)"), ALU.mult))
            signal(S["hm_ready"])
            ada_part(1, 5)

            def residual(stage, m):
                for j in range(KD):
                    wait_full(dve, stage, j)
                    link(V.scalar_tensor_tensor(out=xT[:, j, :], in0=bank(stage, j)[:, :], scalar=mod[:, m, 16 + j:17 + j],
                                                in1=xT[:, j, :], op0=ALU.mult, op1=ALU.add))
                    signal(rsem(stage, j))
                    signal(S["x_upd"])
                    if stage == "aout" and j % 4 == 3:
                        ada_part(2, j // 4)

            residual("aout", 0)

            def moe(l):
                wait_full(dve, f"route{l}")
                dve.wait_ge(S["wr_in"], 16 * 6)
                lg = rt[:, 0:80].rearrange("p (t e) -> p t e", t=NT)
                ex = rt[:, 80:160].rearrange("p (t e) -> p t e", t=NT)
                link(V.tensor_tensor(lg, bank(f"route{l}")[:, 0:80].rearrange("p (t e) -> p t e", t=NT),
                                     dims(rb[:, l, :], [0, NT], [1, 20]), ALU.add))
                signal(rsem(f"route{l}"))
                gl, el = lg[:, :, 0:NG], lg[:, :, NG:]
                m1 = rt[:, 160:164]
                b4 = lambda x: dims(x, [1, NT], [0, NG])
                b16 = lambda x: dims(x, [1, NT], [0, NE])
                ix = lambda n: dims(jj[:, 0:1], [0, NT], [1, n])
                gate = rt[:, 192:256].rearrange("p (t e) -> p t e", t=NT)
                mk = rt[:, 256:320].rearrange("p (t e) -> p t e", t=NT)
                o1 = rt[:, 320:384].rearrange("p (t e) -> p t e", t=NT)
                o2 = rt[:, 384:448].rearrange("p (t e) -> p t e", t=NT)
                ms = rt[:, 448:512].rearrange("p (t e) -> p t e", t=NT)
                og = ixf.rearrange("p (t e) -> p t e", t=NT)
                mg, v1, v2, wa, wb, pg = (rt[:, 164 + 4 * i:168 + 4 * i] for i in range(6))

                def first_max(o, x, mx, n):
                    bx = dims(mx, [1, NT], [0, n])
                    link(V.tensor_reduce(mx, x, AX.X, ALU.max))
                    link(V.tensor_tensor(o, x, bx, ALU.is_equal))
                    link(V.scalar_tensor_tensor(out=gate[:, :, 0:n], in0=ix(n), scalar=-64.0, in1=o, op0=ALU.add, op1=ALU.mult))
                    link(V.tensor_reduce(m1, gate[:, :, 0:n], AX.X, ALU.min))
                    link(V.tensor_scalar(gate[:, :, 0:n], ix(n), -64.0, None, ALU.add))
                    link(V.tensor_tensor(o, gate[:, :, 0:n], dims(m1, [1, NT], [0, n]), ALU.is_equal))

                first_max(og, gl, mg, NG)
                link(V.tensor_tensor(ex[:, :, 0:NG], gl, b4(mg), ALU.subtract))
                link(V.memset(ex[:, :, NG:], 0.0))
                og16 = dims(og[:, 0, :], [NG, NT], [1, NG], [0, NPG])
                four = lambda x: x.rearrange("p t (g e) -> p t g e", g=NG)
                link(V.tensor_copy(four(o2), og16))
                link(V.tensor_tensor(ms, el, o2, ALU.mult))
                link(V.tensor_scalar(o2, o2, -1.0, 1e30, ALU.add, ALU.mult))
                link(V.tensor_tensor(ms, ms, o2, ALU.add))
                first_max(o1, ms, v1, NE)
                link(V.scalar_tensor_tensor(out=ms, in0=o1, scalar=-2e30, in1=ms, op0=ALU.mult, op1=ALU.add))
                first_max(o2, ms, v2, NE)
                link(V.tensor_tensor(dims(ex[:, 0, :], [20, NT], off=NG), v2, v1, ALU.subtract))
                signal(S["route_e"])
                link(V.tensor_tensor(mk, o1, o2, ALU.add))
                signal(S["mask_ready"])
                dve.wait_ge(S["route_s"], l + 1)
                link(V.tensor_reduce(pg, ex[:, :, 0:NG], AX.X, ALU.add))
                e2 = dims(ex[:, 0, :], [20, NT], off=NG)
                link(V.tensor_scalar(wa, e2, 1.0, None, ALU.add))
                link(V.tensor_tensor(wa, wa, pg, ALU.mult))
                link(V.reciprocal(wa, wa))
                link(V.tensor_tensor(wb, wa, e2, ALU.mult))
                link(V.tensor_tensor(gate, o1, b16(wa), ALU.mult))
                link(V.tensor_tensor(ms, o2, b16(wb), ALU.mult))
                link(V.tensor_tensor(vt[:, :, 0:NE, 1], gate, ms, ALU.add))
                link(V.tensor_copy(vt[:, :, :, 0], dims(tokn[:, :], [1, NT], [0, NI2])))
                wait_full(dve, f"pos{l}")
                ps3 = bank(f"pos{l}")[:, 0:NT * NE].rearrange("p (t e) -> p t e", t=NT)
                pe_ = posx[:, :, 0:NE]
                link(V.tensor_tensor(pe_, ps3, mk, ALU.mult))
                link(V.tensor_scalar(pe_, pe_, -1.0, None, ALU.add))
                tot = bank(f"pos{l}")[:, NE * NT:NE * NT + NE]
                link(V.tensor_scalar(nE, tot, float(P), None, ALU.is_gt))
                for r in (2, 3):
                    link(V.tensor_scalar(Si, tot, float(r * P), None, ALU.is_gt))
                    link(V.tensor_tensor(nE, nE, Si, ALU.add))
                signal(rsem(f"pos{l}"))

                def lists(stage, tile, first, n):
                    wait_full(dve, stage, tile)
                    b = bank(stage, tile)[:, 0:2 * n].rearrange("p (e two) -> p two e", two=2)
                    link(V.tensor_scalar(idx[:, first:first + n], b[:, 0], 4096.0, None, ALU.add))
                    link(V.tensor_copy(gc[:, first:first + n], b[:, 1]))
                    signal(rsem(stage, tile))
                    signal(S["idx_ready"])

                def further():
                    link(V.memset(tmx[:, 0, :], 1.0))
                    link(V.tensor_tensor_scan(Si, tmx[:, 0, :], nE, 0.0, ALU.mult, ALU.add))
                    link(V.tensor_tensor(Sx, Si, nE, ALU.subtract))
                    k7 = dims(jj[:, :], [1, NX], [0, NE])
                    row = lambda x: dims(x, [0, NX], [1, NE])
                    link(V.tensor_tensor(sel, row(Sx), k7, ALU.is_le))
                    link(V.tensor_tensor(tmx, row(Si), k7, ALU.is_gt))
                    link(V.tensor_tensor(sel, sel, tmx, ALU.mult))
                    link(V.tensor_tensor(tmx, sel, row(jj[:, 0:NE]), ALU.mult))
                    link(V.tensor_reduce(xkf, tmx, AX.X, ALU.add))
                    link(V.tensor_copy(xk, xkf))
                    signal(S["xk_ready"])
                    link(V.tensor_tensor(tmx, sel, row(Sx), ALU.mult))
                    link(V.tensor_reduce(bk, tmx, AX.X, ALU.add))
                    link(V.tensor_tensor(bk, jj[:, 0:NX], bk, ALU.subtract))
                    link(V.tensor_scalar(bk, bk, 1.0, float(P), ALU.add, ALU.mult))
                    link(V.tensor_reduce(ck, sel, AX.X, ALU.add))
                    link(V.tensor_scalar(ck, ck, -1.0, -8192.0, ALU.add, ALU.mult))
                    link(V.tensor_tensor(bk, bk, ck, ALU.add))
                    for k in range(NX):
                        sk = dims(sel[:, k, :], [0, NT], [1, NE])
                        link(V.tensor_tensor(tmp64, posx[:, :, 0:NE], sk, ALU.mult))
                        link(V.tensor_reduce(posx[:, :, NE + k], tmp64, AX.X, ALU.add))
                        link(V.tensor_tensor(tmp64, vt[:, :, 0:NE, 1], sk, ALU.mult))
                        link(V.tensor_reduce(vt[:, :, NE + k, 1], tmp64, AX.X, ALU.add))
                    link(V.tensor_tensor(posx[:, :, NE:], posx[:, :, NE:], dims(bk, [0, NT], [1, NX]), ALU.subtract))

                def one_hot(e):
                    if e == NE:
                        further()
                    q = e - 2
                    if q >= NPRE and (q - NPRE) % 2:
                        wait_full(dve, f"moe{l}", MT[("i", (q - NPRE) // 2)])
                    elif q >= NPRE:
                        dve.wait_ge(S["g_used"], G_USED * l + NPRE - NPRE // 4 + (q - NPRE) // 2 + 1)
                    elif q >= 0 and q % 4 == 3:
                        wait_full(dve, f"idx{l}", q // 4)
                    elif q >= 0:
                        dve.wait_ge(S["g_used"], G_USED * l + 3 * (q // 4) + q % 4 + 1)
                    link(V.tensor_tensor(Gm[:, e % 2, :, :], dims(posx[:, 0, e:e + 1], [NI2, NT], [0, P]),
                                         dims(jj[:, :], [0, NT], [1, P]), ALU.is_equal))
                    signal(S["g_part"])

                def result_rows():
                    b3 = lambda x: dims(x, [0, NT], [1, NE])
                    link(V.tensor_tensor(nE, Sx, jj[:, 0:NE], ALU.subtract))
                    link(V.tensor_scalar(nE, nE, float(NE - 1), None, ALU.add))
                    link(V.tensor_scalar(tmp64, posx[:, :, 0:NE], float(P), None, ALU.is_ge))
                    link(V.tensor_tensor(tmp64, tmp64, b3(nE), ALU.mult))
                    link(V.tensor_tensor(tmp64, tmp64, b3(jj[:, 0:NE]), ALU.add))
                    link(V.tensor_scalar(tmp64, tmp64, float(P), None, ALU.mult))
                    link(V.tensor_tensor(tmp64, tmp64, posx[:, :, 0:NE], ALU.add))
                    for k, o in enumerate((o1, o2)):
                        link(V.tensor_tensor(ms, tmp64, o, ALU.mult))
                        link(V.tensor_reduce(ixf[:, 4 * k:4 * k + 4], ms, AX.X, ALU.add))
                    link(V.tensor_copy(idx2, ixf[:, 0:8]))
                    signal(S["row_ready"])

                for e in range(NPRE + 2):
                    one_hot(e)
                    if e % 4 == 1 and e > 4:
                        lists(f"idx{l}", e // 4 - 1, 4 * (e // 4 - 1), 4)
                if l == 0:
                    for q in (3, 4, 5):
                        ada_part(2, q)
                stg = f"moe{l}"
                for kind, e in MOE_ORDER:
                    i = MT[(kind, e)]
                    if kind == "i":
                        first = NPRE + 2 * e
                        lists(stg, i, first, min(2, NI2 - first))
                        for ee in range(first + 2, min(first + 4, NI2)):
                            one_hot(ee)
                        if e == PAIRS - 1:
                            result_rows()
                    elif kind == "gu":
                        dve.wait_ge(S["esig"], NI2 * l + e + 1)
                        h = hid[:, e % 2, :]
                        link(V.scalar_tensor_tensor(out=h, in0=bank(stg, i)[:, 0:CC], scalar=gc[:, e:e + 1], in1=h,
                                                    op0=ALU.mult, op1=ALU.mult))
                        link(V.tensor_tensor(h, bank(stg, i)[:, CC:2 * CC], h, ALU.mult))
                        signal(rsem(stg, i))
                        signal(S["hid_ready"])
                    elif kind == "y1":
                        wait_full(dve, stg, i)
                        if e >= 2:
                            dve.wait_ge(S[f"y_out{e % 2}"], 16 * (len(range(e % 2, NI2, 2)) * l + e // 2))
                        dve.wait_ge(S["y0_ready"], NI2 * l + e + 1)
                        link(V.tensor_copy(ysb[:, e % 2, T:D], bank(stg, i)[:, :]))
                        signal(rsem(stg, i))
                        signal(S["y1_ready"])
                for t in range(NT):
                    dve.wait_ge(S[f"ya_in{t}"], 32 * (l + 1))
                    link(V.tensor_tensor(ya[:, 0, t, :], ya[:, 0, t, :], ya[:, 1, t, :], ALU.add))
                    signal(S["yt_ready"])
                m = 2 * l + 1
                for j in range(KD):
                    wait_full(dve, f"yt{l}", j)
                    link(V.scalar_tensor_tensor(out=xT[:, j, :], in0=bank(f"yt{l}", j)[:, :], scalar=mod[:, m, 16 + j:17 + j],
                                                in1=xT[:, j, :], op0=ALU.mult, op1=ALU.add))
                    signal(rsem(f"yt{l}", j))
                    signal(S["x_upd"])

            norm(1)
            ada_part(2, 2)
            moe(0)
            norm(2)
            link(V.memset(chid.rearrange("p a b c d -> p (a b c d)"), 0.0))
            signal(S["cpre"])
            link(V.memset(Vc.rearrange("p a b -> p (a b)"), 0.0))
            link(V.memset(biasC.rearrange("p a b c -> p (a b c)"), NEG))
            wait_full(dve, "ngate")
            dve.wait_ge(S["nsa_in"], NSA_IN)
            link(V.tensor_tensor(gts, bank("ngate")[:, 0:192].rearrange("p (t e) -> p t e", t=NT),
                                 dims(bng[:, :], [0, NT], [1, 48]), ALU.add))
            signal(rsem("ngate"))
            signal(S["ng_ready"])
            for i in range(2):
                wait_full(dve, "fvec", i)
                link(V.tensor_copy(frs[:, T * (1 - i):T * (1 - i) + T], dims(bank("fvec", i)[0:NH, :], [-1, T], off=T - 1)))
                signal(rsem("fvec", i))
            signal(S["f_ready"])
            for j in range(2):
                for f in range(2):
                    wait_full(dve, "cpos", 2 * j + f)
                    if f:
                        dve.wait_ge(S["cw_used"], 2 * j + 2)
                    link(V.tensor_tensor(cb[:, j, f:f + 1], bank("cpos", 2 * j + f)[:, 0:1],
                                         par[:, PB + 80 + 2 * j + f:PB + 81 + 2 * j + f], ALU.add))
                    signal(rsem("cpos", 2 * j + f))
                signal(S["cb_ready"])
            wait_full(dve, "kcmp")
            link(V.tensor_scalar(kcT.rearrange("p a b -> p (a b)"), bank("kcmp")[:, 0:P], par[:, PB + 84:PB + 85], None, ALU.add))
            signal(rsem("kcmp"))
            signal(S["kcmp_ready"])
            wait_full(dve, "vcmp")
            for r in range(R):
                sl = slice(32 * r, 32 * r + 32)
                link(V.tensor_tensor(Vc[sl, :, DH * r:DH * r + DH], bank("vcmp")[sl, 0:CC].rearrange("p (g d) -> p g d", g=NKV),
                                     dims(b2v[sl, :], [0, NKV], [1, DH]), ALU.add))
            signal(rsem("vcmp"))
            signal(S["vcmp_ready"])
            dve.wait_ge(S["gsig"], 1)
            dve.wait_ge(S["bias_in"], 16 * P // REP)
            for i in range(NT):
                x0 = T - P * (i + 1) + CL - 1
                count = min(NCMP, (T - 1 - x0) // CS + 1)
                link(V.tensor_copy(biasC[:, i, :, 0:count], biasT[:, :, x0:x0 + CS * (count - 1) + 1:CS]))
            for i in range(NT):
                p = Pw[:, i % 4, :]
                p3 = p.rearrange("p (h n) -> p h n", h=NH)
                mx, sm = stat[:, 16:32], stat[:, 32:48]
                for odd in range(2):
                    wait_full(dve, "cmpa", 5 * i + odd)
                    link(V.tensor_tensor(p3.rearrange("p (a two) n -> p two a n", two=2)[:, odd],
                                         bank("cmpa", 5 * i + odd)[:, 0:256].rearrange("p (a n) -> p a n", n=32),
                                         biasC[:, i, :, :].rearrange("p (a two) n -> p two a n", two=2)[:, odd], ALU.add))
                    signal(rsem("cmpa", 5 * i + odd))
                link(V.tensor_reduce(mx, p3, AX.X, ALU.max))
                link(V.tensor_tensor(p3, p3, dims(mx, [1, NH], [0, 32]), ALU.subtract))
                signal(S["cs_ready"])
                dve.wait_ge(S["ce_ready"], i + 1)
                link(V.tensor_reduce(sm, p3, AX.X, ALU.add))
                link(V.reciprocal(sm, sm))
                link(V.tensor_tensor(sm, sm, dims(gts[:, i, :], [3, NH]), ALU.mult))
                if i == 0:
                    link(V.memset(sm[0:CL - 1, :], 0.0))
                link(V.tensor_tensor(p3, p3, dims(sm, [1, NH], [0, 32]), ALU.mult))
                signal(S["cp_ready"])
                for s in range(2):
                    wait_full(dve, "cmpa", 5 * i + 3 + s)
                    link(V.tensor_copy(on[:, i, T * s:T * s + T], bank("cmpa", 5 * i + 3 + s)[:, :]))
                    signal(rsem("cmpa", 5 * i + 3 + s))
            for n in range(NI + 3):
                if n < NI:
                    i, h, b = ITEMS[n]
                    w = (i + 1) * P
                    tile = ATT[("s", n)]
                    wait_full(dve, "att", tile)
                    if n >= 4:
                        wait_full(dve, "att", ATT[("t", n - 4)])
                    link(V.tensor_tensor_reduce(Pw[:, n % 4, 0:w], bank("att", tile)[:, 0:w], biasT[:, h, T - w:T], 1.0, NEG * 10,
                                                ALU.add, ALU.max, stat[:, 48:49]))
                    signal(rsem("att", tile))
                    link(V.tensor_scalar(stat[:, n % 8:n % 8 + 1], stat[:, 48:49], -1.0, None, ALU.mult))
                    signal(S["p_ready"])
                if n >= 3:
                    m = n - 3
                    i, h, b = ITEMS[m]
                    tile = ATT[("o", m)]
                    sc = stat[:, 50:51]
                    dve.wait_ge(S["e_done"], m + 1)
                    link(V.reciprocal(sc, stat[:, 8 + m % 8:9 + m % 8]))
                    link(V.tensor_tensor(sc, sc, gts[:, i, 3 * h + 1 + b:3 * h + 2 + b], ALU.mult))
                    wait_full(dve, "att", tile)
                    o = on[:, i, DH * h:DH * h + DH]
                    link(V.scalar_tensor_tensor(out=o, in0=bank("att", tile)[:, 0:DH], scalar=sc, in1=o, op0=ALU.mult, op1=ALU.add))
                    signal(rsem("att", tile))
                    signal(S["o_ready"])
                if n in ADA_AT:
                    q = ADA_AT[n]
                    ada_out(3, 4 * q, 4, "att", ATT[("a", q)])
            residual("nout", 2)
            norm(3)
            moe(1)
            norm(4)

        @block.gpsimd
        def _(pool):
            G = nc.gpsimd
            cnt = [0]

            def link(ins):
                cnt[0] += 1
                ins.then_inc(S["pool_chain"], 1)
                pool.wait_ge(S["pool_chain"], cnt[0])

            link(G.memset(ident[:, :], 0.0))
            link(G.affine_select(out=ident[:, :], in_=ident[:, :], compare_op=ALU.not_equal, fill=1.0, base=0,
                                 pattern=[[-1, P]], channel_multiplier=1))
            link(G.memset(ones[:, :], 1.0))
            link(G.memset(raw[:, :, :], 0.0))
            link(G.memset(cpad[:, :, 0:3], 0.0))
            link(G.memset(sgn[0:64, :], 1.0))
            link(G.memset(sgn[64:128, :], -1.0))
            link(G.memset(cmask[:, :], 1.0))
            link(G.affine_select(out=cmask[:, :], in_=cmask[:, :], compare_op=ALU.is_ge, fill=0.0, base=0,
                                 pattern=[[1, P]], channel_multiplier=-1))
            link(G.memset(perm[:, :], 0.0))
            link(G.affine_select(out=perm[:, :], in_=perm[:, :], compare_op=ALU.not_equal, fill=1.0, base=-64,
                                 pattern=[[-1, P]], channel_multiplier=1))
            link(G.affine_select(out=perm[:, :], in_=perm[:, :], compare_op=ALU.not_equal, fill=-1.0, base=64,
                                 pattern=[[-1, P]], channel_multiplier=1))
            link(G.iota(tokn[:, :], pattern=[[P, NT]], base=-4096, channel_multiplier=1,
                        allow_small_or_imprecise_dtypes=True))
            link(G.iota(jj[:, :], pattern=[[1, P]], base=0, channel_multiplier=0,
                        allow_small_or_imprecise_dtypes=True))
            G.nop().then_inc(S["const_ready"], 1)
            pool.wait_ge(S["g_ready"], 1)
            for tau in range(TAU):
                pool.dma_start(Mt[16 * tau:16 * tau + 16, :, 16 * tau:P], Gk[:, :, 0:P - 16 * tau]).then_inc(S["m_in"], 16)
            pool.wait_ge(S["st_ready"], 1)
            link(G.memset(blk, 1.0))
            link(G.affine_select(out=blk, in_=blk, compare_op=ALU.is_ge, fill=0.0, base=0,
                                 pattern=[[-S5C, TAU]], channel_multiplier=1))
            link(G.affine_select(out=blk, in_=blk, compare_op=ALU.is_ge, fill=0.0, base=S5C - 1,
                                 pattern=[[S5C, TAU]], channel_multiplier=-1))
            for tau in range(TAU):
                pool.dma_start(gluc[S5C * tau:S5C * tau + S5C, :, :],
                               a["s5_glu_w"][0].rearrange("g c e -> c g e")).then_inc(S["glu_in"], 16)
            pool.dma_start(headg[:, :], a["a_head_g"].rearrange("o g -> (o g)").partition_broadcast(P)).then_inc(S["headg_in"], 16)
            for l in range(2):
                pool.dma_start(wr[:, l, :, 0:NG], a["r_grp_w"][l].rearrange("(k p) g -> p k g", p=P)).then_inc(S["wr_in"], 16)
                pool.dma_start(wr[:, l, :, NG:], a["r_exp_w"][l].rearrange("(k p) g e -> p k (g e)", p=P)).then_inc(S["wr_in"], 16)
            pool.dma_start(rb[:, :, 0:NG], a["r_grp_b"].partition_broadcast(P)).then_inc(S["wr_in"], 16)
            pool.dma_start(rb[:, :, NG:], a["r_exp_b"].rearrange("l g e -> l (g e)").partition_broadcast(P)).then_inc(S["wr_in"], 16)
            def ada_sums(m):
                pool.wait_ge(S["sil_ready"], 1)
                for c in range(12):
                    wait_chunk(pool, "ada", m, c)
                    w = chunk("ada", m, c)
                    link(G.tensor_tensor(w, w, dims(sil[:, :], [1, KD], [0, CC]), ALU.mult))
                    k = KD // 2
                    while k:
                        link(G.tensor_tensor(w[:, 0:k, :], w[:, 0:k, :], w[:, k:2 * k, :], ALU.add))
                        k //= 2
                    G.nop().then_inc(S["ada_sum"], 1)

            ada_sums(1)
            ada_sums(2)
            def gathers(l):
                link(G.memset(xg.rearrange("p a b -> p (a b)"), 0.0))
                pool.wait_ge(S["h_out"], 16 * NT * (l + 1))
                for e in range(NI2):
                    pool.wait_ge(S["idx_ready"], LISTS * l + (e // 4 + 1 if e < NPRE else NPRE // 4 + (e - NPRE) // 2 + 1))
                    if e >= 4:
                        wait_full(pool, f"moe{l}", MT[("x1", e - 4)])
                    pool.indirect_dma_start(out=xg[:, e % 4, :], out_offset=None, in_=h_d,
                                            in_offset=bass.IndirectOffsetOnAxis(ap=idx[:, e:e + 1], axis=0),
                                            bounds_check=T - 1, oob_is_err=False).then_inc(xg_in[e % 4], 16)
                pool.wait_ge(S["row_ready"], l + 1)
                wait_full(pool, f"moe{l}", MT[("y1", NI2 - 1)])
                for i in range(2):
                    pool.wait_ge(S[f"y_out{i}"], 16 * len(range(i, NI2, 2)) * (l + 1))
                for t in range(NT):
                    for k in range(2):
                        pool.indirect_dma_start(out=ya[:, k, t, :], out_offset=None, in_=y_d,
                                                in_offset=bass.IndirectOffsetOnAxis(ap=idx2[:, 4 * k + t:4 * k + t + 1], axis=0),
                                                bounds_check=NI2 * P - 1, oob_is_err=False).then_inc(S[f"ya_in{t}"], 16)

            pool.wait_ge(S["x_upd"], KD)
            gathers(0)
            pool.dma_start(wng[:, :, :], a["n_w_in"][0, :, 2560:2608].rearrange("(k p) c -> p k c", p=P)).then_inc(S["nsa_in"], 16)
            for half in range(2):
                pool.dma_start(w2k[:, :, 64 * half:64 * half + 64],
                               a["n_cmp_w2"][0, 0].rearrange("(f p) d -> p f d", p=P)).then_inc(S["nsa_in"], 16)
            pool.dma_start(w2v[:, :, :], a["n_cmp_w2"][0, 1].rearrange("(f p) d -> p f d", p=P)).then_inc(S["nsa_in"], 16)
            pool.dma_start(b2v[:, :], a["n_cmp_b2"][0, 1].partition_broadcast(P)).then_inc(S["nsa_in"], 16)
            pool.dma_start(bng[:, :], a["n_b_gate"][0].partition_broadcast(P)).then_inc(S["nsa_in"], 16)
            link(G.memset(tab[32:33, :], NEG))
            pool.dma_start(tab[0:32, :], a["rel_bias"]).then_inc(S["nsa_in"], 16)
            pool.wait_ge(S["nsa_in"], NSA_IN)
            pool.dma_start(oh[:, :], onehot).then_inc(S["oh_in"], 16)
            pool.wait_ge(S["f_ready"], 1)
            pool.dma_start(bias_d, dims(frs[:, 0:1], [0, REP], [1, 1024])).then_inc(S["f_out"], 16)
            pool.wait_ge(S["f_out"], 16)
            pool.wait_ge(S["x_upd"], 2 * KD)
            for p in range(0, P, REP):
                pool.dma_start(biasT[p:p + REP, :, :],
                               bass.AP(tensor=bias_d.tensor, offset=bias_d.offset + P - 1 - p,
                                       ap=[[1023, REP], [REP * 1024, NH], [1, T]])).then_inc(S["bias_in"], 16)
            ada_sums(3)
            wait_full(pool, "ot", KD - 1)
            gathers(1)


NSA_IN = 16 * 7
RAW_IN = 16 * 17
SMALL_IN = 16 * 17


def bucket_rows():
    dist = np.arange(2 * T) - T
    exact = BUCKETS // 2
    ratio = np.log(np.maximum(dist, 1).astype(np.float32) / np.float32(exact)) / np.float32(np.log(MAXD / exact))
    large = np.minimum(exact + (ratio * np.float32(BUCKETS - exact)).astype(np.int32), BUCKETS - 1)
    bucket = np.where(dist < 0, BUCKETS, np.where(dist < exact, dist, large))
    return (np.arange(BUCKETS + 1)[:, None] == bucket[None, :]).astype(np.float32)


def kernel(**inputs):
    import concourse.bacc as _bacc
    from concourse.bass_utils import run_bass_kernel_spmd as _run

    nc = _bacc.Bacc("TRN2", target_bir_lowering=False, num_devices=1)
    arrays, args = {}, {}
    for name in NAMES:
        v = np.ascontiguousarray(inputs[name])
        arrays[f"in_{name}"] = v
        args[name] = nc.dram_tensor(f"in_{name}", v.shape, mybir.dt.from_np(v.dtype), kind="ExternalInput").ap()
    arrays["in_onehot"] = bucket_rows()
    onehot = nc.dram_tensor("in_onehot", [33, 1024], F32, kind="ExternalInput").ap()
    out = nc.dram_tensor("out0", [1, T, D], F32, kind="ExternalOutput").ap()
    build(nc, args, onehot, out)
    r = _run(nc, [arrays], core_ids=[0])
    return r.results[0]["out0"]
```
